# Optimizing a Trainium2 kernel written in Bass

```python
import jax, jax.numpy as jnp
from jax import lax
import numpy as np
import math

D_MODEL = 1024
BATCH = 1
SEQ = 1024
DEPTH = 1

CHUNK = 64
LEFT_CHUNKS = 8
BAND = (LEFT_CHUNKS + 1) * CHUNK
ATT_HEADS = 8
ATT_HEAD_DIM = 64
ATT_WIDTH = ATT_HEADS * ATT_HEAD_DIM
MAX_REL_DIST = 128
SGU_CHUNK = 128
SGU_GROUPS = 4
SGU_WIDTH = 512
SGU_GROUP_DIM = SGU_WIDTH // SGU_GROUPS
N_BRANCHES = 2
IN_WIDTH = 3 * ATT_WIDTH + 2 * SGU_WIDTH + N_BRANCHES * D_MODEL
D_FF = -(-(8 * D_MODEL) // (3 * 256)) * 256
EPS = 1e-6


def rmsnorm(x, g):
    xf = x.astype(jnp.float32)
    xf = xf * lax.rsqrt(jnp.mean(xf * xf, axis=-1, keepdims=True) + EPS)
    return (xf * g.astype(jnp.float32)).astype(x.dtype)

def layernorm(x, g, b):
    xf = x.astype(jnp.float32)
    mu = jnp.mean(xf, axis=-1, keepdims=True)
    var = jnp.mean(jnp.square(xf - mu), axis=-1, keepdims=True)
    y = (xf - mu) * lax.rsqrt(var + EPS) * g.astype(jnp.float32) + b.astype(jnp.float32)
    return y.astype(x.dtype)

def chunked_rel_attention(q, k, v, rel_bias):
    B, S, H, Dh = q.shape
    nc = S // CHUNK
    pad = LEFT_CHUNKS * CHUNK
    qc = q.reshape(B, nc, CHUNK, H, Dh)
    kp = jnp.pad(k, ((0, 0), (pad, 0), (0, 0), (0, 0)))
    vp = jnp.pad(v, ((0, 0), (pad, 0), (0, 0), (0, 0)))
    band_idx = jnp.arange(nc)[:, None] * CHUNK + jnp.arange(BAND)[None, :]
    kb = kp[:, band_idx]
    vb = vp[:, band_idx]
    scores = jnp.einsum('bcqhd,bckhd->bhcqk', qc, kb).astype(jnp.float32) * (Dh ** -0.5)
    q_pos = pad + jnp.arange(CHUNK)
    k_pos = jnp.arange(BAND)
    rel = jnp.clip(q_pos[:, None] - k_pos[None, :], -MAX_REL_DIST, MAX_REL_DIST) + MAX_REL_DIST
    bias = rel_bias.astype(jnp.float32)[:, rel]
    scores = scores + bias[None, :, None, :, :]
    key_chunk = jnp.arange(nc)[:, None] - LEFT_CHUNKS + (k_pos // CHUNK)[None, :]
    valid = key_chunk >= 0
    scores = jnp.where(valid[None, None, :, None, :], scores, jnp.float32(-1e30))
    probs = jax.nn.softmax(scores, axis=-1).astype(v.dtype)
    out = jnp.einsum('bhcqk,bckhd->bcqhd', probs, vb)
    return out.reshape(B, S, H * Dh)

def spatial_gating(u, v, ln_g, ln_b, w_s, b_s):
    B, S, _ = v.shape
    ng = S // SGU_CHUNK
    v = layernorm(v, ln_g, ln_b)
    vg = v.reshape(B, ng, SGU_CHUNK, SGU_GROUPS, SGU_GROUP_DIM)
    causal = jnp.tril(jnp.ones((SGU_CHUNK, SGU_CHUNK), dtype=bool))
    w = jnp.where(causal[None], w_s, jnp.zeros_like(w_s))
    mixed = jnp.einsum('gts,bnsgd->bntgd', w, vg) + b_s.T[None, None, :, :, None]
    return u * mixed.reshape(B, S, SGU_WIDTH)

def first_inputs(seed: int = 0) -> dict:
    key = jax.random.key(seed)
    ks = jax.random.split(key, 16)
    f32 = jnp.float32

    def nrm(k, shape, scale):
        return jax.random.normal(k, shape, f32) * scale

    x = nrm(ks[0], (BATCH, SEQ, D_MODEL), 1.0)
    norm_mix = 1.0 + nrm(ks[1], (DEPTH, D_MODEL), 0.02)
    w_in = nrm(ks[2], (DEPTH, D_MODEL, IN_WIDTH), D_MODEL ** -0.5)
    att_rel_bias = nrm(ks[3], (DEPTH, ATT_HEADS, 2 * MAX_REL_DIST + 1), 0.1)
    sgu_norm_gain = 1.0 + nrm(ks[4], (DEPTH, SGU_WIDTH), 0.02)
    sgu_norm_bias = nrm(ks[5], (DEPTH, SGU_WIDTH), 0.02)
    sgu_w = nrm(ks[6], (DEPTH, SGU_GROUPS, SGU_CHUNK, SGU_CHUNK), 0.5 * SGU_CHUNK ** -0.5)
    sgu_b = 1.0 + nrm(ks[7], (DEPTH, SGU_GROUPS, SGU_CHUNK), 0.02)
    w_br_att = nrm(ks[8], (DEPTH, ATT_WIDTH, D_MODEL), ATT_WIDTH ** -0.5)
    w_br_sgu = nrm(ks[9], (DEPTH, SGU_WIDTH, D_MODEL), SGU_WIDTH ** -0.5)
    b_gate = nrm(ks[10], (DEPTH, N_BRANCHES, D_MODEL), 0.02)
    w_out = nrm(ks[11], (DEPTH, D_MODEL, D_MODEL), D_MODEL ** -0.5)
    norm_ffn = 1.0 + nrm(ks[12], (DEPTH, D_MODEL), 0.02)
    w_ffn_in = nrm(ks[13], (DEPTH, D_MODEL, 2 * D_FF), D_MODEL ** -0.5)
    w_ffn_out = nrm(ks[14], (DEPTH, D_FF, D_MODEL), D_FF ** -0.5)
    norm_final = 1.0 + nrm(ks[15], (D_MODEL,), 0.02)
    return {"x": x, "norm_mix": norm_mix, "w_in": w_in, "att_rel_bias": att_rel_bias,
            "sgu_norm_gain": sgu_norm_gain, "sgu_norm_bias": sgu_norm_bias,
            "sgu_w": sgu_w, "sgu_b": sgu_b, "w_br_att": w_br_att, "w_br_sgu": w_br_sgu,
            "b_gate": b_gate, "w_out": w_out, "norm_ffn": norm_ffn,
            "w_ffn_in": w_ffn_in, "w_ffn_out": w_ffn_out, "norm_final": norm_final}

def first_block(x, norm_mix, w_in, att_rel_bias, sgu_norm_gain, sgu_norm_bias, sgu_w, sgu_b,
              w_br_att, w_br_sgu, b_gate, w_out, norm_ffn, w_ffn_in, w_ffn_out, norm_final):
    B, S, D = x.shape
    h = x
    for l in range(DEPTH):
        xn = rmsnorm(h, norm_mix[l])
        proj = xn @ w_in[l]
        q, k, v, u, vs, gate_logits = jnp.split(
            proj, np.cumsum([ATT_WIDTH, ATT_WIDTH, ATT_WIDTH, SGU_WIDTH, SGU_WIDTH]).tolist(), axis=-1)
        q = q.reshape(B, S, ATT_HEADS, ATT_HEAD_DIM)
        k = k.reshape(B, S, ATT_HEADS, ATT_HEAD_DIM)
        v = v.reshape(B, S, ATT_HEADS, ATT_HEAD_DIM)
        att = chunked_rel_attention(q, k, v, att_rel_bias[l])
        sgu = spatial_gating(jax.nn.gelu(u), jax.nn.gelu(vs), sgu_norm_gain[l], sgu_norm_bias[l],
                             sgu_w[l], sgu_b[l])
        br_att = att @ w_br_att[l]
        br_sgu = sgu @ w_br_sgu[l]
        gates = jax.nn.sigmoid(gate_logits.reshape(B, S, N_BRANCHES, D) + b_gate[l])
        merged = gates[:, :, 0] * br_att + gates[:, :, 1] * br_sgu
        h = h + merged @ w_out[l]
        hn = rmsnorm(h, norm_ffn[l])
        g, up = jnp.split(hn @ w_ffn_in[l], 2, axis=-1)
        h = h + (jax.nn.silu(g) * up) @ w_ffn_out[l]
    return rmsnorm(h, norm_final)


_first_inputs = first_inputs


def first_inputs(seed=0):
    import zlib

    import numpy as np

    out = dict(_first_inputs(seed))
    spreads = {}
    factors = {'norm_mix': 5.586,
     'att_rel_bias': 22.663,
     'sgu_norm_gain': 62.274,
     'sgu_norm_bias': 56.36,
     'sgu_b': 23.324,
     'b_gate': 8.0,
     'norm_ffn': 17.117,
     'norm_final': 8.203}
    for name, (base, spread) in spreads.items():
        noise = np.random.default_rng([zlib.crc32(name.encode()), seed]).standard_normal(out[name].shape)
        drawn = base * np.exp(spread * noise) if base else spread * noise
        out[name] = __import__('jax').numpy.asarray(drawn.astype(out[name].dtype))
    for name, factor in factors.items():
        out[name] = (out[name] * factor).astype(out[name].dtype)
    return out


_narrow_inputs = first_inputs


def first_inputs(seed=0):

    out = dict(_narrow_inputs(seed))
    wider = {'att_rel_bias': 4.12,
     'sgu_norm_gain': 3.64,
     'sgu_norm_bias': 3.61,
     'sgu_b': 3.26,
     'norm_final': 3.22}
    for name, times in wider.items():
        mean = out[name].mean()
        out[name] = (mean + times * (out[name] - mean)).astype(out[name].dtype)
    return out


D_PLE = 256
M_HEADS = 4
M_HEAD_DIM = 128
M_WIDTH = M_HEADS * M_HEAD_DIM
M_CONV = 5
M_CHUNK = 64
N_GATE = 4 * M_HEADS
A_HEADS = 8
A_KV_HEADS = 2
A_HEAD_DIM = 64
A_WIDTH = A_HEADS * A_HEAD_DIM
A_KV_WIDTH = A_KV_HEADS * A_HEAD_DIM
A_GROUP = A_HEADS // A_KV_HEADS
WINDOW = 128
A_BLOCK = 128
MIX_WIDTH = M_WIDTH + A_WIDTH
IN_WIDTH_2 = 4 * M_WIDTH + N_GATE + A_WIDTH + 2 * A_KV_WIDTH
D_FF_2 = ((-(-8 * D_MODEL // 3) + 255) // 256) * 256
ALPHA = (2 * DEPTH) ** 0.25
BETA = (8 * DEPTH) ** -0.25
LN_EPS = 1e-5
MH_EPS = 1e-6


def _layer_norm(x, g, b):
    xf = x.astype(jnp.float32)
    mu = xf.mean(-1, keepdims=True)
    var = jnp.mean(jnp.square(xf - mu), -1, keepdims=True)
    return ((xf - mu) * lax.rsqrt(var + LN_EPS) * g + b).astype(x.dtype)

def _centred_dwconv(x, w, b):
    pad = w.shape[0] // 2
    y = lax.conv_general_dilated(x, w[:, None, :], window_strides=(1,), padding=[(pad, pad)],
                                 dimension_numbers=("NWC", "WIO", "NWC"),
                                 feature_group_count=x.shape[-1])
    return y + b

def _mlstm_scan(q, k, v, i_pre, log_f):
    B, H, S, dh = q.shape
    L = M_CHUNK
    nc = S // L

    def chunks(t):
        return jnp.moveaxis(t.reshape(B, H, nc, L, *t.shape[3:]), 2, 0)

    lower = jnp.tril(jnp.ones((L, L), dtype=bool))

    def step(carry, xs):
        C, n, m = carry
        qc, kc, vc, ic, fc = xs
        b = jnp.cumsum(fc, axis=-1)
        dmat = b[..., :, None] - b[..., None, :] + ic[..., None, :]
        dmat = jnp.where(lower, dmat, -jnp.inf)
        inter = b + m[..., None]
        m_t = jnp.maximum(dmat.max(-1), inter)
        w_intra = jnp.exp(dmat - m_t[..., None])
        w_inter = jnp.exp(inter - m_t)
        s = jnp.einsum('bhtd,bhsd->bhts', qc, kc) * w_intra
        num = jnp.einsum('bhts,bhse->bhte', s, vc) + w_inter[..., None] * jnp.einsum('bhed,bhtd->bhte', C, qc)
        den = s.sum(-1) + w_inter * jnp.einsum('bhd,bhtd->bht', n, qc)
        h = num / jnp.maximum(jnp.abs(den), jnp.exp(-m_t))[..., None]
        g = b[..., -1]
        a = g[..., None] - b + ic
        m_new = jnp.maximum(g + m, a.max(-1))
        decay = jnp.exp(g + m - m_new)
        wa = jnp.exp(a - m_new[..., None])
        C = decay[..., None, None] * C + jnp.einsum('bhs,bhse,bhsd->bhed', wa, vc, kc)
        n = decay[..., None] * n + jnp.einsum('bhs,bhsd->bhd', wa, kc)
        return (C, n, m_new), h

    init = (jnp.zeros((B, H, dh, dh), jnp.float32), jnp.zeros((B, H, dh), jnp.float32),
            jnp.zeros((B, H), jnp.float32))
    _, h = lax.scan(step, init, (chunks(q), chunks(k), chunks(v), chunks(i_pre), chunks(log_f)))
    return jnp.moveaxis(h, 0, 2).reshape(B, H, S, dh)

def _mlstm_group(qk, v, o, gates, b_gate, conv_w, conv_b, norm_g):
    B, S, _ = v.shape
    qk = jax.nn.silu(_centred_dwconv(qk, conv_w, conv_b))
    q, k = jnp.split(qk, 2, axis=-1)

    def to_heads(t):
        return t.reshape(B, S, M_HEADS, M_HEAD_DIM).transpose(0, 2, 1, 3).astype(jnp.float32)

    q, k, vh = to_heads(q), to_heads(k) * (M_HEAD_DIM ** -0.5), to_heads(v)
    g = (gates + b_gate).astype(jnp.float32).reshape(B, S, 4, M_HEADS).transpose(2, 0, 3, 1)
    h_fwd = _mlstm_scan(q, k, vh, g[0], jax.nn.log_sigmoid(g[2]))

    def flip(t):
        return jnp.flip(t, axis=2)

    h_bwd = flip(_mlstm_scan(flip(q), flip(k), flip(vh), flip(g[1]), flip(jax.nn.log_sigmoid(g[3]))))
    h = h_fwd + h_bwd
    mu = h.mean(-1, keepdims=True)
    var = jnp.mean(jnp.square(h - mu), -1, keepdims=True)
    h = ((h - mu) * lax.rsqrt(var + MH_EPS)).transpose(0, 2, 1, 3).reshape(B, S, M_WIDTH)
    return (h * norm_g * jax.nn.sigmoid(o.astype(jnp.float32))).astype(v.dtype)

def _window_gqa(q, k, v, sink):
    B, S, _ = q.shape
    nb = S // A_BLOCK
    qb = q.reshape(B, nb, A_BLOCK, A_KV_HEADS, A_GROUP, A_HEAD_DIM)

    def band(t):
        t = t.reshape(B, nb, A_BLOCK, A_KV_HEADS, A_HEAD_DIM)
        t = jnp.pad(t, ((0, 0), (1, 1), (0, 0), (0, 0), (0, 0)))
        return jnp.concatenate([t[:, :-2], t[:, 1:-1], t[:, 2:]], axis=2)

    kb, vb = band(k), band(v)
    s = jnp.einsum('bnqhgd,bnkhd->bnhgqk', qb, kb).astype(jnp.float32) * (A_HEAD_DIM ** -0.5)
    blk = jnp.arange(nb)[:, None]
    qpos = blk * A_BLOCK + jnp.arange(A_BLOCK)[None]
    kpos = (blk - 1) * A_BLOCK + jnp.arange(3 * A_BLOCK)[None]
    rel = jnp.abs(kpos[:, None, :] - qpos[:, :, None])
    valid = (rel <= WINDOW) & (kpos[:, None, :] >= 0) & (kpos[:, None, :] < S)
    slopes = jnp.exp2(-8.0 * jnp.arange(1, A_HEADS + 1, dtype=jnp.float32) / A_HEADS)
    bias = -slopes.reshape(A_KV_HEADS, A_GROUP)[None, :, :, None, None] * rel[:, None, None].astype(jnp.float32)
    s = jnp.where(valid[:, None, None], s + bias, -jnp.inf)
    sk = sink.astype(jnp.float32).reshape(A_KV_HEADS, A_GROUP)[None, None, :, :, None, None]
    mx = jnp.maximum(s.max(-1, keepdims=True), sk)
    e = jnp.exp(s - mx)
    prob = e / (e.sum(-1, keepdims=True) + jnp.exp(sk - mx))
    out = jnp.einsum('bnhgqk,bnkhd->bnqhgd', prob.astype(v.dtype), vb)
    return out.reshape(B, S, A_WIDTH)

def _hybrid_layer(x, p_i, w_in, b_gate, conv_w, conv_b, mlstm_norm_g, attn_sink, w_out,
                  ln1_g, ln1_b, w_ffn_in, w_ffn_out, ln2_g, ln2_b, w_ple_gate, w_ple_proj):
    u = x @ w_in
    cuts = np.cumsum([2 * M_WIDTH, M_WIDTH, M_WIDTH, N_GATE, A_WIDTH, A_KV_WIDTH]).tolist()
    m_qk, m_v, m_o, m_gates, a_q, a_k, a_v = jnp.split(u, cuts, axis=-1)
    h_m = _mlstm_group(m_qk, m_v, m_o, m_gates, b_gate, conv_w, conv_b, mlstm_norm_g)
    h_a = _window_gqa(a_q, a_k, a_v, attn_sink)
    mix = jnp.concatenate([h_m, h_a], axis=-1) @ w_out
    x = _layer_norm(ALPHA * x + mix, ln1_g, ln1_b)
    gate_ff, up_ff = jnp.split(x @ w_ffn_in, 2, axis=-1)
    ffn = (jax.nn.silu(gate_ff) * up_ff) @ w_ffn_out
    ple = jax.nn.sigmoid(x @ w_ple_gate) * (p_i @ w_ple_proj)
    return _layer_norm(ALPHA * x + ffn + ple, ln2_g, ln2_b)

def second_inputs(seed: int = 0) -> dict:
    key = jax.random.key(seed)
    ks = jax.random.split(key, 20)
    nrm = lambda k, shape: jax.random.normal(k, shape, jnp.float32)
    col_scale = np.ones((IN_WIDTH_2,), np.float32)
    col_scale[3 * M_WIDTH - M_WIDTH:3 * M_WIDTH] = BETA
    av0 = 4 * M_WIDTH + N_GATE + A_WIDTH + A_KV_WIDTH
    col_scale[av0:av0 + A_KV_WIDTH] = BETA
    w_in = nrm(ks[2], (DEPTH, D_MODEL, IN_WIDTH_2)) * (D_MODEL ** -0.5) * jnp.asarray(col_scale)
    f_lin = jnp.linspace(3.0, 6.0, M_HEADS, dtype=jnp.float32)
    b_gate = jnp.concatenate([0.1 * nrm(ks[3], (DEPTH, 2 * M_HEADS)),
                              jnp.concatenate([f_lin, f_lin])[None] + 0.1 * nrm(ks[4], (DEPTH, 2 * M_HEADS))], axis=-1)
    return {
        "x": nrm(ks[0], (BATCH, SEQ, D_MODEL)),
        "p": nrm(ks[1], (DEPTH, BATCH, SEQ, D_PLE)),
        "w_in": w_in,
        "b_gate": b_gate,
        "conv_w": nrm(ks[5], (DEPTH, M_CONV, 2 * M_WIDTH)) * (M_CONV ** -0.5),
        "conv_b": 0.01 * nrm(ks[6], (DEPTH, 2 * M_WIDTH)),
        "mlstm_norm_g": 1.0 + 0.01 * nrm(ks[7], (DEPTH, M_WIDTH)),
        "attn_sink": 0.5 * nrm(ks[8], (DEPTH, A_HEADS)),
        "w_out": nrm(ks[9], (DEPTH, MIX_WIDTH, D_MODEL)) * (MIX_WIDTH ** -0.5) * BETA,
        "ln1_g": 1.0 + 0.01 * nrm(ks[10], (DEPTH, D_MODEL)),
        "ln1_b": 0.01 * nrm(ks[11], (DEPTH, D_MODEL)),
        "w_ffn_in": nrm(ks[12], (DEPTH, D_MODEL, 2 * D_FF_2)) * (D_MODEL ** -0.5) * BETA,
        "w_ffn_out": nrm(ks[13], (DEPTH, D_FF_2, D_MODEL)) * (D_FF_2 ** -0.5) * BETA,
        "ln2_g": 1.0 + 0.01 * nrm(ks[14], (DEPTH, D_MODEL)),
        "ln2_b": 0.01 * nrm(ks[15], (DEPTH, D_MODEL)),
        "w_ple_gate": nrm(ks[16], (DEPTH, D_MODEL, D_MODEL)) * (D_MODEL ** -0.5),
        "w_ple_proj": nrm(ks[17], (DEPTH, D_PLE, D_MODEL)) * (D_PLE ** -0.5) * BETA,
    }

def second_block(x, p, w_in, b_gate, conv_w, conv_b, mlstm_norm_g, attn_sink, w_out,
              ln1_g, ln1_b, w_ffn_in, w_ffn_out, ln2_g, ln2_b, w_ple_gate, w_ple_proj):
    h = x
    for i in range(DEPTH):
        h = _hybrid_layer(h, p[i], w_in[i], b_gate[i], conv_w[i], conv_b[i], mlstm_norm_g[i],
                          attn_sink[i], w_out[i], ln1_g[i], ln1_b[i], w_ffn_in[i], w_ffn_out[i],
                          ln2_g[i], ln2_b[i], w_ple_gate[i], w_ple_proj[i])
    return h


_first_inputs_2 = second_inputs


def second_inputs(seed=0):
    import zlib

    import numpy as np

    out = dict(_first_inputs_2(seed))
    spreads = {}
    factors = {'conv_b': 8.0,
     'mlstm_norm_g': 8.0,
     'attn_sink': 8.0,
     'ln1_g': 5.994,
     'ln1_b': 5.808,
     'ln2_g': 5.753,
     'ln2_b': 5.727}
    for name, (base, spread) in spreads.items():
        noise = np.random.default_rng([zlib.crc32(name.encode()), seed]).standard_normal(out[name].shape)
        drawn = base * np.exp(spread * noise) if base else spread * noise
        out[name] = __import__('jax').numpy.asarray(drawn.astype(out[name].dtype))
    for name, factor in factors.items():
        out[name] = (out[name] * factor).astype(out[name].dtype)
    return out


_narrow_inputs_2 = second_inputs


def second_inputs(seed=0):

    out = dict(_narrow_inputs_2(seed))
    wider = {'mlstm_norm_g': 6.4,
     'attn_sink': 7.66,
     'ln1_g': 5.68,
     'ln1_b': 5.66,
     'ln2_g': 6.5,
     'ln2_b': 6.47}
    for name, times in wider.items():
        mean = out[name].mean()
        out[name] = (mean + times * (out[name] - mean)).astype(out[name].dtype)
    return out


D_MIX = D_MODEL
CONV_CH = D_MIX // 2
CONV_GROUPS = 8
N_HEADS = 8
HEAD_DIM = 64
ATT_CH = N_HEADS * HEAD_DIM
CONV_WIDTH = 31
GRID_W = 64
MAX_KH = 8
KW = 16
PROJ_OUT = 3 * CONV_CH + 4 * ATT_CH


def rms_norm(x, g):
    x32 = x.astype(jnp.float32)
    y = x32 * lax.rsqrt(jnp.mean(x32 * x32, axis=-1, keepdims=True) + EPS)
    return (y * g.astype(jnp.float32)).astype(x.dtype)

def layer_norm(x, g, b):
    x32 = x.astype(jnp.float32)
    mu = jnp.mean(x32, axis=-1, keepdims=True)
    var = jnp.mean(jnp.square(x32 - mu), axis=-1, keepdims=True)
    y = (x32 - mu) * lax.rsqrt(var + EPS)
    return (y * g.astype(jnp.float32) + b.astype(jnp.float32)).astype(x.dtype)

def grouped_rms_norm(y, g, n_groups):
    B, T, C = y.shape
    y32 = y.astype(jnp.float32).reshape(B, T, n_groups, C // n_groups)
    y32 = y32 * lax.rsqrt(jnp.mean(y32 * y32, axis=-1, keepdims=True) + EPS)
    return (y32.reshape(B, T, C) * g.astype(jnp.float32)).astype(y.dtype)

def conformer_conv(glu_a, glu_b, dw_w, dw_b, cln_g, cln_b, pw_w, pw_b):
    u = glu_a * jax.nn.sigmoid(glu_b)
    pad = CONV_WIDTH // 2
    u = lax.conv_general_dilated(
        u, dw_w[:, None, :].astype(u.dtype), window_strides=(1,),
        padding=[(pad, pad)], dimension_numbers=("NWC", "WIO", "NWC"),
        feature_group_count=u.shape[-1]) + dw_b
    u = layer_norm(u, cln_g, cln_b)
    u = jax.nn.silu(u)
    return u @ pw_w + pw_b

def neighbourhood_attention(q, k, v, rpb):
    B, T, _ = q.shape
    rows = T // GRID_W
    kh = min(MAX_KH, rows)

    def to_grid(t):
        return t.reshape(B, rows, GRID_W, N_HEADS, HEAD_DIM).transpose(0, 3, 1, 2, 4)

    qg, kg, vg = to_grid(q), to_grid(k), to_grid(v)
    scale = HEAD_DIM ** -0.5

    row_ids = jnp.arange(rows)
    row_start = jnp.clip(row_ids - kh // 2, 0, rows - kh)
    col_ids = jnp.arange(GRID_W)
    col_start = jnp.clip(col_ids - KW // 2, 0, GRID_W - KW)
    col_idx = col_start[:, None] + jnp.arange(KW)[None, :]
    col_rel = col_idx - col_ids[:, None] + (KW - 1)

    def one_row(args):
        r, rs = args
        q_row = lax.dynamic_index_in_dim(qg, r, axis=2, keepdims=False)
        k_rows = lax.dynamic_slice_in_dim(kg, rs, kh, axis=2)
        v_rows = lax.dynamic_slice_in_dim(vg, rs, kh, axis=2)
        k_win = k_rows[:, :, :, col_idx, :]
        v_win = v_rows[:, :, :, col_idx, :]
        s = jnp.einsum("bhwd,bhiwjd->bhwij", q_row, k_win).astype(jnp.float32) * scale
        row_rel = rs + jnp.arange(kh) - r + (MAX_KH - 1)
        bias = rpb[:, row_rel[:, None, None], col_rel[None, :, :]]
        s = s + bias.transpose(0, 2, 1, 3).astype(jnp.float32)[None]
        p = jax.nn.softmax(s.reshape(B, N_HEADS, GRID_W, kh * KW), axis=-1)
        p = p.reshape(B, N_HEADS, GRID_W, kh, KW).astype(v.dtype)
        return jnp.einsum("bhwij,bhiwjd->bhwd", p, v_win)

    out = lax.map(one_row, (row_ids, row_start))
    return out.transpose(1, 0, 3, 2, 4).reshape(B, T, ATT_CH)

def third_inputs(seed: int = 0) -> dict:
    key = jax.random.key(seed)
    ks = jax.random.split(key, 16)
    f32 = jnp.float32
    nrm = lambda k, s: jax.random.normal(k, s, f32)
    return {
        "x": nrm(ks[0], (BATCH, SEQ, D_MODEL)),
        "ln_g": 1.0 + 0.01 * nrm(ks[1], (DEPTH, D_MODEL)),
        "w_in": nrm(ks[2], (DEPTH, D_MODEL, PROJ_OUT)) * D_MODEL ** -0.5,
        "b_in": 0.01 * nrm(ks[3], (DEPTH, PROJ_OUT)),
        "dw_w": nrm(ks[4], (DEPTH, CONV_WIDTH, CONV_CH)) * CONV_WIDTH ** -0.5,
        "dw_b": 0.01 * nrm(ks[5], (DEPTH, CONV_CH)),
        "cln_g": 1.0 + 0.01 * nrm(ks[6], (DEPTH, CONV_CH)),
        "cln_b": 0.01 * nrm(ks[7], (DEPTH, CONV_CH)),
        "pw_w": nrm(ks[8], (DEPTH, CONV_CH, CONV_CH)) * CONV_CH ** -0.5,
        "pw_b": 0.01 * nrm(ks[9], (DEPTH, CONV_CH)),
        "rpb": 0.02 * nrm(ks[10], (DEPTH, N_HEADS, 2 * MAX_KH - 1, 2 * KW - 1)),
        "gn_conv_g": 1.0 + 0.01 * nrm(ks[11], (DEPTH, CONV_CH)),
        "gn_att_g": 1.0 + 0.01 * nrm(ks[12], (DEPTH, ATT_CH)),
        "w_out": nrm(ks[13], (DEPTH, D_MIX, D_MODEL)) * D_MIX ** -0.5,
        "final_g": 1.0 + 0.01 * nrm(ks[14], (D_MODEL,)),
    }

def third_block(x, ln_g, w_in, b_in, dw_w, dw_b, cln_g, cln_b, pw_w, pw_b, rpb,
              gn_conv_g, gn_att_g, w_out, final_g):
    h = x
    cuts = [CONV_CH, 2 * CONV_CH, 3 * CONV_CH, 3 * CONV_CH + ATT_CH,
            3 * CONV_CH + 2 * ATT_CH, 3 * CONV_CH + 3 * ATT_CH]
    for l in range(DEPTH):
        hn = rms_norm(h, ln_g[l])
        proj = hn @ w_in[l] + b_in[l]
        glu_a, glu_b, z_conv, q, k, v, z_att = jnp.split(proj, cuts, axis=-1)
        y_conv = conformer_conv(glu_a, glu_b, dw_w[l], dw_b[l], cln_g[l], cln_b[l],
                                pw_w[l], pw_b[l])
        y_att = neighbourhood_attention(q, k, v, rpb[l])
        y_conv = grouped_rms_norm(y_conv, gn_conv_g[l], CONV_GROUPS) * jax.nn.silu(z_conv)
        y_att = grouped_rms_norm(y_att, gn_att_g[l], N_HEADS) * jax.nn.silu(z_att)
        y = jnp.concatenate([y_conv, y_att], axis=-1)
        h = h + y @ w_out[l]
    return rms_norm(h, final_g)


_first_inputs_3 = third_inputs


def third_inputs(seed=0):
    import zlib

    import numpy as np

    out = dict(_first_inputs_3(seed))
    spreads = {}
    factors = {'ln_g': 5.827,
     'dw_b': 29.293,
     'cln_g': 62.635,
     'cln_b': 64.0,
     'pw_b': 45.797,
     'rpb': 8.0,
     'gn_conv_g': 62.548,
     'gn_att_g': 64.0,
     'final_g': 33.043,
     'b_in': 6.355}
    for name, (base, spread) in spreads.items():
        noise = np.random.default_rng([zlib.crc32(name.encode()), seed]).standard_normal(out[name].shape)
        drawn = base * np.exp(spread * noise) if base else spread * noise
        out[name] = __import__('jax').numpy.asarray(drawn.astype(out[name].dtype))
    for name, factor in factors.items():
        out[name] = (out[name] * factor).astype(out[name].dtype)
    return out


_narrow_inputs_3 = third_inputs


def third_inputs(seed=0):

    out = dict(_narrow_inputs_3(seed))
    wider = {'cln_g': 8.97,
     'cln_b': 9.09,
     'pw_b': 8.93,
     'gn_conv_g': 8.89,
     'gn_att_g': 9.11,
     'final_g': 6.47}
    for name, times in wider.items():
        mean = out[name].mean()
        out[name] = (mean + times * (out[name] - mean)).astype(out[name].dtype)
    return out


def setup_inputs(seed=0):
    out = dict(first_inputs(seed))
    for name, value in second_inputs(seed + 1).items():
        if name != "x":
            out[name + "_2"] = value
    for name, value in third_inputs(seed + 2).items():
        if name != "x":
            out[name + "_3"] = value
    return out


def reference(
    x, norm_mix, w_in, att_rel_bias, sgu_norm_gain, sgu_norm_bias, sgu_w, sgu_b, w_br_att,
    w_br_sgu, b_gate, w_out, norm_ffn, w_ffn_in, w_ffn_out, norm_final, p_2, w_in_2, b_gate_2,
    conv_w_2, conv_b_2, mlstm_norm_g_2, attn_sink_2, w_out_2, ln1_g_2, ln1_b_2, w_ffn_in_2,
    w_ffn_out_2, ln2_g_2, ln2_b_2, w_ple_gate_2, w_ple_proj_2, ln_g_3, w_in_3, b_in_3, dw_w_3,
    dw_b_3, cln_g_3, cln_b_3, pw_w_3, pw_b_3, rpb_3, gn_conv_g_3, gn_att_g_3, w_out_3,
    final_g_3,
):
    x = first_block(
        x, norm_mix, w_in, att_rel_bias, sgu_norm_gain, sgu_norm_bias, sgu_w, sgu_b, w_br_att,
        w_br_sgu, b_gate, w_out, norm_ffn, w_ffn_in, w_ffn_out, norm_final,
    )
    x = second_block(
        x, p_2, w_in_2, b_gate_2, conv_w_2, conv_b_2, mlstm_norm_g_2, attn_sink_2, w_out_2,
        ln1_g_2, ln1_b_2, w_ffn_in_2, w_ffn_out_2, ln2_g_2, ln2_b_2, w_ple_gate_2, w_ple_proj_2,
    )
    return third_block(
        x, ln_g_3, w_in_3, b_in_3, dw_w_3, dw_b_3, cln_g_3, cln_b_3, pw_w_3, pw_b_3, rpb_3,
        gn_conv_g_3, gn_att_g_3, w_out_3, final_g_3,
    )


_drawn_inputs = setup_inputs


def setup_inputs(seed=0):
    import zlib

    import numpy as np

    out = dict(_drawn_inputs(seed))
    spreads = {}
    factors = {'conv_b_2': 35.832}
    for name, (base, spread) in spreads.items():
        noise = np.random.default_rng([zlib.crc32(name.encode()), seed]).standard_normal(out[name].shape)
        drawn = base * np.exp(spread * noise) if base else spread * noise
        out[name] = __import__('jax').numpy.asarray(drawn.astype(out[name].dtype))
    for name, factor in factors.items():
        out[name] = (out[name] * factor).astype(out[name].dtype)
    return out
```

```python
from contextlib import ExitStack, contextmanager

import numpy as np
import concourse.bass as bass
from concourse import mybir

F32 = mybir.dt.float32
F32R = mybir.dt.float32r
ALU = mybir.AluOpType
ACT = mybir.ActivationFunctionType
AX = mybir.AxisListType

P = 128
TOK = 1024
HALF = 512
D = 1024
KT = D // P
TT = TOK // P
EPS = 1e-6
ALPHA = 2.0 ** 0.25
NEG = -1e30


class Buffers:

    def __init__(self, q_t, k_t, v_tok, scores, probs, probs_t, total, bias):
        self.q_t, self.k_t, self.v_tok, self.scores = q_t, k_t, v_tok, scores
        self.probs, self.probs_t, self.total, self.bias = probs, probs_t, total, bias


class Turns:

    def __init__(self, engine):
        self.engine, self.base, self.per, self.reg, self.start = engine, {}, {}, None, {}
        self.turn = self.block = 0

    def count(self, name):
        n = self.base.get(name, 0)
        return n if self.reg is None or not self.per.get(name) else self.reg * self.per[name] + n

    def next(self, name):
        self.base[name] = self.base.get(name, 0) + 1
        return self.count(name)

    def some(self, name):
        return self.base.get(name, 0) > 0

    @contextmanager
    def loop(self, times, **per):
        first, turn, block = dict(self.base), self.turn, self.block
        with self.engine.Fori(0, times) as i:
            self.reg, self.per = i, per
            yield i
        self.reg, self.per = None, {}
        for name in {*self.base, *first}:
            grown = self.base.get(name, 0) - first.get(name, 0)
            assert grown == per.get(name, 0), (name, grown, per.get(name, 0))
            self.base[name] = first.get(name, 0) + grown * times
        assert (self.turn - turn) % 2 == 0 and (self.block - block) % 2 == 0


class Chain:

    def __init__(self, engine, sem):
        self.engine, self.sem, self.n, self.waited = engine, sem, 0, 0

    def link(self, instruction):
        instruction.then_inc(self.sem, 1)
        self.n += 1
        return instruction

    def sync(self):
        if self.n > self.waited:
            self.engine.wait_ge(self.sem, self.n)
            self.waited = self.n

    def reset(self):
        self.sync()
        if self.n:
            self.engine.sem_clear(self.sem)
        self.n = self.waited = 0


PARAMS = [("norm_mix", 8), ("b_gate", 16), ("norm_ffn", 8), ("norm_final", 8),
          ("heads", 52), ("gate_b", 1), ("sink", 8),
          ("ln1_g", 8), ("ln1_b", 8), ("ln2_g", 8), ("ln2_b", 8),
          ("ln3_g", 8), ("glu", 136), ("b_z", 4), ("cln_g", 4), ("cln_b", 4),
          ("pw_b", 4), ("gn_conv", 4), ("pairs", 20), ("final_g", 8),
          ("eps6", 1), ("eps5", 1)]
COL, N_PARAMS = {}, 0
for _name, _n in PARAMS:
    COL[_name] = N_PARAMS
    N_PARAMS += _n

RESERVED = 16512
M_HEADS = 4
TAPS = 5
HEAD_PAR = 2 * (TAPS + 1) + 1
FFN_TILES = 22
FFN_PAIRS = FFN_TILES // 2
ATT_BIAS_1 = 640
HEADS = 8
HEAD_PAIRS = HEADS // 2
SGU_TILES = 4
CONV_TILES = 4
CONV_TAPS = 31
REACH = CONV_TAPS // 2
GLU_PAR = CONV_TAPS + 3
PAIR_PAR = 5
UNITS = [(side, p) for side in range(2) for p in range(TT)]


def keys_1(p):
    first = max(0, p - 4)
    return first * P, (p + 1 - first) * P, ATT_BIAS_1 - (p + 1 - first) * P


def keys_2(p):
    first, last = max(0, p - 1), min(TT - 1, p + 1)
    return first * P, (last + 1 - first) * P, (first - p + 1) * P


BIAS_3 = [(0, 512, 0), (0, 512, 512)] + [((p - 2) * P, 576, 1024) for p in range(2, 6)] \
    + [(512, 512, 1600), (512, 512, 2112)]
N_BIAS_3 = 2624


def keys_3(p):
    return BIAS_3[p]


def mixer_program(nc, x_t, blocks, n_blocks, params, consts, bias_1, bias_2, bias_3, sgu_rows, sgu_w, p_t,
                  out_t):
    with ExitStack() as ctx:
        def at(name, kib, shape, dtype=F32):
            return nc.alloc_sbuf_tensor_at(name, shape, dtype, offset=RESERVED + int(kib * 1024))

        ctx.enter_context(nc.sbuf_tensor("arena", [P, 52 * 1024 - 256], F32))

        raw = at("raw", 0, [P, 2, 1024])
        w_hi = at("w_hi", 8, [P, 2, 8, P], F32R)
        w_lo = at("w_lo", 16, [P, 2, 8, P], F32R)
        x_hi = at("x_hi", 24, [P, KT, TOK], F32R)
        x_lo = at("x_lo", 56, [P, KT, TOK], F32R)
        h = at("h", 88, [P, KT, TOK])
        par = at("par", 200, [P, N_PARAMS])
        zero = at("zero", 202, [P, 1])
        ident = at("ident", 202.125, [P, P])
        mean_w = at("mean_w", 202.625, [P, P])
        small = at("small", 203.125, [P, 64])
        square = at("square", 180, [P, 2, TOK])
        rstd = at("rstd", 188, [P, TOK])
        normed = at("normed", 192, [P, 2, TOK])
        out_rows = at("out_rows", 24, [P, KT, TOK])
        def attention_buffers(base, kib, bias_kib, bias_width):
            return Buffers(
                q_t=at(base + "q_t", kib, [P, TOK]), k_t=at(base + "k_t", kib + 4, [P, TOK]),
                v_tok=at(base + "v_tok", kib + 8, [P, TT, P]),
                scores=at(base + "scores", kib + 12, [P, 2, 640]), probs=at(base + "probs", kib + 17, [P, 2, 640]),
                probs_t=at(base + "probs_t", kib + 22, [P, 2, 5, P]), total=at(base + "att_sum", kib + 27, [P, TOK]),
                bias=at(base + "bias", bias_kib, [P, 2, bias_width]))

        band = attention_buffers("band_", 88, 190, ATT_BIAS_1)
        att_hi = at("att_hi", 120, [P, 4, TOK], F32R)
        att_lo = at("att_lo", 136, [P, 4, TOK], F32R)
        u_t = at("u_t", 88, [P, SGU_TILES, TOK])
        vs_tok = at("vs_tok", 104, [P, TT, 512])
        sgu_hi = at("sgu_hi", 152, [P, SGU_TILES, TOK], F32R)
        sgu_lo = at("sgu_lo", 168, [P, SGU_TILES, TOK], F32R)
        sgu_par = at("sgu_par", 184, [P, 3, 512])
        sgu_wt = at("sgu_wt", 204, [P, 4, P])
        mixed = at("mixed", 192, [P, TOK])
        gate = at("gate", 184, [P, 2, TOK])
        part_hi = at("part_hi", 192, [P, TOK], F32R)
        part_lo = at("part_lo", 196, [P, TOK], F32R)
        act_g = at("act_g", 120, [P, TOK])
        hid = at("hid", 124, [P, TOK])
        hid_hi = at("hid_hi", 128, [P, 2, TOK], F32R)
        hid_lo = at("hid_lo", 136, [P, 2, TOK], F32R)
        gate_rows = at("gate_rows", 120, [P, TOK])
        f_rows = at("f_rows", 124, [64, TOK])
        log_f = at("log_f", 128, [64, TOK])
        m_rows = at("m_rows", 132, [64, TOK])
        b_rows = at("b_rows", 136, [64, TOK])
        c_rows = at("c_rows", 140, [64, TOK])
        carry = at("carry", 144, [64, TOK])
        soft = at("soft", 148, [64, TOK])
        c_col = at("c_col", 152.75, [P, TT, 64])
        g_diag = at("g_diag", 156.75, [64, TT, 64])
        g_all = at("g_all", 154.75, [P, TT, 64])
        r_rows = at("r_rows", 182.25, [64, TOK])
        em_col = at("em_col", 186.25, [P, TT, 2, 32])
        a_col = at("a_col", 188.25, [P, 2, TT, TT, 4])
        a_head = at("a_head", 190.25, [P, 2, TT, TT])
        em_head = at("em_head", 190.75, [P, TT, 2])
        pick = at("pick", 191, [64, 2, P])
        masks = at("masks", 192, [P, 2, P])
        head_par = at("head_par", 193, [P, HEAD_PAR])
        conv_in = at("conv_in", 120, [P, 2, TOK + 8])
        conv_out = at("conv_out", 128.5, [P, 2, TOK])
        v_one = at("v_one", 136.5, [P, TT, 132])
        o_gate = at("o_gate", 140.75, [P, TT, P])
        r_all = at("r_all", 144.75, [P, 2, TOK])
        wts = at("wts", 152.75, [P, 3, TT + 1, P])
        h_tok = at("h_tok", 166.25, [P, TT, P])
        mix_t = at("mix_t", 170.25, [P, TOK])
        mix_hi = at("mix_hi", 174.25, [P, TOK], F32R)
        mix_lo = at("mix_lo", 178.25, [P, TOK], F32R)
        stats = at("stats", 194, [P, 64])
        local = attention_buffers("local_", 120, 160, N_BIAS_3)
        att2_hi = at("att2_hi", 151, [P, TOK], F32R)
        att2_lo = at("att2_lo", 155, [P, TOK], F32R)
        p_rows = at("p_rows", 120, [P, 2, TOK])
        p_hi = at("p_hi", 176, [P, 2, TOK], F32R)
        p_lo = at("p_lo", 184, [P, 2, TOK], F32R)
        ple = at("ple", 144, [P, KT, TOK])
        ple_gate = at("ple_gate", 120, [P, 2, TOK])
        glu_par = at("glu_par", 203.375, [P, 2, GLU_PAR])
        pair_par = at("pair_par", 203.6875, [P, 2, 6])
        group_w = at("group_w", 204, [P, P])
        u_pad = at("u_pad", 120, [P, 2, TOK + 2 * REACH])
        sigmoid = at("sigmoid", 128.5, [P, 2, TOK])
        conv_sum = at("conv_sum", 136.5, [P, CONV_TILES, TOK])
        c_lo = at("c_lo", 136.5, [P, CONV_TILES, TOK], F32R)
        c_hi = at("c_hi", 152.5, [P, CONV_TILES, TOK], F32R)
        z_conv = [at(f"z_conv{j}", kib, [P, TOK])[:, :] for j, kib in enumerate((168.5, 172.5, 192, 196))]
        y_conv = at("y_conv", 120, [P, CONV_TILES, TOK])
        square3 = at("square3", 180, [P, 3, TOK])
        z_att = at("z_att", 192, [P, 2, TOK])

        acc_all = ctx.enter_context(nc.psum_tensor("acc", [P, 4 * TOK], F32))
        acc = [acc_all[:, s * TOK:(s + 1) * TOK] for s in range(2)]
        turned = acc_all[:, 2 * TOK:3 * TOK]
        att_out = acc_all[:, 3 * TOK:4 * TOK]

        def sem(name):
            return ctx.enter_context(nc.semaphore(name))

        raw_in = [sem("raw_in0"), sem("raw_in1")]
        w_split, w_used, hi_split = sem("w_split"), sem("w_used"), sem("hi_split")
        acc_full = [sem("acc_full0"), sem("acc_full1")]
        acc_free = [sem("acc_free0"), sem("acc_free1")]
        const_in, x_in, bias_in, sgu_in = sem("const_in"), sem("x_in"), sem("bias_in"), sem("sgu_in")
        zero_ready = sem("zero_ready")
        sgu_w_ready = sem("sgu_w_ready")
        squared, square_used = sem("squared"), sem("square_used")
        centred = sem("centred")
        rows_ready = sem("rows_ready")
        hi_ready = sem("hi_ready")
        lo_ready = sem("lo_ready")
        scores_ready, exp_done, p_ready = sem("scores_ready"), sem("exp_done"), sem("p_ready")
        turned_full, turned_copied = sem("turned_full"), sem("turned_copied")
        pv_done = sem("pv_done")
        att_copied = sem("att_copied")
        var_ready, std_ready, ln_ready = sem("var_ready"), sem("std_ready"), sem("ln_ready")
        stored = sem("stored")
        head_ready, pick_ready = sem("head_ready"), sem("pick_ready")
        rows_done, soft_ready, cols_ready = sem("rows_done"), sem("soft_ready"), sem("cols_ready")
        conv_raw, conv_summed, conv_ready = sem("conv_raw"), sem("conv_summed"), sem("conv_ready")
        args_ready, w_exp, w_ready = sem("args_ready"), sem("w_exp"), sem("w_ready")
        num_full, num_free = sem("num_full"), sem("num_free")
        h_ready, mask_in, p_in, ple_used = sem("h_ready"), sem("mask_in"), sem("p_in"), sem("ple_used")
        conv_done, group_in = sem("conv_done"), sem("group_in")
        v_chain, s_chain = sem("v_chain"), sem("s_chain")

        def col(name, k=0):
            return par[:, COL[name] + k:COL[name] + k + 1]

        block = ctx.enter_context(nc.Block())

        def claim(e, t):
            s = t.turn % 2
            if t.some(f"acc{s}"):
                e.wait_ge(acc_free[s], t.count(f"acc{s}"))
            return s

        def await_acc(e, t):
            s = t.turn % 2
            e.wait_ge(acc_full[s], t.next(f"acc{s}"))
            t.turn += 1
            return s

        def pass_acc(t, turns=1):
            for _ in range(turns):
                t.next(f"acc{t.turn % 2}")
                t.turn += 1

        def await_all_taken(e, t):
            for s in range(2):
                e.wait_ge(acc_free[s], t.count(f"acc{s}"))

        def take_block(pe, t):
            pe.wait_ge(w_split, t.next("block"))
            t.block += 1
            return (t.block - 1) % 2

        def product(pe, t, pieces, fresh):
            s = claim(pe, t)
            last = len(pieces) - 1
            for n, (slot, tile, hi, lo) in enumerate(pieces):
                for m, (w, part) in enumerate(((w_hi, hi), (w_hi, lo), (w_lo, hi))):
                    for half in range(2):
                        c = slice(half * HALF, (half + 1) * HALF)
                        ins = pe.matmul(acc[s][:, c], w[:, slot, tile, :], part[:, c],
                                        start=(n == 0 and m == 0), stop=(n == last and m == 2))
                        if fresh and n == 0 and m == 0 and half == 0:
                            ins.then_inc(w_used, 1)
            ins.then_inc(acc_full[s], 1)
            t.next(f"acc{s}")
            t.turn += 1

        def feature_block(pe, t):
            slot = take_block(pe, t)
            product(pe, t, [(slot, k, x_hi[:, k, :], x_lo[:, k, :]) for k in range(KT)], True)

        def token_block(pe, t, padded=False):
            s = claim(pe, t)
            if padded:
                slot = take_block(pe, t)
                pe.matmul(acc[s][:, 0:P], x_hi[:, 0, 0:P], w_hi[:, slot, 0, :], start=True, stop=True).then_inc(w_used, 1)
            slot = take_block(pe, t)
            for i in range(TT):
                tok = slice(i * P, (i + 1) * P)
                for k in range(KT):
                    for m, (xs, w) in enumerate(((x_hi, w_hi), (x_hi, w_lo), (x_lo, w_hi))):
                        ins = pe.matmul(acc[s][:, tok], xs[:, k, tok], w[:, slot, k, :],
                                        start=(k == 0 and m == 0), stop=(k == KT - 1 and m == 2))
                        if i == 0 and k == 0 and m == 0:
                            ins.then_inc(w_used, 1)
            ins.then_inc(acc_full[s], 1)
            t.next(f"acc{s}")
            t.turn += 1

        def row_block(pe, t, operands):
            n = len(operands)
            for _ in range(n):
                slot = take_block(pe, t)
                for j in range(KT // n):
                    product(pe, t, [(slot, j * n + k, hi, lo) for k, (hi, lo) in enumerate(operands)], j == 0)

        def sum_squares(pe, t, tiles=KT, weights=None):
            s = claim(pe, t)
            for k in range(tiles):
                pe.wait_ge(squared, t.next("squared"))
                for half in range(2):
                    c = slice(half * HALF, (half + 1) * HALF)
                    ins = pe.matmul(acc[s][:, c], mean_w[:, :], square[:, k % 2, c],
                                    start=(k == 0), stop=(k == tiles - 1))
                if k < tiles - 1:
                    ins.then_inc(square_used, 1)
            ins.then_inc(acc_full[s], 1)
            t.next(f"acc{s}")
            t.turn += 1

        def split_hi(act, t, source, hi):
            act.activation(hi, source, ACT.Copy).then_inc(hi_ready, 1)
            t.next("hi_ready")

        def split_lo(dve, t, source, hi, lo):
            dve.wait_ge(hi_ready, t.next("hi_ready"))
            dve.tensor_tensor(lo, source, hi.bitcast(F32), ALU.subtract).then_inc(lo_ready, 1)
            t.next("lo_ready")

        def norm_tensor(pe, t, centre=False):
            if centre:
                await_all_taken(pe, t)
                s = claim(pe, t)
                for k in range(KT):
                    for half in range(2):
                        c = slice(half * HALF, (half + 1) * HALF)
                        ins = pe.matmul(acc[s][:, c], mean_w[:, :], h[:, k, c], start=(k == 0), stop=(k == KT - 1))
                ins.then_inc(acc_full[s], 1)
                t.next(f"acc{s}")
                t.turn += 1
            sum_squares(pe, t)

        def squares(act, t, k, source):
            if k >= 2:
                act.wait_ge(square_used, t.next("square_used"))
            act.activation(square[:, k % 2, :], source, ACT.Square).then_inc(squared, 1)

        def norm_scalar(act, t, ch, mode, centre=False, eps="eps6", beta=None):
            if centre:
                pass_acc(t)
            elif t.some("acc0"):
                await_all_taken(act, t)
                act.wait_ge(hi_ready, t.count("hi_ready"))
            else:
                act.wait_ge(x_in, 16 * KT)
            for k in range(KT):
                if centre and k < KT - 1:
                    act.wait_ge(centred, t.next("centred"))
                elif centre:
                    act.wait_ge(acc_free[(t.turn - 1) % 2], t.count(f"acc{(t.turn - 1) % 2}"))
                squares(act, t, k, h[:, k, :])
            t.next("square_used")
            s = await_acc(act, t)
            act.activation(rstd[:, :], acc[s], ACT.Sqrt, bias=col(eps)).then_inc(acc_free[s], 1)
            for k in range(KT):
                row = normed[:, k % 2, :]
                act.wait_ge(rows_ready, t.next("rows_ready"))
                if mode == "out":
                    act.dma_start(out_t[k * P:(k + 1) * P, :], out_rows[:, k, :]).then_inc(stored, 16)
                    continue
                if mode == "hold":
                    act.activation(h[:, k, :], row, ACT.Identity, bias=col(beta, k)).then_inc(hi_ready, 1)
                    t.next("hi_ready")
                    continue
                if beta is not None:
                    ch.link(act.activation(row, row, ACT.Identity, bias=col(beta, k)))
                    ch.sync()
                if mode == "keep":
                    ch.link(act.activation(h[:, k, :], row, ACT.Copy, scale=ALPHA))
                split_hi(act, t, row, x_hi[:, k, :])
                t.next("lo_ready")
            if mode in ("split", "keep"):
                act.wait_ge(lo_ready, t.count("lo_ready"))

        def norm_vector(dve, t, ch, mode, gain, centre=False):
            if centre:
                s = await_acc(dve, t)
                for k in range(KT):
                    ins = dve.tensor_tensor(h[:, k, :], h[:, k, :], acc[s], ALU.subtract)
                    ins.then_inc(centred if k < KT - 1 else acc_free[s], 1)
            s = t.turn % 2
            pass_acc(t)
            dve.wait_ge(acc_free[s], t.count(f"acc{s}"))
            for half in range(2):
                c = slice(half * HALF, (half + 1) * HALF)
                ch.link(dve.reciprocal(rstd[:, c], rstd[:, c]))
            ch.sync()
            for k in range(KT + 1):
                if k < KT:
                    if k >= 2 and mode == "hold":
                        dve.wait_ge(hi_ready, t.next("hi_ready"))
                    if k >= 2 and mode in ("split", "keep"):
                        dve.wait_ge(lo_ready, t.count("lo_ready"))
                    row = out_rows[:, k, :] if mode == "out" else normed[:, k % 2, :]
                    dve.scalar_tensor_tensor(out=row, in0=h[:, k, :], scalar=col(gain, k), in1=rstd[:, :],
                                             op0=ALU.mult, op1=ALU.mult).then_inc(rows_ready, 1)
                if k >= 1 and mode in ("split", "keep"):
                    split_lo(dve, t, normed[:, (k - 1) % 2, :], x_hi[:, k - 1, :], x_lo[:, k - 1, :])
            if mode == "hold":
                t.next("hi_ready")
                dve.wait_ge(hi_ready, t.next("hi_ready"))

        def await_parts(pe, t, n):
            for _ in range(n):
                t.next("hi_ready")
                t.next("lo_ready")
            pe.wait_ge(lo_ready, t.count("lo_ready"))

        def att_tensor(pe, t, a, keys):
            def score(n):
                side, p = UNITS[n]
                rows = slice(64 * side, 64 * side + 64)
                first, count, _ = keys(p)
                s = claim(pe, t)
                for c0 in range(0, count, 512):
                    c1 = min(count, c0 + 512)
                    ins = pe.matmul(acc[s][:, c0:c1], a.q_t[rows, p * P:(p + 1) * P],
                                    a.k_t[rows, first + c0:first + c1], start=True, stop=True)
                ins.then_inc(acc_full[s], 1)
                t.next(f"acc{s}")
                t.turn += 1

            def turn_probs(n):
                side, p = UNITS[n]
                count = keys(p)[1]
                pe.wait_ge(p_ready, t.next("p_ready"))
                for c in range(-(-count // P)):
                    w = min(P, count - c * P)
                    ins = pe.transpose(turned[0:w, c * P:(c + 1) * P], a.probs[:, n % 2, c * P:c * P + w], ident[:, :])
                ins.then_inc(turned_full, 1)

            def weigh_values(n):
                side, p = UNITS[n]
                first, count, _ = keys(p)
                cols = slice(64 * side, 64 * side + 64)
                pe.wait_ge(turned_copied, t.next("turned_copied"))
                tiles = -(-count // P)
                for c in range(tiles):
                    w = min(P, count - c * P)
                    ins = pe.matmul(att_out[cols, p * P:(p + 1) * P], a.v_tok[0:w, first // P + c, cols],
                                    a.probs_t[0:w, n % 2, c, :], start=(c == 0), stop=(c == tiles - 1))
                ins.then_inc(pv_done, 1)

            for n in range(len(UNITS) + 2):
                if n < len(UNITS):
                    score(n)
                if n >= 2:
                    weigh_values(n - 2)
                if 1 <= n <= len(UNITS):
                    turn_probs(n - 1)

        def att_vector(dve, t, ch, a, keys, sink=None):
            for n in range(len(UNITS) + 1):
                if n < len(UNITS):
                    side, p = UNITS[n]
                    _, count, bias_at = keys(p)
                    s = await_acc(dve, t)
                    seed = small[:, 60 + n % 2:61 + n % 2]
                    ch.link(dve.memset(seed, 3e38) if sink is None else dve.tensor_copy(seed, sink(side)))
                    ch.sync()
                    dve.tensor_tensor_reduce(
                        out=a.scores[:, n % 2, 0:count], in0=acc[s][:, 0:count],
                        in1=a.bias[:, side, bias_at:bias_at + count], scale=-1.0,
                        scalar=seed, op0=ALU.add, op1=ALU.min,
                        accum_out=small[:, n % 2:n % 2 + 1]).then_inc(acc_free[s], 1)
                if n >= 1:
                    b = (n - 1) % 2
                    count = keys(UNITS[n - 1][1])[1]
                    dve.wait_ge(exp_done, t.next("exp_done"))
                    total = small[:, 2 + b:3 + b]
                    if sink is not None:
                        ch.link(dve.tensor_tensor(total, total, small[:, 6 + b:7 + b], ALU.add))
                        ch.sync()
                    ch.link(dve.reciprocal(small[:, 4 + b:5 + b], total))
                    ch.sync()
                    dve.tensor_scalar(a.probs[:, b, 0:count], a.probs[:, b, 0:count], small[:, 4 + b:5 + b], None,
                                      ALU.mult).then_inc(p_ready, 1)

        def att_scalar(act, t, ch, a, keys, sink=None):
            for n in range(len(UNITS) + 1):
                if n < len(UNITS):
                    side, p = UNITS[n]
                    count = keys(p)[1]
                    s = t.turn % 2
                    pass_acc(t)
                    act.wait_ge(acc_free[s], t.count(f"acc{s}"))
                    if sink is not None:
                        ch.link(act.activation(small[:, 6 + n % 2:7 + n % 2], small[:, n % 2:n % 2 + 1], ACT.Exp,
                                               bias=sink(side)))
                    act.activation(a.probs[:, n % 2, 0:count], a.scores[:, n % 2, 0:count], ACT.Exp, scale=-1.0,
                                   bias=small[:, n % 2:n % 2 + 1],
                                   accum_out=small[:, 2 + n % 2:3 + n % 2]).then_inc(exp_done, 1)
                if n >= 1:
                    count = keys(UNITS[n - 1][1])[1]
                    act.wait_ge(turned_full, t.next("turned_full"))
                    if n >= 3:
                        act.wait_ge(pv_done, t.next("pv_done"))
                    t_full, w = count // P, count % P
                    ins = act.activation(a.probs_t[:, (n - 1) % 2, 0:t_full, :],
                                         turned[:, 0:t_full * P].rearrange("p (c q) -> p c q", q=P), ACT.Copy)
                    if w:
                        ins = act.activation(a.probs_t[0:w, (n - 1) % 2, t_full, :],
                                             turned[0:w, t_full * P:(t_full + 1) * P], ACT.Copy)
                    ins.then_inc(turned_copied, 1)
            t.next("pv_done")
            act.wait_ge(pv_done, t.next("pv_done"))

        def add_rows(dve, t, ch):
            for j in range(KT):
                s = await_acc(dve, t)
                dve.tensor_tensor(h[:, j, :], h[:, j, :], acc[s], ALU.add).then_inc(acc_free[s], 1)

        def projections_tensor(pe, t):
            feature_block(pe, t)
            feature_block(pe, t)
            token_block(pe, t)
            await_all_taken(pe, t)

        def qkv_scalar(act, t, a):
            for dst, scale in ((a.q_t[:, :], 0.125), (a.k_t[:, :], 1.0), (a.v_tok[:, :, :].rearrange("p a b -> p (a b)"), 1.0)):
                s = await_acc(act, t)
                act.activation(dst, acc[s], ACT.Copy, scale=scale).then_inc(acc_free[s], 1)



        def att1_tensor(pe, t):
            await_parts(pe, t, KT)
            with t.loop(2, acc0=19, acc1=19, block=6, p_ready=32, turned_copied=32, hi_ready=2, lo_ready=2):
                for _ in range(2):
                    projections_tensor(pe, t)
                    att_tensor(pe, t, band, keys_1)
                    t.next("hi_ready")
                    t.next("lo_ready")

        def att1_scalar(act, t, ch):
            ch.reset()
            with t.loop(2, acc0=19, acc1=19, turned_full=32, pv_done=32, hi_ready=2, lo_ready=2) as i:
                for q in range(2):
                    act.dma_start(band.bias[:, :, :], bias_1[bass.ds(2 * i + q, 1)].rearrange("a p s k -> p (a s) k"))\
                        .then_inc(bias_in, 16)
                    qkv_scalar(act, t, band)
                    att_scalar(act, t, ch, band, keys_1)
                    act.wait_ge(lo_ready, t.count("lo_ready"))
                    ch.link(act.activation(band.total[:, :], att_out, ACT.Copy))
                    ch.sync()
                    split_hi(act, t, band.total[:, :],
                             att_hi[:, bass.ds(2 * i + q, 1), :].rearrange("p a n -> p (a n)"))
                    t.next("lo_ready")
                ch.reset()

        def att1_vector(dve, t, ch):
            ch.reset()
            with t.loop(2, acc0=19, acc1=19, exp_done=32, bias_in=2, hi_ready=2, lo_ready=2) as i:
                for q in range(2):
                    pass_acc(t, 3)
                    dve.wait_ge(bias_in, t.next("bias_in") * 16)
                    att_vector(dve, t, ch, band, keys_1)
                    where = bass.ds(2 * i + q, 1)
                    split_lo(dve, t, band.total[:, :], att_hi[:, where, :].rearrange("p a n -> p (a n)"),
                             att_lo[:, where, :].rearrange("p a n -> p (a n)"))
                ch.reset()

        def sgu_tensor(pe, t):
            with t.loop(2, acc0=1, acc1=1, block=2):
                token_block(pe, t)
                token_block(pe, t)
            with t.loop(2, acc0=1, acc1=1, block=2):
                feature_block(pe, t)
                feature_block(pe, t)
            pe.wait_ge(sgu_w_ready, 1)
            pe.wait_ge(ln_ready, TT)
            for g in range(SGU_TILES):
                s = claim(pe, t)
                for n in range(TT):
                    ins = pe.matmul(acc[s][:, n * P:(n + 1) * P], vs_tok[:, n, g * P:(g + 1) * P], sgu_wt[:, g, :],
                                    start=True, stop=True)
                ins.then_inc(acc_full[s], 1)
                t.next(f"acc{s}")
                t.turn += 1
            await_parts(pe, t, SGU_TILES)

        def sgu_scalar(act, t, ch):
            act.wait_ge(lo_ready, t.count("lo_ready"))
            act.dma_start(sgu_par[:, :, :], sgu_rows.rearrange("r n -> (r n)").partition_broadcast(P)).then_inc(sgu_in, 16)
            for j in range(4):
                s = await_acc(act, t)
                act.activation(vs_tok[:, :, j * P:(j + 1) * P], acc[s].rearrange("p (a b) -> p a b", b=P),
                               ACT.Gelu_apprx_tanh).then_inc(acc_free[s], 1)
            for j in range(SGU_TILES):
                s = await_acc(act, t)
                act.activation(u_t[:, j, :], acc[s], ACT.Gelu_apprx_tanh).then_inc(acc_free[s], 1)
            act.wait_ge(var_ready, TT)
            act.activation(small[:, 24:32], small[:, 32:48].rearrange("p (n two) -> p n two", two=2)[:, :, 1],
                           ACT.Sqrt, bias=col("eps6")).then_inc(std_ready, 1)
            for g in range(SGU_TILES):
                pass_acc(t)
                act.wait_ge(rows_ready, t.next("rows_ready"))
                split_hi(act, t, mixed[:, :], sgu_hi[:, g, :])
                t.next("lo_ready")
            act.wait_ge(lo_ready, t.count("lo_ready"))
            act.dma_start(h[:, :, :], x_t.rearrange("(k p) n -> p k n", p=P)).then_inc(x_in, 16)

        def sgu_vector(dve, t, ch):
            pass_acc(t, 4)
            for s in range(2):
                dve.wait_ge(acc_free[s], t.count(f"acc{s}"))
            for n in range(TT):
                ch.link(dve.bn_stats(small[:, 48:54], vs_tok[:, n, :]))
                ch.sync()
                ins = dve.bn_aggr(small[:, 32 + 2 * n:34 + 2 * n], small[:, 48:54])
                ins.then_inc(var_ready, 1)
                dve.wait_ge(var_ready, n + 1)
            dve.wait_ge(std_ready, 1)
            ch.link(dve.reciprocal(small[:, 24:32], small[:, 24:32]))
            dve.wait_ge(sgu_in, 32)
            for n in range(TT):
                ch.sync()
                row = vs_tok[:, n, :]
                ch.link(dve.tensor_scalar(row, row, small[:, 32 + 2 * n:33 + 2 * n], small[:, 24 + n:25 + n],
                                          ALU.subtract, ALU.mult))
                ch.sync()
                ch.link(dve.tensor_tensor(row, row, sgu_par[:, 0, :], ALU.mult))
                ch.sync()
                dve.tensor_tensor(row, row, sgu_par[:, 1, :], ALU.add).then_inc(ln_ready, 1)
            pass_acc(t, SGU_TILES)
            for g in range(SGU_TILES):
                s = await_acc(dve, t)
                if g:
                    dve.wait_ge(lo_ready, t.count("lo_ready"))
                b_row = sgu_par[:, 2, g * P:(g + 1) * P].unsqueeze(1).to_broadcast([P, TT, P])
                ins = dve.tensor_tensor(mixed[:, :].rearrange("p (n q) -> p n q", q=P),
                                        acc[s].rearrange("p (n q) -> p n q", q=P), b_row, ALU.add)
                ins.then_inc(acc_free[s], 1)
                dve.wait_ge(acc_free[s], t.count(f"acc{s}"))
                dve.tensor_tensor(mixed[:, :], mixed[:, :], u_t[:, g, :], ALU.mult).then_inc(rows_ready, 1)
                split_lo(dve, t, mixed[:, :], sgu_hi[:, g, :], sgu_lo[:, g, :])

        def merge_gates_tensor(pe, t):
            feature_block(pe, t)
            feature_block(pe, t)

        def merge_branches_tensor(pe, t):
            slot = take_block(pe, t)
            product(pe, t, [(slot, k, att_hi[:, k, :], att_lo[:, k, :]) for k in range(4)], True)
            product(pe, t, [(slot, 4 + k, sgu_hi[:, k, :], sgu_lo[:, k, :]) for k in range(4)], False)

        def merge_rows_tensor(pe, t):
            await_parts(pe, t, 1)
            row_block(pe, t, [(part_hi[:, :], part_lo[:, :])])

        def merge_tensor(pe, t):
            merge_gates_tensor(pe, t)
            merge_branches_tensor(pe, t)
            with t.loop(KT - 1, acc0=6, acc1=6, block=4, hi_ready=1, lo_ready=1):
                merge_gates_tensor(pe, t)
                merge_rows_tensor(pe, t)
                merge_branches_tensor(pe, t)
            merge_rows_tensor(pe, t)

        def merge_gates_scalar(act, t, ch, n):
            for branch in range(2):
                ch.link(act.activation(small[:, 56 + branch:57 + branch],
                                       par[:, bass.ds(n + COL["b_gate"] + 8 * branch, 1)], ACT.Copy))
            ch.reset()
            act.wait_ge(lo_ready, t.count("lo_ready"))
            for branch in range(2):
                s = await_acc(act, t)
                act.activation(gate[:, branch, :], acc[s], ACT.Sigmoid, bias=small[:, 56 + branch:57 + branch])\
                   .then_inc(acc_free[s], 1)

        def merge_branches_scalar(act, t):
            pass_acc(t, 2)
            act.wait_ge(rows_ready, t.next("rows_ready"))
            split_hi(act, t, gate[:, 0, :], part_hi[:, :])
            t.next("lo_ready")

        def merge_scalar(act, t, ch):
            merge_gates_scalar(act, t, ch, 0)
            merge_branches_scalar(act, t)
            ch.reset()
            with t.loop(KT - 1, acc0=6, acc1=6, rows_ready=1, hi_ready=1, lo_ready=1) as i:
                merge_gates_scalar(act, t, ch, i + 1)
                pass_acc(t, KT)
                merge_branches_scalar(act, t)
            pass_acc(t, KT)

        def merge_branches_vector(dve, t, ch):
            for branch in range(2):
                s = t.turn % 2
                s = await_acc(dve, t)
                dve.tensor_tensor(gate[:, branch, :], gate[:, branch, :], acc[s], ALU.mult).then_inc(acc_free[s], 1)
            for s in range(2):
                dve.wait_ge(acc_free[s], t.count(f"acc{s}"))
            dve.tensor_tensor(gate[:, 0, :], gate[:, 0, :], gate[:, 1, :], ALU.add).then_inc(rows_ready, 1)
            split_lo(dve, t, gate[:, 0, :], part_hi[:, :], part_lo[:, :])

        def merge_vector(dve, t, ch):
            pass_acc(t, 2)
            merge_branches_vector(dve, t, ch)
            dve.wait_ge(x_in, 16 * (KT + 1))
            with t.loop(KT - 1, acc0=6, acc1=6, hi_ready=1, lo_ready=1):
                pass_acc(t, 2)
                add_rows(dve, t, ch)
                merge_branches_vector(dve, t, ch)
            add_rows(dve, t, ch)

        def ffn_tensor(pe, t):
            await_parts(pe, t, KT)
            for _ in range(4):
                feature_block(pe, t)
            with t.loop(FFN_PAIRS - 1, acc0=6, acc1=6, block=6, hi_ready=2, lo_ready=2):
                feature_block(pe, t)
                await_parts(pe, t, 2)
                row_block(pe, t, [(hid_hi[:, k, :], hid_lo[:, k, :]) for k in range(2)])
                for _ in range(3):
                    feature_block(pe, t)
            await_parts(pe, t, 2)
            row_block(pe, t, [(hid_hi[:, k, :], hid_lo[:, k, :]) for k in range(2)])

        def hidden_scalar(act, t, rows):
            for k in range(2):
                s = await_acc(act, t)
                if t.some("lo_ready"):
                    act.wait_ge(lo_ready, t.count("lo_ready"))
                act.activation(act_g[:, :], acc[s], ACT.Silu).then_inc(acc_free[s], 1)
                if k == 0 and rows:
                    pass_acc(t, KT)
                s = t.turn % 2
                pass_acc(t)
                act.wait_ge(acc_free[s], t.count(f"acc{s}"))
                split_hi(act, t, hid[:, :], hid_hi[:, k, :])
                t.next("lo_ready")

        def ffn_scalar(act, t, ch):
            hidden_scalar(act, t, False)
            with t.loop(FFN_PAIRS - 1, acc0=6, acc1=6, hi_ready=2, lo_ready=2):
                hidden_scalar(act, t, True)
            pass_acc(t, KT)

        def hidden_vector(dve, t, ch, rows):
            for k in range(2):
                g = t.turn % 2
                pass_acc(t)
                gates = t.count(f"acc{g}")
                if k == 0 and rows:
                    add_rows(dve, t, ch)
                dve.wait_ge(acc_free[g], gates)
                s = await_acc(dve, t)
                dve.wait_ge(lo_ready, t.count("lo_ready"))
                dve.tensor_tensor(hid[:, :], act_g[:, :], acc[s], ALU.mult).then_inc(acc_free[s], 1)
                dve.wait_ge(acc_free[s], t.count(f"acc{s}"))
                split_lo(dve, t, hid[:, :], hid_hi[:, k, :], hid_lo[:, k, :])

        def ffn_vector(dve, t, ch):
            hidden_vector(dve, t, ch, False)
            with t.loop(FFN_PAIRS - 1, acc0=6, acc1=6, hi_ready=2, lo_ready=2):
                hidden_vector(dve, t, ch, True)
            add_rows(dve, t, ch)

        def gates_tensor(pe, t):
            await_parts(pe, t, KT)
            feature_block(pe, t)
            pe.wait_ge(rows_done, 3)
            s = claim(pe, t)
            for half, rows in enumerate((c_rows, m_rows)):
                for n in range(TT):
                    ins = pe.transpose(acc[s][:, half * HALF + n * 64:half * HALF + (n + 1) * 64],
                                       rows[:, n * P:(n + 1) * P], ident[0:64, 0:64])
            ins.then_inc(acc_full[s], 1)
            t.next(f"acc{s}")
            t.turn += 1
            pe.wait_ge(rows_done, 4)
            s = claim(pe, t)
            pe.matmul(acc[s][:, 0:HALF], mean_w[0:64, :], g_diag[:, :, :].rearrange("p a b -> p (a b)"),
                      start=True, stop=True).then_inc(acc_full[s], 1)
            t.next(f"acc{s}")
            t.turn += 1

        def gates_scalar(act, t, ch):
            act.dma_start(masks[:, :, :], consts[:, 2 * P:4 * P].rearrange("p (a b) -> p a b", b=P)).then_inc(mask_in, 16)
            s = await_acc(act, t)
            act.activation(gate_rows[:, :], acc[s], ACT.Identity, bias=col("gate_b")).then_inc(acc_free[s], 1)
            act.wait_ge(rows_done, 1)
            ch.link(act.activation(soft[:, :], soft[:, :], ACT.Exp, scale=-1.0))
            ch.sync()
            act.activation(soft[:, :], soft[:, :], ACT.Ln, bias=1.0).then_inc(soft_ready, 1)
            t.next("soft_ready")
            s = await_acc(act, t)
            ch.link(act.activation(c_col[:, :, :].rearrange("p a b -> p (a b)"), acc[s][:, 0:HALF], ACT.Copy))
            act.activation(em_col[:, :, :, :].rearrange("p a b c -> p (a b c)"), acc[s][:, HALF:TOK], ACT.Exp)\
               .then_inc(acc_free[s], 1)
            s = await_acc(act, t)
            act.activation(g_all[:, :, :].rearrange("p a b -> p (a b)"), acc[s][:, 0:HALF], ACT.Copy,
                           scale=float(D)).then_inc(acc_free[s], 1)
            ch.sync()

        def gates_vector(dve, t, ch):
            s = t.turn % 2
            pass_acc(t)
            dve.wait_ge(acc_free[s], t.count(f"acc{s}"))
            ch.link(dve.tensor_copy(f_rows[:, :], gate_rows[64:128, :]))
            ch.link(dve.memset(carry[:, :], 1.0))
            ch.link(dve.memset(a_col[:, :, :, :, :], 0.0))
            ch.sync()
            ch.link(dve.tensor_scalar(log_f[:, :], f_rows[:, :], -1.0, None, ALU.mult))
            ch.sync()
            dve.tensor_tensor(soft[:, :], f_rows[:, :], log_f[:, :], ALU.max).then_inc(rows_done, 1)
            ch.link(dve.memset(carry[0:32, 0:TOK:P], 0.0))
            ch.link(dve.memset(carry[32:64, P - 1:TOK:P], 0.0))
            dve.wait_ge(soft_ready, t.next("soft_ready"))
            ch.link(dve.scalar_tensor_tensor(out=log_f[:, :], in0=f_rows[:, :], scalar=0.0, in1=soft[:, :],
                                             op0=ALU.min, op1=ALU.subtract))
            ch.sync()
            forward, backward = (slice(0, 32), slice(None)), (slice(32, 64), slice(None, None, -1))
            for at_ in (forward, backward):
                ch.link(dve.tensor_tensor_scan(m_rows[at_], log_f[at_], gate_rows[at_], 0.0, ALU.add, ALU.max))
                ch.link(dve.tensor_tensor_scan(b_rows[at_], carry[at_], log_f[at_], 0.0, ALU.mult, ALU.add))
            ch.sync()
            ch.link(dve.tensor_tensor(r_rows[:, :], b_rows[:, :], m_rows[:, :], ALU.subtract))
            ch.sync()
            dve.tensor_tensor(c_rows[:, :], gate_rows[0:64, :], b_rows[:, :], ALU.subtract).then_inc(rows_done, 1)
            dve.tensor_scalar(m_rows[:, :], m_rows[:, :], -1.0, None, ALU.mult).then_inc(rows_done, 1)
            for n in range(TT):
                for rows, end in ((slice(0, 32), n * P + P - 1), (slice(32, 64), n * P)):
                    ins = dve.tensor_scalar(g_diag[rows, n, :], ident[rows, 0:64], b_rows[rows, end:end + 1], None,
                                            ALU.mult)
                    if n == TT - 1 and end == n * P:
                        ins.then_inc(rows_done, 1)
                    else:
                        ch.link(ins)
            for _ in range(2):
                s = t.turn % 2
                pass_acc(t)
                dve.wait_ge(acc_free[s], t.count(f"acc{s}"))
            for n in range(TT):
                back = TT - 1 - n
                if n:
                    g = g_all[:, n - 1, 0:4].unsqueeze(1).to_broadcast([P, n, 4])
                    ch.link(dve.tensor_tensor(a_col[:, 0, n, 0:n, :], a_col[:, 0, n - 1, 0:n, :], g, ALU.add))
                    g = g_all[:, back + 1, 32:36].unsqueeze(1).to_broadcast([P, n, 4])
                    ch.link(dve.tensor_tensor(a_col[:, 1, back, back + 1:TT, :], a_col[:, 1, back + 1, back + 1:TT, :],
                                              g, ALU.add))
                ch.link(dve.tensor_copy(a_col[:, 0, n, n, :], c_col[:, n, 0:4]))
                ch.link(dve.tensor_copy(a_col[:, 1, back, back, :], c_col[:, back, 32:36]))
                ch.sync()
            ch.link(dve.memset(conv_in[:, :, 0:4], 0.0))
            ch.link(dve.memset(conv_in[:, :, TOK + 4:TOK + 8], 0.0))
            ch.link(dve.memset(v_one[:, :, P:P + 1], 1.0))
            dve.wait_ge(mask_in, 16)
            ch.reset()

        NUM = [turned, att_out]

        def head_tensor(pe, t, rows):
            feature_block(pe, t)
            feature_block(pe, t)
            if rows:
                await_parts(pe, t, 1)
                row_block(pe, t, [(mix_hi[:, :], mix_lo[:, :])])
            token_block(pe, t, padded=rows)
            token_block(pe, t)
            pe.wait_ge(pick_ready, t.next("pick_ready"))
            for way in range(2):
                s = claim(pe, t)
                for half in range(2):
                    c = slice(half * HALF, (half + 1) * HALF)
                    ins = pe.matmul(acc[s][:, c], pick[:, way, :], r_rows[:, c], start=True, stop=True)
                ins.then_inc(acc_full[s], 1)
                t.next(f"acc{s}")
                t.turn += 1
            for _ in range(2):
                pe.wait_ge(conv_ready, t.next("conv_ready"))

            def score(i):
                s = claim(pe, t)
                for j in range(TT):
                    ins = pe.matmul(acc[s][:, j * P:(j + 1) * P], conv_out[:, 1, j * P:(j + 1) * P],
                                    conv_out[:, 0, i * P:(i + 1) * P], start=True, stop=True)
                ins.then_inc(acc_full[s], 1)
                t.next(f"acc{s}")
                t.turn += 1

            def weigh(i):
                s = (t.turn - (2 if i < TT - 1 else 1)) % 2
                pe.wait_ge(acc_free[s], t.count(f"acc{s}"))
                made = t.count("num")
                if t.some("num") and (i == 0 or t.base["num"] >= 2):
                    pe.wait_ge(num_free, made if i == 0 else made - 1)
                for way, tiles in enumerate((range(i + 1), range(i, TT))):
                    out = NUM[i % 2][:, way * HALF:way * HALF + P + 1]
                    for j in tiles:
                        ins = pe.matmul(out, wts[:, i % 3, j + way, :], v_one[:, j, 0:P + 1],
                                        start=(j == tiles[0]), stop=(j == tiles[-1]))
                ins.then_inc(num_full, 1)
                t.next("num")

            score(0)
            for i in range(TT):
                if i < TT - 1:
                    score(i + 1)
                weigh(i)
            pe.wait_ge(h_ready, t.next("h_ready"))
            for i in range(TT):
                ins = pe.transpose(NUM[0][:, i * P:(i + 1) * P], h_tok[:, i, :], ident[:, :])
            ins.then_inc(num_full, 1)
            t.next("num")

        def head_scalar(act, t, ch, rows):
            act.wait_ge(head_ready, t.next("head_ready"))
            for part in range(2):
                s = await_acc(act, t)
                act.activation(conv_in[:, part, 4:TOK + 4], acc[s], ACT.Copy).then_inc(acc_free[s], 1)
            for part in range(2):
                act.wait_ge(conv_summed, t.next("conv_summed"))
                act.activation(conv_out[:, part, :], conv_out[:, part, :], ACT.Silu,
                               bias=head_par[:, TAPS + part * (TAPS + 1):TAPS + 1 + part * (TAPS + 1)])\
                   .then_inc(conv_ready, 1)
            if rows:
                pass_acc(t, KT)
            s = await_acc(act, t)
            act.activation(v_one[:, :, 0:P], acc[s].rearrange("p (a b) -> p a b", b=P), ACT.Copy).then_inc(acc_free[s], 1)
            s = await_acc(act, t)
            act.activation(o_gate[:, :, :].rearrange("p a b -> p (a b)"), acc[s], ACT.Sigmoid).then_inc(acc_free[s], 1)
            for way in range(2):
                s = await_acc(act, t)
                act.activation(r_all[:, way, :], acc[s], ACT.Copy).then_inc(acc_free[s], 1)
            for i in range(TT):
                pass_acc(t)
                act.wait_ge(args_ready, t.next("args_ready"))
                act.activation(wts[:, i % 3, :, :], wts[:, i % 3, :, :], ACT.Exp).then_inc(w_exp, 1)
                t.next("num")
            act.wait_ge(cols_ready, t.next("cols_ready"))
            act.activation(stats[:, 32:40], stats[:, 16:32].rearrange("p (n two) -> p n two", two=2)[:, :, 1], ACT.Sqrt,
                           bias=col("eps6")).then_inc(soft_ready, 1)
            t.next("soft_ready")
            if t.some("lo_ready"):
                act.wait_ge(lo_ready, t.count("lo_ready"))
            act.wait_ge(num_full, t.next("num"))
            act.activation(mix_t[:, :], NUM[0], ACT.Identity, scale=head_par[:, HEAD_PAR - 1:HEAD_PAR]).then_inc(num_free, 1)
            act.wait_ge(num_free, t.count("num"))
            split_hi(act, t, mix_t[:, :], mix_hi[:, :])
            t.next("lo_ready")

        def head_vector(dve, t, ch, head, rows):
            ch.link(dve.tensor_copy(a_head[:, :, :, :].rearrange("p a b c -> p (a b c)"),
                                    a_col[:, :, :, :, :].rearrange("p a b c d -> p (a b c) d")[:, :, bass.ds(head, 1)]
                                    .rearrange("p a b -> p (a b)")))
            ch.link(dve.tensor_copy(em_head[:, :, :].rearrange("p a b -> p (a b)"),
                                    em_col[:, :, :, :].rearrange("p a b c -> p (a b) c")[:, :, bass.ds(head, 1)]
                                    .rearrange("p a b -> p (a b)")))
            dve.tensor_copy(head_par[:, :], par[:, bass.ds(COL["heads"] + head * HEAD_PAR, HEAD_PAR)])\
               .then_inc(head_ready, 1)
            t.next("head_ready")
            for way in range(2):
                ins = dve.tensor_copy(pick[:, way, :], ident[0:64, bass.ds(32 * way + head, 1)].to_broadcast([64, P]))
                ch.link(ins) if way == 0 else ins.then_inc(pick_ready, 1)
            dve.wait_ge(head_ready, t.count("head_ready"))
            for part in range(2):
                s = t.turn % 2
                pass_acc(t)
                dve.wait_ge(acc_free[s], t.count(f"acc{s}"))
                for j in range(TAPS):
                    shifted = conv_in[:, part, 2 + j:2 + j + TOK]
                    tap = head_par[:, part * (TAPS + 1) + j:part * (TAPS + 1) + j + 1]
                    out = conv_out[:, part, :]
                    if j == 0:
                        ins = dve.tensor_scalar(out, shifted, tap, None, ALU.mult)
                    else:
                        ch.sync()
                        ins = dve.scalar_tensor_tensor(out=out, in0=shifted, scalar=tap, in1=out, op0=ALU.mult, op1=ALU.add)
                    ch.link(ins) if j < TAPS - 1 else ins.then_inc(conv_summed, 1)
            if rows:
                add_rows(dve, t, ch)
            pass_acc(t, 2)
            for _ in range(2):
                s = t.turn % 2
                pass_acc(t)
                dve.wait_ge(acc_free[s], t.count(f"acc{s}"))
            ch.sync()

            def arguments(i):
                for way, tiles in enumerate((range(i + 1), range(i, TT))):
                    n = len(tiles)
                    row = r_all[:, way, i * P:(i + 1) * P].unsqueeze(1).to_broadcast([P, n, P])
                    a = a_head[:, way, i, tiles[0]:tiles[-1] + 1].unsqueeze(2).to_broadcast([P, n, P])
                    ch.link(dve.tensor_tensor(wts[:, i % 3, tiles[0] + way:tiles[-1] + 1 + way, :], row, a, ALU.add))
                ch.sync()
                diagonal = wts[:, i % 3, i:i + 2, :]
                dve.tensor_tensor(diagonal, diagonal, masks[:, :, :], ALU.add).then_inc(args_ready, 1)

            def weights(i):
                dve.wait_ge(w_exp, t.next("w_exp"))
                s = await_acc(dve, t)
                for way in range(2):
                    j0, j1 = (0, i + 1) if way == 0 else (i, TT)
                    w = wts[:, i % 3, j0 + way:j1 + way, :].rearrange("p a b -> p (a b)")
                    ins = dve.scalar_tensor_tensor(out=w, in0=acc[s][:, j0 * P:j1 * P], scalar=float(P) ** -0.5, in1=w,
                                                   op0=ALU.mult, op1=ALU.mult)
                    ch.link(ins) if way == 0 else ins.then_inc(acc_free[s], 1)

            def take_sums(i):
                num = NUM[i % 2]
                both = num.rearrange("p (w c) -> p w c", w=2)[:, :, P]
                ch.link(dve.scalar_tensor_tensor(out=stats[:, 0:2], in0=both, scalar=-1.0, in1=em_head[:, i, :],
                                                 op0=ALU.mult, op1=ALU.max))
                ch.sync()
                ch.link(dve.tensor_tensor(stats[:, 0:2], stats[:, 0:2], both, ALU.max))
                ch.sync()
                ch.link(dve.reciprocal(stats[:, 2:4], stats[:, 0:2]))
                ch.sync()
                ch.link(dve.tensor_scalar(h_tok[:, i, :], num[:, 0:P], stats[:, 2:3], None, ALU.mult))
                ch.sync()
                dve.scalar_tensor_tensor(out=h_tok[:, i, :], in0=num[:, HALF:HALF + P], scalar=stats[:, 3:4],
                                         in1=h_tok[:, i, :], op0=ALU.mult, op1=ALU.add).then_inc(num_free, 1)
                dve.wait_ge(num_free, t.count("num"))
                ch.link(dve.bn_stats(stats[:, 4:10], h_tok[:, i, :]))
                ch.sync()
                ins = dve.bn_aggr(stats[:, 16 + 2 * i:18 + 2 * i], stats[:, 4:10])
                ch.link(ins) if i < TT - 1 else ins.then_inc(cols_ready, 1)

            arguments(0)
            arguments(1)
            for i in range(TT + 1):
                if i < TT:
                    weights(i)
                if i >= 1:
                    dve.wait_ge(num_full, t.next("num"))
                if i + 2 < TT:
                    arguments(i + 2)
                if i >= 1:
                    take_sums(i - 1)
            dve.wait_ge(soft_ready, t.next("soft_ready"))
            ch.link(dve.reciprocal(stats[:, 32:40], stats[:, 32:40]))
            mean = stats[:, 16:32].rearrange("p (n two) -> p n two", two=2)[:, :, 0:1].to_broadcast([P, TT, P])
            ch.link(dve.tensor_tensor(h_tok[:, :, :], h_tok[:, :, :], mean, ALU.subtract))
            ch.sync()
            ch.link(dve.tensor_tensor(h_tok[:, :, :], h_tok[:, :, :], stats[:, 32:40].unsqueeze(2).to_broadcast([P, TT, P]),
                                      ALU.mult))
            ch.sync()
            dve.tensor_tensor(h_tok[:, :, :], h_tok[:, :, :], o_gate[:, :, :], ALU.mult).then_inc(h_ready, 1)
            t.next("num")
            split_lo(dve, t, mix_t[:, :], mix_hi[:, :], mix_lo[:, :])

        def mlstm_tensor(pe, t):
            head_tensor(pe, t, False)
            with t.loop(M_HEADS - 1, acc0=11, acc1=11, block=6, hi_ready=1, lo_ready=1, pick_ready=1, conv_ready=2,
                        num=9, h_ready=1):
                head_tensor(pe, t, True)

        def mlstm_scalar(act, t, ch):
            head_scalar(act, t, ch, False)
            with t.loop(M_HEADS - 1, acc0=11, acc1=11, hi_ready=1, lo_ready=1, head_ready=1, conv_summed=2,
                        num=9, args_ready=8, cols_ready=1, soft_ready=1):
                head_scalar(act, t, ch, True)

        def mlstm_vector(dve, t, ch):
            head_vector(dve, t, ch, 0, False)
            ch.reset()
            with t.loop(M_HEADS - 1, acc0=11, acc1=11, hi_ready=1, lo_ready=1, head_ready=1, w_exp=8,
                        num=9, soft_ready=1) as i:
                head_vector(dve, t, ch, i + 1, True)
                ch.reset()

        def window_tensor(pe, t):
            await_parts(pe, t, 1)
            row_block(pe, t, [(mix_hi[:, :], mix_lo[:, :])])
            feature_block(pe, t)
            token_block(pe, t)
            for n in range(HEAD_PAIRS):
                feature_block(pe, t)
                if n:
                    await_parts(pe, t, 1)
                    row_block(pe, t, [(att2_hi[:, :], att2_lo[:, :])])
                await_all_taken(pe, t)
                att_tensor(pe, t, local, keys_2)
            await_parts(pe, t, 1)
            row_block(pe, t, [(att2_hi[:, :], att2_lo[:, :])])

        def take_total(act, t, ch, a, hi):
            act.wait_ge(lo_ready, t.count("lo_ready"))
            ch.link(act.activation(a.total[:, :], att_out, ACT.Copy))
            ch.sync()
            split_hi(act, t, a.total[:, :], hi)
            t.next("lo_ready")

        def window_scalar(act, t, ch):
            pass_acc(t, KT)
            act.wait_ge(lo_ready, t.count("lo_ready"))
            for dst in (local.k_t[:, :], local.v_tok[:, :, :].rearrange("p a b -> p (a b)")):
                s = await_acc(act, t)
                act.activation(dst, acc[s], ACT.Copy).then_inc(acc_free[s], 1)
            for n in range(HEAD_PAIRS):
                act.dma_start(local.bias[:, :, 0:3 * P], bias_2[n]).then_inc(bias_in, 16)
                s = await_acc(act, t)
                act.activation(local.q_t[:, :], acc[s], ACT.Copy, scale=0.125).then_inc(acc_free[s], 1)
                if n:
                    pass_acc(t, KT)
                att_scalar(act, t, ch, local, keys_2, sink=lambda side: col("sink", 2 * n + side))
                take_total(act, t, ch, local, att2_hi[:, :])
            pass_acc(t, KT)

        def window_vector(dve, t, ch):
            add_rows(dve, t, ch)
            pass_acc(t, 2)
            ch.link(dve.tensor_scalar(small[:, 40:48], par[:, COL["sink"]:COL["sink"] + 8], -1.0, None, ALU.mult))
            ch.sync()
            for n in range(HEAD_PAIRS):
                pass_acc(t)
                if n:
                    add_rows(dve, t, ch)
                dve.wait_ge(bias_in, t.next("bias_in") * 16)
                att_vector(dve, t, ch, local, keys_2, sink=lambda side: small[:, 40 + 2 * n + side:41 + 2 * n + side])
                split_lo(dve, t, local.total[:, :], att2_hi[:, :], att2_lo[:, :])
            add_rows(dve, t, ch)

        def ple_tensor(pe, t):
            await_parts(pe, t, 2)
            row_block(pe, t, [(p_hi[:, k, :], p_lo[:, k, :]) for k in range(2)])
            with t.loop(KT // 2, acc0=1, acc1=1, block=2):
                feature_block(pe, t)
                feature_block(pe, t)
            pe.wait_ge(ple_used, KT)

        def ple_scalar(act, t, ch):
            act.wait_ge(lo_ready, t.count("lo_ready"))
            act.dma_start(p_rows[:, :, :], p_t.rearrange("(k p) n -> p k n", p=P)).then_inc(p_in, 16)
            act.wait_ge(p_in, 16)
            for k in range(2):
                split_hi(act, t, p_rows[:, k, :], p_hi[:, k, :])
                t.next("lo_ready")
            for n in range(KT):
                s = await_acc(act, t)
                act.activation(ple[:, n, :], acc[s], ACT.Copy).then_inc(acc_free[s], 1)
            act.wait_ge(lo_ready, t.count("lo_ready"))

            def gates(first):
                for q in range(2):
                    if not first:
                        act.wait_ge(ple_used, t.next("ple_used"))
                    s = await_acc(act, t)
                    act.activation(ple_gate[:, q, :], acc[s], ACT.Sigmoid).then_inc(acc_free[s], 1)

            gates(True)
            with t.loop(KT // 2 - 1, acc0=1, acc1=1, ple_used=2):
                gates(False)

        def ple_vector(dve, t, ch):
            for k in range(2):
                split_lo(dve, t, p_rows[:, k, :], p_hi[:, k, :], p_lo[:, k, :])
            pass_acc(t, KT)
            for s in range(2):
                dve.wait_ge(acc_free[s], t.count(f"acc{s}"))
            ch.reset()
            with t.loop(KT // 2, acc0=1, acc1=1) as i:
                for q in range(2):
                    where = bass.ds(2 * i + q, 1)
                    s = t.turn % 2
                    pass_acc(t)
                    dve.wait_ge(acc_free[s], t.count(f"acc{s}"))
                    ch.link(dve.tensor_tensor(ple_gate[:, q, :], ple_gate[:, q, :],
                                              ple[:, where, :].rearrange("p a n -> p (a n)"), ALU.mult))
                    ch.sync()
                    row = h[:, where, :].rearrange("p a n -> p (a n)")
                    dve.tensor_tensor(row, row, ple_gate[:, q, :], ALU.add).then_inc(ple_used, 1)
                ch.reset()

        def take_turn(pe, t):
            t.next(f"acc{t.turn % 2}")
            t.turn += 1

        def glu_tensor(pe, t):
            await_all_taken(pe, t)
            await_parts(pe, t, KT)
            with t.loop(CONV_TILES // 2, acc0=2, acc1=2, block=4):
                for _ in range(4):
                    feature_block(pe, t)
            with t.loop(CONV_TILES // 2, acc0=1, acc1=1, block=2):
                for _ in range(2):
                    feature_block(pe, t)

        def glu_scalar(act, t, ch):
            with t.loop(CONV_TILES // 2, acc0=2, acc1=2, head_ready=1):
                act.wait_ge(head_ready, t.next("head_ready"))
                for q in range(2):
                    act.wait_ge(acc_free[(t.turn + 1) % 2], t.count(f"acc{(t.turn + 1) % 2}"))
                    s = await_acc(act, t)
                    act.activation(sigmoid[:, q, :], acc[s], ACT.Sigmoid, bias=glu_par[:, q, GLU_PAR - 1:GLU_PAR])\
                       .then_inc(acc_free[s], 1)
                    pass_acc(t)
            for j in range(CONV_TILES):
                s = await_acc(act, t)
                act.activation(z_conv[j], acc[s], ACT.Silu, bias=col("b_z", j)).then_inc(acc_free[s], 1)

        def glu_vector(dve, t, ch):
            ch.link(dve.memset(u_pad[:, :, :], 0.0))
            ch.reset()
            with t.loop(CONV_TILES // 2, acc0=2, acc1=2, head_ready=1) as i:
                dve.tensor_copy(glu_par[:, :, :].rearrange("p a b -> p (a b)"),
                                par[:, bass.ds(COL["glu"] + i * (2 * GLU_PAR), 2 * GLU_PAR)]).then_inc(head_ready, 1)
                t.next("head_ready")
                for q in range(2):
                    s = t.turn % 2
                    pass_acc(t)
                    dve.wait_ge(acc_free[s], t.count(f"acc{s}"))
                    s = await_acc(dve, t)
                    if q == 0:
                        dve.wait_ge(head_ready, t.count("head_ready"))
                    dve.scalar_tensor_tensor(out=u_pad[:, q, REACH:REACH + TOK], in0=acc[s],
                                             scalar=glu_par[:, q, GLU_PAR - 2:GLU_PAR - 1], in1=sigmoid[:, q, :],
                                             op0=ALU.add, op1=ALU.mult).then_inc(acc_free[s], 1)
                    dve.wait_ge(acc_free[s], t.count(f"acc{s}"))
                    out = conv_sum[:, bass.ds(2 * i + q, 1), :].rearrange("p a n -> p (a n)")
                    for j in range(CONV_TAPS):
                        tap, shifted = glu_par[:, q, j:j + 1], u_pad[:, q, j:j + TOK]
                        if j == 0:
                            ch.link(dve.tensor_scalar(out, shifted, tap, glu_par[:, q, CONV_TAPS:CONV_TAPS + 1],
                                                      ALU.mult, ALU.add))
                        else:
                            ch.sync()
                            ch.link(dve.scalar_tensor_tensor(out=out, in0=shifted, scalar=tap, in1=out,
                                                             op0=ALU.mult, op1=ALU.add))
                ch.reset()
            pass_acc(t, CONV_TILES)
            dve.memset(small[:, 62:63], 0.0).then_inc(conv_done, 1)

        def conv_tensor(pe, t):
            pe.wait_ge(conv_done, 1)
            s = claim(pe, t)
            for k in range(CONV_TILES):
                for half in range(2):
                    c = slice(half * HALF, (half + 1) * HALF)
                    ins = pe.matmul(acc[s][:, c], mean_w[:, :], conv_sum[:, k, c], start=(k == 0), stop=(k == CONV_TILES - 1))
            ins.then_inc(acc_full[s], 1)
            take_turn(pe, t)
            sum_squares(pe, t, CONV_TILES)
            await_parts(pe, t, CONV_TILES)
            for _ in range(CONV_TILES // 2):
                slot = take_block(pe, t)
                for o in range(2):
                    product(pe, t, [(slot, 4 * o + k, c_hi[:, k, :], c_lo[:, k, :]) for k in range(4)], o == 0)
            for g in range(CONV_TILES):
                group_sums(pe, t, square3[:, g % 3, :])
            await_parts(pe, t, CONV_TILES)
            row_block(pe, t, [(c_hi[:, k, :], c_lo[:, k, :]) for k in range(CONV_TILES)])

        def group_sums(pe, t, squares_of):
            pe.wait_ge(group_in, 16)
            pe.wait_ge(squared, t.next("squared"))
            s = claim(pe, t)
            for half in range(2):
                c = slice(half * HALF, (half + 1) * HALF)
                ins = pe.matmul(acc[s][:, c], group_w[:, :], squares_of[:, c], start=True, stop=True)
            ins.then_inc(acc_full[s], 1)
            take_turn(pe, t)

        def conv_scalar(act, t, ch):
            act.dma_start(group_w[:, :], consts[:, 4 * P:5 * P]).then_inc(group_in, 16)
            pass_acc(t)
            for k in range(CONV_TILES):
                if k < CONV_TILES - 1:
                    act.wait_ge(centred, t.next("centred"))
                else:
                    act.wait_ge(acc_free[(t.turn - 1) % 2], t.count(f"acc{(t.turn - 1) % 2}"))
                squares(act, t, k, conv_sum[:, k, :])
            t.next("square_used")
            s = await_acc(act, t)
            act.activation(rstd[:, :], acc[s], ACT.Sqrt, bias=col("eps6"), scale=2.0).then_inc(acc_free[s], 1)
            for k in range(CONV_TILES):
                row = conv_sum[:, k, :]
                act.wait_ge(rows_ready, t.next("rows_ready"))
                ch.link(act.activation(row, row, ACT.Silu, bias=col("cln_b", k)))
                ch.sync()
                split_hi(act, t, row, c_hi[:, k, :])
                t.next("lo_ready")

            def square_group(g):
                act.activation(square3[:, g % 3, :], y_conv[:, g, :], ACT.Square).then_inc(squared, 1)

            for g in range(CONV_TILES):
                s = await_acc(act, t)
                act.activation(y_conv[:, g, :], acc[s], ACT.Identity, bias=col("pw_b", g)).then_inc(acc_free[s], 1)
                if g < 3:
                    act.wait_ge(acc_free[s], t.count(f"acc{s}"))
                    if g == 2:
                        act.wait_ge(lo_ready, t.count("lo_ready"))
                    square_group(g)
            for g in range(CONV_TILES):
                s = await_acc(act, t)
                act.activation(square3[:, g % 3, :], acc[s], ACT.Sqrt, bias=col("eps6")).then_inc(acc_free[s], 1)
                act.wait_ge(rows_ready, t.next("rows_ready"))
                split_hi(act, t, y_conv[:, g, :], c_hi[:, g, :])
                t.next("lo_ready")
                if g == 0:
                    square_group(3)
            pass_acc(t, KT)
            await_all_taken(act, t)

        def gate_group(dve, ch, t, y, root, gain, z):
            for half in range(2):
                c = slice(half * HALF, (half + 1) * HALF)
                ch.link(dve.reciprocal(root[:, c], root[:, c]))
            ch.sync()
            ch.link(dve.scalar_tensor_tensor(out=y, in0=y, scalar=gain, in1=root, op0=ALU.mult, op1=ALU.mult))
            ch.sync()
            dve.tensor_tensor(y, y, z, ALU.mult).then_inc(rows_ready, 1)

        def conv_vector(dve, t, ch):
            s = await_acc(dve, t)
            for k in range(CONV_TILES):
                ins = dve.scalar_tensor_tensor(out=conv_sum[:, k, :], in0=acc[s], scalar=-2.0, in1=conv_sum[:, k, :],
                                               op0=ALU.mult, op1=ALU.add)
                ins.then_inc(centred if k < CONV_TILES - 1 else acc_free[s], 1)
            s = t.turn % 2
            pass_acc(t)
            dve.wait_ge(acc_free[s], t.count(f"acc{s}"))
            for half in range(2):
                c = slice(half * HALF, (half + 1) * HALF)
                ch.link(dve.reciprocal(rstd[:, c], rstd[:, c]))
            ch.sync()
            for k in range(CONV_TILES + 1):
                if k < CONV_TILES:
                    row = conv_sum[:, k, :]
                    dve.scalar_tensor_tensor(out=row, in0=row, scalar=col("cln_g", k), in1=rstd[:, :],
                                             op0=ALU.mult, op1=ALU.mult).then_inc(rows_ready, 1)
                if k >= 1:
                    split_lo(dve, t, conv_sum[:, k - 1, :], c_hi[:, k - 1, :], c_lo[:, k - 1, :])
            pass_acc(t, CONV_TILES)
            for g in range(CONV_TILES):
                s = t.turn % 2
                pass_acc(t)
                dve.wait_ge(acc_free[s], t.count(f"acc{s}"))
                gate_group(dve, ch, t, y_conv[:, g, :], square3[:, g % 3, :], col("gn_conv", g), z_conv[g])
                split_lo(dve, t, y_conv[:, g, :], c_hi[:, g, :], c_lo[:, g, :])
            add_rows(dve, t, ch)

        def near_projections(pe, t):
            feature_block(pe, t)
            feature_block(pe, t)
            token_block(pe, t)
            feature_block(pe, t)

        def near_rows(pe, t):
            group_sums(pe, t, square[:, 1, :])
            await_parts(pe, t, 1)
            row_block(pe, t, [(att2_hi[:, :], att2_lo[:, :])])

        def near_tensor(pe, t):
            with t.loop(HEAD_PAIRS // 2, acc0=29, acc1=29, block=10, p_ready=32, turned_copied=32, squared=2,
                        hi_ready=2, lo_ready=2):
                near_projections(pe, t)
                await_all_taken(pe, t)
                att_tensor(pe, t, local, keys_3)
                near_projections(pe, t)
                near_rows(pe, t)
                await_all_taken(pe, t)
                att_tensor(pe, t, local, keys_3)
                near_rows(pe, t)

        def near_scalar(act, t, ch):
            def project(pair, q):
                own = pair_par[:, q, :]
                act.dma_start(local.bias[:, :, :], bias_3[bass.ds(pair, 1)].rearrange("a p s k -> p (a s) k"))\
                    .then_inc(bias_in, 16)
                ch.link(act.activation(own[:, 0:PAIR_PAR], par[:, bass.ds(COL["pairs"] + pair * PAIR_PAR, PAIR_PAR)],
                                       ACT.Copy))
                ch.sync()
                ch.link(act.activation(own[:, 5:6], own[:, 0:1], ACT.Copy, scale=0.125))
                ch.sync()
                for dst, func, scale, bias in ((local.q_t[:, :], ACT.Identity, 0.125, own[:, 5:6]),
                                               (local.k_t[:, :], ACT.Identity, 1.0, own[:, 1:2]),
                                               (local.v_tok[:, :, :].rearrange("p a b -> p (a b)"), ACT.Copy, 1.0, 0.0),
                                               (z_att[:, q, :], ACT.Silu, 1.0, own[:, 3:4])):
                    s = await_acc(act, t)
                    act.activation(dst, acc[s], func, scale=scale, bias=bias).then_inc(acc_free[s], 1)

            def outputs(q):
                ch.link(act.activation(local.total[:, :], att_out, ACT.Identity, bias=pair_par[:, q, 2:3]))
                ch.sync()
                act.activation(square[:, 1, :], local.total[:, :], ACT.Square).then_inc(squared, 1)

            def gated_outputs():
                s = await_acc(act, t)
                act.activation(rstd[:, :], acc[s], ACT.Sqrt, bias=col("eps6")).then_inc(acc_free[s], 1)
                act.wait_ge(rows_ready, t.next("rows_ready"))
                split_hi(act, t, local.total[:, :], att2_hi[:, :])
                t.next("lo_ready")
                pass_acc(t, KT)

            ch.reset()
            with t.loop(HEAD_PAIRS // 2, acc0=29, acc1=29, turned_full=32, pv_done=32, rows_ready=2, hi_ready=2,
                        lo_ready=2) as i:
                act.wait_ge(lo_ready, t.count("lo_ready"))
                project(2 * i, 0)
                att_scalar(act, t, ch, local, keys_3)
                outputs(0)
                project(2 * i + 1, 1)
                gated_outputs()
                att_scalar(act, t, ch, local, keys_3)
                outputs(1)
                gated_outputs()
                ch.reset()

        def near_vector(dve, t, ch):
            def gated_outputs(q):
                s = t.turn % 2
                pass_acc(t)
                dve.wait_ge(acc_free[s], t.count(f"acc{s}"))
                gate_group(dve, ch, t, local.total[:, :], rstd[:, :], pair_par[:, q, 4:5], z_att[:, q, :])
                split_lo(dve, t, local.total[:, :], att2_hi[:, :], att2_lo[:, :])
                add_rows(dve, t, ch)

            ch.reset()
            with t.loop(HEAD_PAIRS // 2, acc0=29, acc1=29, exp_done=32, bias_in=2, hi_ready=2, lo_ready=2):
                pass_acc(t, 4)
                dve.wait_ge(bias_in, t.next("bias_in") * 16)
                att_vector(dve, t, ch, local, keys_3)
                pass_acc(t, 4)
                gated_outputs(0)
                dve.wait_ge(bias_in, t.next("bias_in") * 16)
                att_vector(dve, t, ch, local, keys_3)
                gated_outputs(1)
                ch.reset()


        @block.sync
        def _(sp):
            sp.dma_start(raw[:, 0, :], blocks[0]).then_inc(raw_in[0], 16)
            sp.dma_start(raw[:, 1, :], blocks[1]).then_inc(raw_in[1], 16)
            with sp.Fori(1, n_blocks // 2) as i:
                for slot in range(2):
                    sp.wait_ge(w_split, 2 * i - 1 + slot)
                    sp.dma_start(raw[:, slot, :], blocks[bass.ds(2 * i + slot, 1)].rearrange("a p n -> p (a n)"))\
                      .then_inc(raw_in[slot], 16)

        @block.gpsimd
        def _(pool):
            pool.memset(zero[:, :], 0.0).then_inc(zero_ready, 1)
            pool.wait_ge(zero_ready, 1)
            pool.wait_ge(sgu_in, 16)
            pool.affine_select(out=sgu_wt[:, :, :], in_=sgu_wt[:, :, :], compare_op=ALU.is_ge, fill=0.0, base=0,
                               pattern=[[0, 4], [1, P]], channel_multiplier=-1).then_inc(sgu_w_ready, 1)
            nothing = zero[:, 0:1].to_broadcast([P, 1024])

            def split_block(slot):
                whole = raw[:, slot, :]
                hi = w_hi[:, slot, :, :].rearrange("p a b -> p (a b)")
                pool.tensor_tensor(hi, whole, nothing, ALU.add).then_inc(hi_split, 1)
                return whole, hi, w_lo[:, slot, :, :].rearrange("p a b -> p (a b)")

            for b in range(2):
                pool.wait_ge(raw_in[b], 16)
                whole, hi, lo = split_block(b)
                pool.wait_ge(hi_split, b + 1)
                pool.tensor_tensor(lo, whole, hi.bitcast(F32), ALU.subtract).then_inc(w_split, 1)
            with pool.Fori(1, n_blocks // 2) as i:
                for slot in range(2):
                    pool.wait_ge(w_used, 2 * i + slot)
                    pool.wait_ge(raw_in[slot], 16 * i + 16)
                    whole, hi, lo = split_block(slot)
                    pool.wait_ge(hi_split, 2 * i + slot + 1)
                    pool.tensor_tensor(lo, whole, hi.bitcast(F32), ALU.subtract).then_inc(w_split, 1)

        @block.tensor
        def _(pe):
            t = Turns(pe)
            pe.wait_ge(const_in, 48)
            norm_tensor(pe, t)
            att1_tensor(pe, t)
            sgu_tensor(pe, t)
            merge_tensor(pe, t)
            norm_tensor(pe, t)
            ffn_tensor(pe, t)
            norm_tensor(pe, t)
            gates_tensor(pe, t)
            mlstm_tensor(pe, t)
            window_tensor(pe, t)
            norm_tensor(pe, t, centre=True)
            ffn_tensor(pe, t)
            ple_tensor(pe, t)
            norm_tensor(pe, t, centre=True)
            norm_tensor(pe, t)
            glu_tensor(pe, t)
            conv_tensor(pe, t)
            near_tensor(pe, t)
            norm_tensor(pe, t)

        @block.scalar
        def _(act):
            t, ch = Turns(act), Chain(act, s_chain)
            act.dma_start(par[:, :], params).then_inc(const_in, 16)
            act.dma_start(ident[:, :], consts[:, 0:P]).then_inc(const_in, 16)
            act.dma_start(mean_w[:, :], consts[:, P:2 * P]).then_inc(const_in, 16)
            act.dma_start(sgu_wt[:, :, :], sgu_w).then_inc(sgu_in, 16)
            for k in range(KT):
                act.dma_start(h[:, k, :], x_t[k * P:(k + 1) * P, :]).then_inc(x_in, 16)
            act.wait_ge(const_in, 48)
            norm_scalar(act, t, ch, "split")
            att1_scalar(act, t, ch)
            sgu_scalar(act, t, ch)
            merge_scalar(act, t, ch)
            norm_scalar(act, t, ch, "split")
            ffn_scalar(act, t, ch)
            norm_scalar(act, t, ch, "keep")
            gates_scalar(act, t, ch)
            mlstm_scalar(act, t, ch)
            window_scalar(act, t, ch)
            norm_scalar(act, t, ch, "keep", centre=True, eps="eps5", beta="ln1_b")
            ffn_scalar(act, t, ch)
            ple_scalar(act, t, ch)
            norm_scalar(act, t, ch, "hold", centre=True, eps="eps5", beta="ln2_b")
            norm_scalar(act, t, ch, "split")
            glu_scalar(act, t, ch)
            conv_scalar(act, t, ch)
            near_scalar(act, t, ch)
            norm_scalar(act, t, ch, "out")
            act.wait_ge(stored, 16 * KT)

        @block.vector
        def _(dve):
            t, ch = Turns(dve), Chain(dve, v_chain)
            dve.wait_ge(const_in, 48)
            norm_vector(dve, t, ch, "split", "norm_mix")
            att1_vector(dve, t, ch)
            sgu_vector(dve, t, ch)
            merge_vector(dve, t, ch)
            norm_vector(dve, t, ch, "split", "norm_ffn")
            ffn_vector(dve, t, ch)
            norm_vector(dve, t, ch, "keep", "norm_final")
            gates_vector(dve, t, ch)
            mlstm_vector(dve, t, ch)
            window_vector(dve, t, ch)
            norm_vector(dve, t, ch, "keep", "ln1_g", centre=True)
            ffn_vector(dve, t, ch)
            ple_vector(dve, t, ch)
            norm_vector(dve, t, ch, "hold", "ln2_g", centre=True)
            norm_vector(dve, t, ch, "split", "ln3_g")
            glu_vector(dve, t, ch)
            conv_vector(dve, t, ch)
            near_vector(dve, t, ch)
            norm_vector(dve, t, ch, "out", "final_g")


def tile(w, k, n):
    return w[k * P:(k + 1) * P, n * P:(n + 1) * P]


def column_block(w, n):
    return w[:, n * P:(n + 1) * P].reshape(KT, P, P).transpose(1, 0, 2)


def row_blocks(w, k, n=1):
    parts = w[k * P:(k + n) * P].reshape(n, P, KT, P).transpose(1, 2, 0, 3)
    return [parts[:, g * (KT // n):(g + 1) * (KT // n)].reshape(P, KT, P) for g in range(n)]


def ffn_blocks(w_in, w_out):
    hidden = w_in.shape[1] // 2 // P
    for i in range(hidden // 2 + 1):
        columns = [c for k in (2 * i, 2 * i + 1) if k < hidden for c in (k, hidden + k)]
        rows = row_blocks(w_out, 2 * i - 2, 2) if i else []
        yield from [column_block(w_in, c) for c in columns[:1]] + rows + [column_block(w_in, c) for c in columns[1:]]


def first_blocks(w_in, w_br_att, w_br_sgu, w_out, w_ffn_in, w_ffn_out):
    for hp in range(HEAD_PAIRS):
        for group in range(3):
            yield column_block(w_in, 4 * group + hp)
    for group in (4, 3):
        for j in range(4):
            yield column_block(w_in, 4 * group + j)
    for n in range(KT + 1):
        if n < KT:
            yield column_block(w_in, 20 + n)
            yield column_block(w_in, 28 + n)
        if n:
            yield from row_blocks(w_out, n - 1)
        if n < KT:
            both = np.concatenate([w_br_att, w_br_sgu])[:, n * P:(n + 1) * P]
            yield both.reshape(KT, P, P).transpose(1, 0, 2)
    yield from ffn_blocks(w_ffn_in, w_ffn_out)


def spread_gates(v):
    out = np.zeros(v.shape[:-1] + (P,), np.float32)
    for group in range(4):
        out[..., 32 * group:32 * group + M_HEADS] = v[..., M_HEADS * group:M_HEADS * (group + 1)]
    return out


def second_blocks(w_in, w_out, w_ffn_in, w_ffn_out, w_ple_gate, w_ple_proj):
    gates, a_q, a_k = 2048, 2064, 2576
    yield column_block(spread_gates(w_in[:, gates:a_q]), 0)
    for head in range(M_HEADS):
        yield column_block(w_in, head)
        yield column_block(w_in, 4 + head)
        if head:
            yield from row_blocks(w_out, head - 1)
            yield np.zeros((P, KT, P), np.float32)
        yield column_block(w_in, 8 + head)
        yield column_block(w_in, 12 + head)
    yield from row_blocks(w_out, M_HEADS - 1)
    yield column_block(w_in[:, a_k:], 0)
    yield column_block(w_in[:, a_k:], 1)
    q_heads = w_in[:, a_q:a_k].reshape(D, 2, 4, 64)
    out_heads = w_out[512:].reshape(2, 4, 64, D)
    for n in range(HEAD_PAIRS + 1):
        if n < HEAD_PAIRS:
            yield column_block(q_heads[:, :, n].reshape(D, P), 0)
        if n:
            yield from row_blocks(out_heads[:, n - 1].reshape(P, D), 0)
    yield from ffn_blocks(w_ffn_in, w_ffn_out)
    yield from row_blocks(w_ple_proj, 0, 2)
    for n in range(KT):
        yield column_block(w_ple_gate, n)


def third_blocks(w_in, pw_w, w_out):
    for j in range(CONV_TILES):
        yield column_block(w_in, 4 + j)
        yield column_block(w_in, j)
    for j in range(CONV_TILES):
        yield column_block(w_in, 8 + j)
    for b in range(2):
        yield pw_w[:, 2 * b * P:(2 * b + 2) * P].reshape(4, P, 2, P).transpose(1, 2, 0, 3).reshape(P, KT, P)
    yield from row_blocks(w_out, 0, 4)
    for i in range(HEAD_PAIRS // 2):
        for pair in (2 * i, 2 * i + 1):
            for group in (12, 16, 20, 24):
                yield column_block(w_in, group + pair)
        for pair in (2 * i, 2 * i + 1):
            yield from row_blocks(w_out, 4 + pair)


def near_bias(rpb):
    table = np.full((HEADS, P, N_BIAS_3), NEG, np.float32)
    for p in (0, 1, 2, 6, 7):
        first, count, at = BIAS_3[p]
        q, k = p * P + np.arange(P)[:, None], first + np.arange(count)[None, :]
        row, column, key_row, key_column = q // 64, q % 64, k // 64, k % 64
        row_start, column_start = np.clip(row - 4, 0, 8), np.clip(column - 8, 0, 48)
        seen = (key_row >= row_start) & (key_row < row_start + 8) \
            & (key_column >= column_start) & (key_column < column_start + 16)
        row_at, column_at = np.clip(key_row - row + 7, 0, 14), np.clip(key_column - column + 15, 0, 30)
        table[:, :, at:at + count] = np.where(seen, rpb[:, row_at, column_at], np.float32(NEG))
    return np.ascontiguousarray(table.reshape(HEAD_PAIRS, 2, P, N_BIAS_3).transpose(0, 2, 1, 3))


def window_bias():
    q, k = np.arange(P)[:, None], np.arange(3 * P)[None, :] - P
    distance = np.abs(k - q).astype(np.float32)
    slopes = np.exp2(-np.arange(1, HEADS + 1, dtype=np.float32))
    table = np.where(distance <= P, -slopes[:, None, None] * distance, np.float32(NEG))
    return np.ascontiguousarray(table.reshape(2, HEAD_PAIRS, P, 3 * P).transpose(1, 2, 0, 3))


def per_feature(v):
    return np.asarray(v).reshape(-1, P).T


def banded_bias(rel_bias):
    q, k = np.arange(P)[:, None], np.arange(ATT_BIAS_1)[None, :]
    distance = np.clip(q - (k - 512), -128, 128) + 128
    key_chunk, query_chunk = k // 64 - 8, q // 64
    seen = (key_chunk <= query_chunk) & (key_chunk >= query_chunk - 8)
    table = np.where(seen[None], rel_bias[:, distance], np.float32(NEG))
    return np.ascontiguousarray(table.reshape(HEAD_PAIRS, 2, P, ATT_BIAS_1).transpose(0, 2, 1, 3))


_INS = ["x_t", "blocks", "params", "consts", "bias_1", "bias_2", "bias_3", "sgu_rows", "sgu_w", "p_t"]


def kernel(**inputs):
    import concourse.bacc as bacc
    from concourse.bass_utils import run_bass_kernel_spmd

    g = {name: np.asarray(a) for name, a in inputs.items()}
    stream = list(first_blocks(g["w_in"][0], g["w_br_att"][0], g["w_br_sgu"][0], g["w_out"][0],
                               g["w_ffn_in"][0], g["w_ffn_out"][0]))
    stream += second_blocks(g["w_in_2"][0], g["w_out_2"][0], g["w_ffn_in_2"][0], g["w_ffn_out_2"][0],
                            g["w_ple_gate_2"][0], g["w_ple_proj_2"][0])
    stream += third_blocks(g["w_in_3"][0], g["pw_w_3"][0], g["w_out_3"][0])
    if len(stream) % 2:
        stream.append(stream[-1])
    params = np.zeros((P, N_PARAMS), np.float32)

    def put(name, columns):
        columns = np.asarray(columns)
        params[:, COL[name]:COL[name] + columns.shape[1]] = columns

    put("norm_mix", per_feature(g["norm_mix"][0]))
    put("b_gate", per_feature(g["b_gate"][0]))
    put("norm_ffn", per_feature(g["norm_ffn"][0]))
    put("norm_final", per_feature(g["norm_final"]))
    conv = np.concatenate([g["conv_w_2"][0], g["conv_b_2"]]).reshape(TAPS + 1, 2, M_HEADS, P)
    for head in range(M_HEADS):
        own = np.concatenate([conv[:, :, head].transpose(2, 1, 0).reshape(P, -1),
                              g["mlstm_norm_g_2"][0, head * P:(head + 1) * P, None]], 1)
        params[:, COL["heads"] + head * HEAD_PAR:COL["heads"] + (head + 1) * HEAD_PAR] = own
    put("gate_b", spread_gates(g["b_gate_2"]).T)
    put("sink", np.broadcast_to(g["attn_sink_2"][0].reshape(2, HEAD_PAIRS).T.reshape(1, HEADS), (P, HEADS)))
    for name in ("ln1_g", "ln1_b", "ln2_g", "ln2_b"):
        put(name, per_feature(g[name + "_2"][0]))
    put("ln3_g", per_feature(g["ln_g_3"][0]))
    b_in = per_feature(g["b_in_3"][0])
    taps = g["dw_w_3"][0].reshape(CONV_TAPS, CONV_TILES, P).transpose(2, 1, 0)
    glu = np.concatenate([taps, per_feature(g["dw_b_3"][0])[:, :, None], b_in[:, 0:4, None], b_in[:, 4:8, None]], 2)
    put("glu", glu.reshape(P, -1))
    put("b_z", b_in[:, 8:12])
    gains = per_feature(g["gn_att_g_3"][0])
    put("pairs", np.stack([b_in[:, 12:16], b_in[:, 16:20], b_in[:, 20:24], b_in[:, 24:28], gains], 2).reshape(P, -1))
    for name, source in (("cln_g", "cln_g_3"), ("cln_b", "cln_b_3"), ("pw_b", "pw_b_3"), ("gn_conv", "gn_conv_g_3")):
        put(name, per_feature(g[source][0]))
    put("final_g", per_feature(g["final_g_3"]))
    put("eps5", np.full((P, 1), 1e-5))
    put("eps6", np.full((P, 1), EPS))
    arrays = {
        "x_t": np.ascontiguousarray(g["x"][0].T),
        "blocks": np.stack(stream).reshape(len(stream), P, 1024),
        "params": params,
        "consts": np.concatenate([np.eye(P), np.full((P, P), 1.0 / D), np.tril(np.full((P, P), NEG), -1),
                                  np.triu(np.full((P, P), NEG), 1),
                                  np.kron(np.eye(2), np.full((64, 64), 1.0 / 64))], 1).astype(np.float32),
        "bias_1": banded_bias(g["att_rel_bias"][0]),
        "bias_2": window_bias(),
        "bias_3": near_bias(g["rpb_3"][0]),
        "p_t": np.ascontiguousarray(g["p_2"][0, 0].T),
        "sgu_rows": np.stack([g["sgu_norm_gain"][0], g["sgu_norm_bias"][0], g["sgu_b"][0].reshape(-1)]),
        "sgu_w": np.ascontiguousarray(g["sgu_w"][0].transpose(2, 0, 1)),
    }
    nc = bacc.Bacc("TRN2", target_bir_lowering=False, num_devices=1)
    refs = {n: nc.dram_tensor(n, arrays[n].shape, F32, kind="ExternalInput").ap() for n in _INS}
    out_t = nc.dram_tensor("out_t", (D, TOK), F32, kind="ExternalOutput").ap()
    mixer_program(nc, n_blocks=len(stream), out_t=out_t, **refs)
    got = run_bass_kernel_spmd(nc, [arrays], core_ids=[0]).results[0]["out_t"]
    return np.ascontiguousarray(got.T)[None]
```

```python
from contextlib import ExitStack, contextmanager

import numpy as np
import concourse.bass as bass
from concourse import mybir

F32 = mybir.dt.float32
F32R = mybir.dt.float32r
ALU = mybir.AluOpType
ACT = mybir.ActivationFunctionType

P = 128
TOK = 1024
HALF = 512
D = 1024
KT = D // P
TT = TOK // P
EPS = 1e-6
ALPHA = 2.0 ** 0.25
NEG = -1e30


class Buffers:

    def __init__(self, q_t, k_t, v_tok, v_t, scores, probs, probs_t, total, bias):
        self.q_t, self.k_t, self.v_tok, self.v_t, self.scores = q_t, k_t, v_tok, v_t, scores
        self.probs, self.probs_t, self.total, self.bias = probs, probs_t, total, bias


class Turns:

    def __init__(self, engine):
        self.engine, self.base, self.per, self.reg, self.start = engine, {}, {}, None, {}
        self.turn = self.block = 0

    def count(self, name):
        n = self.base.get(name, 0)
        return n if self.reg is None or not self.per.get(name) else self.reg * self.per[name] + n

    def next(self, name):
        self.base[name] = self.base.get(name, 0) + 1
        return self.count(name)

    def some(self, name):
        return self.base.get(name, 0) > 0

    @contextmanager
    def loop(self, times, **per):
        first, turn, block = dict(self.base), self.turn, self.block
        with self.engine.Fori(0, times) as i:
            self.reg, self.per = i, per
            yield i
        self.reg, self.per = None, {}
        for name in {*self.base, *first}:
            grown = self.base.get(name, 0) - first.get(name, 0)
            assert grown == per.get(name, 0), (name, grown, per.get(name, 0))
            self.base[name] = first.get(name, 0) + grown * times
        assert (self.turn - turn) % 2 == 0 and (self.block - block) % 2 == 0


class Chain:

    def __init__(self, engine, sem):
        self.engine, self.sem, self.n, self.waited = engine, sem, 0, 0

    def link(self, instruction):
        instruction.then_inc(self.sem, 1)
        self.n += 1
        return instruction

    def sync(self):
        if self.n > self.waited:
            self.engine.wait_ge(self.sem, self.n)
            self.waited = self.n

    def reset(self):
        self.sync()
        if self.n:
            self.engine.sem_clear(self.sem)
        self.n = self.waited = 0


PARAMS = [("norm_mix", 8), ("b_gate", 16), ("norm_ffn", 8), ("norm_final", 8),
          ("heads", 52), ("gate_b", 1), ("sink", 8),
          ("ln1_g", 8), ("ln1_b", 8), ("ln2_g", 8), ("ln2_b", 8),
          ("ln3_g", 8), ("glu", 136), ("b_z", 4), ("cln_g", 4), ("cln_b", 4),
          ("pw_b", 4), ("gn_conv", 4), ("pairs", 20), ("final_g", 8),
          ("eps6", 1), ("eps5", 1)]
COL, N_PARAMS = {}, 0
for _name, _n in PARAMS:
    COL[_name] = N_PARAMS
    N_PARAMS += _n

RESERVED = 16512
M_HEADS = 4
TAPS = 5
HEAD_PAR = 2 * (TAPS + 1) + 1
FFN_TILES = 22
FFN_PAIRS = FFN_TILES // 2
ATT_BIAS_1 = 640
HEADS = 8
HEAD_PAIRS = HEADS // 2
SGU_TILES = 4
CONV_TILES = 4
CONV_TAPS = 31
REACH = CONV_TAPS // 2
GLU_PAR = CONV_TAPS + 3
PAIR_PAR = 5
UNITS = [(side, p) for side in range(2) for p in range(TT)]


def keys_1(p):
    first = max(0, p - 4)
    return first * P, (p + 1 - first) * P, ATT_BIAS_1 - (p + 1 - first) * P


def keys_2(p):
    first, last = max(0, p - 1), min(TT - 1, p + 1)
    return first * P, (last + 1 - first) * P, (first - p + 1) * P


BIAS_3 = [(0, 512, 0), (0, 512, 512)] + [((p - 2) * P, 576, 1024) for p in range(2, 6)] \
    + [(512, 512, 1600), (512, 512, 2112)]
N_BIAS_3 = 2624


def keys_3(p):
    return BIAS_3[p]


def mixer_program(nc, x_t, blocks, n_blocks, params, consts, bias_1, bias_2, bias_3, sgu_rows, sgu_w, p_t,
                  out_t):
    with ExitStack() as ctx:
        def at(name, kib, shape, dtype=F32):
            return nc.alloc_sbuf_tensor_at(name, shape, dtype, offset=RESERVED + int(kib * 1024))

        ctx.enter_context(nc.sbuf_tensor("arena", [P, 52 * 1024 - 256], F32))

        raw = at("raw", 0, [P, 2, 1024])
        w_hi = at("w_hi", 8, [P, 2, 8, P], F32R)
        w_lo = at("w_lo", 16, [P, 2, 8, P], F32R)
        x_hi = at("x_hi", 24, [P, KT, TOK], F32R)
        x_lo = at("x_lo", 56, [P, KT, TOK], F32R)
        h = at("h", 88, [P, KT, TOK])
        par = at("par", 200, [P, N_PARAMS])
        zero = at("zero", 202, [P, 1])
        ident = at("ident", 202.125, [P, P])
        mean_w = at("mean_w", 202.625, [P, P])
        small = at("small", 203.125, [P, 64])
        square = at("square", 180, [P, 2, TOK])
        rstd = at("rstd", 188, [P, TOK])
        normed = at("normed", 192, [P, 2, TOK])
        next_sum = at("next_sum", 24, [P, TOK])
        out_rows = at("out_rows", 24, [P, KT, TOK])
        def attention_buffers(base, kib, probs_kib, bias_kib, bias_width):
            return Buffers(
                q_t=at(base + "q_t", kib, [P, TOK]), k_t=at(base + "k_t", kib + 4, [P, TOK]),
                v_tok=at(base + "v_tok", kib + 8, [P, TT, P]), v_t=at(base + "v_t", kib + 12, [P, TOK]),
                scores=at(base + "scores", kib + 12, [P, 2, 640]), probs_t=at(base + "probs_t", kib + 17, [P, 2, 5, P]),
                total=at(base + "att_sum", kib + 22, [P, TOK]), probs=at(base + "probs", probs_kib, [P, 3, 640]),
                bias=at(base + "bias", bias_kib, [P, 2, bias_width]))

        band = attention_buffers("band_", 88, 152, 190, ATT_BIAS_1)
        att_hi = at("att_hi", 120, [P, 4, TOK], F32R)
        att_lo = at("att_lo", 136, [P, 4, TOK], F32R)
        u_t = at("u_t", 88, [P, SGU_TILES, TOK])
        vs_t = at("vs_t", 152, [P, 2, TOK])
        vs_tok = at("vs_tok", 104, [P, TT, 512])
        sgu_hi = at("sgu_hi", 152, [P, SGU_TILES, TOK], F32R)
        sgu_lo = at("sgu_lo", 168, [P, SGU_TILES, TOK], F32R)
        sgu_par = at("sgu_par", 184, [P, 3, 512])
        sgu_wt = at("sgu_wt", 204, [P, 4, P])
        mixed = at("mixed", 192, [P, TOK])
        gate = at("gate", 184, [P, 2, TOK])
        part_hi = at("part_hi", 192, [P, TOK], F32R)
        part_lo = at("part_lo", 196, [P, TOK], F32R)
        act_g = at("act_g", 120, [P, TOK])
        hid = at("hid", 124, [P, TOK])
        hid_hi = at("hid_hi", 128, [P, 2, TOK], F32R)
        hid_lo = at("hid_lo", 136, [P, 2, TOK], F32R)
        gate_rows = at("gate_rows", 120, [P, TOK])
        f_rows = at("f_rows", 124, [64, TOK])
        log_f = at("log_f", 128, [64, TOK])
        m_rows = at("m_rows", 132, [64, TOK])
        b_rows = at("b_rows", 136, [64, TOK])
        c_rows = at("c_rows", 140, [64, TOK])
        carry = at("carry", 144, [64, TOK])
        soft = at("soft", 148, [64, TOK])
        c_col = at("c_col", 152.75, [P, TT, 64])
        g_diag = at("g_diag", 156.75, [64, TT, 64])
        g_all = at("g_all", 154.75, [P, TT, 64])
        r_rows = at("r_rows", 182.25, [64, TOK])
        em_col = at("em_col", 186.25, [P, TT, 2, 32])
        a_col = at("a_col", 188.25, [P, 2, TT, TT, 4])
        a_head = at("a_head", 190.25, [P, 2, TT, TT])
        em_head = at("em_head", 190.75, [P, TT, 2])
        pick = at("pick", 191, [64, 2, P])
        masks = at("masks", 192, [P, 2, P])
        head_par = at("head_par", 193, [P, HEAD_PAR])
        conv_in = at("conv_in", 166.125, [P, 2, TOK + 8])
        conv_out = at("conv_out", 128.5, [P, 2, TOK])
        v_one = at("v_one", 136.5, [P, TT, 132])
        o_gate = at("o_gate", 140.625, [P, TOK])
        vm_t = at("vm_t", 124, [P, TOK])
        r_all = at("r_all", 144.625, [P, 2, TOK])
        wts = at("wts", 152.625, [P, 3, TT + 1, P])
        h_tok = at("h_tok", 124, [P, TT, P])
        mix_t = at("mix_t", 178.1875, [P, TOK])
        mix_hi = at("mix_hi", 174.1875, [P, TOK], F32R)
        mix_lo = at("mix_lo", 120, [P, TOK], F32R)
        stats = at("stats", 194, [P, 64])
        local = attention_buffers("local_", 120, 146, 161.5, N_BIAS_3)
        att2_hi = at("att2_hi", 153.5, [P, TOK], F32R)
        att2_lo = at("att2_lo", 157.5, [P, TOK], F32R)
        p_rows = at("p_rows", 120, [P, 2, TOK])
        p_hi = at("p_hi", 176, [P, 2, TOK], F32R)
        p_lo = at("p_lo", 184, [P, 2, TOK], F32R)
        ple = at("ple", 144, [P, KT, TOK])
        ple_gate = at("ple_gate", 120, [P, 2, TOK])
        glu_par = at("glu_par", 203.375, [P, 2, GLU_PAR])
        pair_par = at("pair_par", 203.6875, [P, 6])
        group_w = at("group_w", 204, [P, P])
        u_pad = at("u_pad", 120, [P, 2, TOK + 2 * REACH])
        sigmoid = at("sigmoid", 128.5, [P, 2, TOK])
        conv_sum = at("conv_sum", 136.5, [P, CONV_TILES, TOK])
        c_lo = at("c_lo", 136.5, [P, CONV_TILES, TOK], F32R)
        c_hi = at("c_hi", 152.5, [P, CONV_TILES, TOK], F32R)
        z_conv = [at(f"z_conv{j}", kib, [P, TOK])[:, :] for j, kib in enumerate((168.5, 172.5, 192, 196))]
        y_conv = at("y_conv", 120, [P, CONV_TILES, TOK])
        square3 = at("square3", 180, [P, 3, TOK])
        z_att = at("z_att", 192, [P, TOK])

        acc_all = ctx.enter_context(nc.psum_tensor("acc", [P, 4 * TOK], F32))
        acc = [acc_all[:, s * TOK:(s + 1) * TOK] for s in range(2)]
        turned = acc_all[:, 2 * TOK:3 * TOK]
        att_out = acc_all[:, 3 * TOK:4 * TOK]

        def sem(name):
            return ctx.enter_context(nc.semaphore(name))

        raw_in = [sem("raw_in0"), sem("raw_in1")]
        hi_split, w_split, w_used = sem("hi_split"), sem("w_split"), sem("w_used")
        acc_full = [sem("acc_full0"), sem("acc_full1")]
        acc_free = [sem("acc_free0"), sem("acc_free1")]
        x_in = [sem(f"x_in{k}") for k in range(KT)]
        const_in, x_back, bias_in, sgu_in = sem("const_in"), sem("x_back"), sem("bias_in"), sem("sgu_in")
        mask_in, p_in, group_in, stored = sem("mask_in"), sem("p_in"), sem("group_in"), sem("stored")
        rows_ready, hi_ready, lo_ready = sem("rows_ready"), sem("hi_ready"), sem("lo_ready")
        squared, square_used = sem("squared"), sem("square_used")
        sum_ready, centred = sem("sum_ready"), sem("centred")
        exp_done, p_ready = sem("exp_done"), sem("p_ready")
        turned_full, turned_copied, pv_done = sem("turned_full"), sem("turned_copied"), sem("pv_done")
        zero_ready, sgu_w_ready = sem("zero_ready"), sem("sgu_w_ready")
        var_ready, std_ready, ln_ready = sem("var_ready"), sem("std_ready"), sem("ln_ready")
        rows_done, soft_ready, cols_ready = sem("rows_done"), sem("soft_ready"), sem("cols_ready")
        head_ready, pick_ready = sem("head_ready"), sem("pick_ready")
        conv_summed, conv_ready = sem("conv_summed"), sem("conv_ready")
        args_ready, w_exp = sem("args_ready"), sem("w_exp")
        num_full, num_free, h_ready = sem("num_full"), sem("num_free"), sem("h_ready")
        ple_used, conv_done = sem("ple_used"), sem("conv_done")
        v_chain, s_chain = sem("v_chain"), sem("s_chain")

        def col(name, k=0):
            return par[:, COL[name] + k:COL[name] + k + 1]

        block = ctx.enter_context(nc.Block())

        def claim(e, t):
            s = t.turn % 2
            if t.some(f"acc{s}"):
                e.wait_ge(acc_free[s], t.count(f"acc{s}"))
            return s

        def await_acc(e, t):
            s = t.turn % 2
            e.wait_ge(acc_full[s], t.next(f"acc{s}"))
            t.turn += 1
            return s

        def pass_acc(t, turns=1):
            for _ in range(turns):
                t.next(f"acc{t.turn % 2}")
                t.turn += 1

        def await_all_taken(e, t):
            for s in range(2):
                e.wait_ge(acc_free[s], t.count(f"acc{s}"))

        def take_block(pe, t):
            pe.wait_ge(w_split, t.next("block"))
            t.block += 1
            return (t.block - 1) % 2

        def take_turn(pe, t):
            t.next(f"acc{t.turn % 2}")
            t.turn += 1

        def product(pe, t, pieces, fresh, parts_from=None):
            s = claim(pe, t)
            last = len(pieces) - 1
            for n, (slot, tile, hi, lo) in enumerate(pieces):
                if parts_from is not None:
                    pe.wait_ge(lo_ready, parts_from + n + 1)
                for m, (w, part) in enumerate(((w_hi, hi), (w_hi, lo), (w_lo, hi))):
                    for half in range(2):
                        c = slice(half * HALF, (half + 1) * HALF)
                        ins = pe.matmul(acc[s][:, c], w[:, slot, tile, :], part[:, c],
                                        start=(n == 0 and m == 0), stop=(n == last and m == 2))
                        if fresh and n == 0 and m == 0 and half == 0:
                            ins.then_inc(w_used, 1)
            ins.then_inc(acc_full[s], 1)
            t.next(f"acc{s}")
            t.turn += 1

        def feature_block(pe, t, parts_from=None):
            slot = take_block(pe, t)
            product(pe, t, [(slot, k, x_hi[:, k, :], x_lo[:, k, :]) for k in range(KT)], True, parts_from)

        def skip_block(pe, t):
            slot, s = take_block(pe, t), claim(pe, t)
            pe.matmul(acc[s][:, 0:P], w_hi[:, slot, 0, :], x_hi[:, 0, 0:P], start=True, stop=True).then_inc(w_used, 1)

        def turn_tiles(pe, t, source):
            s = claim(pe, t)
            for i in range(TT):
                ins = pe.transpose(acc[s][:, i * P:(i + 1) * P], source[:, i * P:(i + 1) * P], ident[:, :])
            ins.then_inc(acc_full[s], 1)
            take_turn(pe, t)

        def row_block(pe, t, operands):
            n = len(operands)
            for _ in range(n):
                slot = take_block(pe, t)
                for j in range(KT // n):
                    product(pe, t, [(slot, j * n + k, hi, lo) for k, (hi, lo) in enumerate(operands)], j == 0)

        def sum_squares(pe, t, tiles=KT, weights=None):
            s = claim(pe, t)
            for k in range(tiles):
                pe.wait_ge(squared, t.next("squared"))
                for half in range(2):
                    c = slice(half * HALF, (half + 1) * HALF)
                    ins = pe.matmul(acc[s][:, c], mean_w[:, :], square[:, k % 2, c],
                                    start=(k == 0), stop=(k == tiles - 1))
                if k < tiles - 1:
                    ins.then_inc(square_used, 1)
            ins.then_inc(acc_full[s], 1)
            t.next(f"acc{s}")
            t.turn += 1

        def split_hi(act, t, source, hi):
            act.activation(hi, source, ACT.Copy).then_inc(hi_ready, 1)
            t.next("hi_ready")

        def split_lo(dve, t, source, hi, lo):
            dve.wait_ge(hi_ready, t.next("hi_ready"))
            dve.tensor_tensor(lo, source, hi.bitcast(F32), ALU.subtract).then_inc(lo_ready, 1)
            t.next("lo_ready")

        def mean_of_sum(pe, t):
            pe.wait_ge(sum_ready, t.next("sum_ready"))
            s = claim(pe, t)
            for half in range(2):
                c = slice(half * HALF, (half + 1) * HALF)
                ins = pe.matmul(acc[s][:, c], mean_w[:, :], rstd[:, c], start=True, stop=True)
            ins.then_inc(acc_full[s], 1)
            take_turn(pe, t)

        def norm_tensor(pe, t, centre=False):
            mean_of_sum(pe, t)
            if centre:
                sum_squares(pe, t)
            else:
                for _ in range(KT):
                    t.next("squared")

        def inverse_root(act, ch, out, source, eps, scale=1.0):
            ch.link(act.activation(out, source, ACT.Ln, bias=col(eps), scale=scale))
            ch.sync()
            return act.activation(out, out, ACT.Exp, scale=-0.5)

        def squares(act, t, k, source):
            if k >= 2:
                act.wait_ge(square_used, t.next("square_used"))
            act.activation(square[:, k % 2, :], source, ACT.Square).then_inc(squared, 1)

        def square_to_sum(act, t, k):
            if k == 2 or k >= 4:
                t.next("square_used")
            if k >= 2:
                act.wait_ge(square_used, t.count("square_used"))
            act.activation(square[:, k % 2, :], h[:, k, :], ACT.Square).then_inc(squared, 1)
            if k == KT - 1:
                t.next("square_used")

        def norm_scalar(act, t, ch, mode, centre=False, rows=False, eps="eps6", beta=None,
                        summed=False):
            if centre:
                pass_acc(t, KT + 1 if rows else 1)
                for k in range(KT):
                    if k < KT - 1:
                        act.wait_ge(centred, t.next("centred"))
                    else:
                        act.wait_ge(acc_free[(t.turn - 1) % 2], t.count(f"acc{(t.turn - 1) % 2}"))
                    squares(act, t, k, h[:, k, :])
                t.next("square_used")
            elif not summed:
                if not rows and t.some("acc0"):
                    await_all_taken(act, t)
                    act.wait_ge(hi_ready, t.count("hi_ready"))
                first = not rows and not t.some("acc0")
                for k in range(KT):
                    if first:
                        act.wait_ge(x_in[k], 16)
                    if rows:
                        s = t.turn % 2
                        pass_acc(t)
                        act.wait_ge(acc_free[s], t.count(f"acc{s}"))
                    square_to_sum(act, t, k)
            s = await_acc(act, t)
            inverse_root(act, ch, rstd[:, :], acc[s], eps).then_inc(acc_free[s], 1)
            for k in range(KT):
                row = normed[:, k % 2, :]
                act.wait_ge(rows_ready, t.next("rows_ready"))
                if mode == "out":
                    act.dma_start(out_t[k * P:(k + 1) * P, :], out_rows[:, k, :]).then_inc(stored, 16)
                    continue
                if mode == "hold":
                    act.activation(h[:, k, :], row, ACT.Identity, bias=col(beta, k)).then_inc(hi_ready, 1)
                    act.wait_ge(hi_ready, t.next("hi_ready"))
                    square_to_sum(act, t, k)
                    continue
                if beta is not None:
                    ch.link(act.activation(row, row, ACT.Identity, bias=col(beta, k)))
                    ch.sync()
                if mode == "keep":
                    ch.link(act.activation(h[:, k, :], row, ACT.Copy, scale=ALPHA))
                split_hi(act, t, row, x_hi[:, k, :])
                t.next("lo_ready")
            if mode in ("split", "keep"):
                act.wait_ge(lo_ready, t.count("lo_ready"))

        def sum_tiles(dve, t, ch, centre, rows):
            for k in range(KT + 1):
                if rows and k < KT:
                    s = await_acc(dve, t)
                    dve.tensor_tensor(h[:, k, :], h[:, k, :], acc[s], ALU.add).then_inc(acc_free[s], 1)
                j = k - 1
                if j < 0:
                    continue
                if not centre:
                    dve.wait_ge(squared, t.next("squared"))
                if j == 0:
                    continue
                if centre and rows:
                    done = t.turn - 1 if k == KT else t.turn - 2
                    dve.wait_ge(acc_free[done % 2], t.count(f"acc{done % 2}"))
                if j > 1:
                    ch.sync()
                    if not centre:
                        dve.wait_ge(square_used, t.count("square_used"))
                new = h[:, j, :] if centre else square[:, j % 2, :]
                old = rstd[:, :] if j > 1 else h[:, 0, :] if centre else square[:, 0, :]
                ins = dve.tensor_tensor(rstd[:, :], old, new, ALU.add)
                if j == KT - 1:
                    ins.then_inc(sum_ready, 1)
                elif centre:
                    ch.link(ins)
                else:
                    ins.then_inc(square_used, 1)
                    t.next("square_used")

        def sum_next_square(dve, t, j):
            dve.wait_ge(squared, t.next("squared"))
            if j == 0:
                return
            if j > 1:
                dve.wait_ge(square_used, t.count("square_used"))
            old = next_sum[:, :] if j > 1 else square[:, 0, :]
            if j == KT - 1:
                dve.tensor_tensor(rstd[:, :], old, square[:, j % 2, :], ALU.add).then_inc(sum_ready, 1)
            else:
                dve.tensor_tensor(next_sum[:, :], old, square[:, j % 2, :], ALU.add).then_inc(square_used, 1)
                t.next("square_used")

        def norm_vector(dve, t, ch, mode, gain, centre=False, rows=False, summed=False):
            if not summed:
                sum_tiles(dve, t, ch, centre, rows)
            if centre:
                s = await_acc(dve, t)
                for k in range(KT):
                    t.next("squared")
                    if k < KT - 1:
                        t.next("square_used")
                    ins = dve.tensor_tensor(h[:, k, :], h[:, k, :], acc[s], ALU.subtract)
                    ins.then_inc(centred if k < KT - 1 else acc_free[s], 1)
            s = t.turn % 2
            pass_acc(t)
            dve.wait_ge(acc_free[s], t.count(f"acc{s}"))
            for k in range(KT + 1):
                if k < KT:
                    if k >= 2 and mode == "hold":
                        dve.wait_ge(hi_ready, t.next("hi_ready"))
                    if k >= 2 and mode in ("split", "keep"):
                        dve.wait_ge(lo_ready, t.count("lo_ready"))
                    row = out_rows[:, k, :] if mode == "out" else normed[:, k % 2, :]
                    dve.scalar_tensor_tensor(out=row, in0=h[:, k, :], scalar=col(gain, k), in1=rstd[:, :],
                                             op0=ALU.mult, op1=ALU.mult).then_inc(rows_ready, 1)
                if k >= 1 and mode == "hold":
                    sum_next_square(dve, t, k - 1)
                if k >= 1 and mode in ("split", "keep"):
                    split_lo(dve, t, normed[:, (k - 1) % 2, :], x_hi[:, k - 1, :], x_lo[:, k - 1, :])
            if mode == "hold":
                t.next("hi_ready")
                dve.wait_ge(hi_ready, t.next("hi_ready"))

        def expect_parts(t, n):
            before = t.base.get("lo_ready", 0)
            for _ in range(n):
                t.next("hi_ready")
                t.next("lo_ready")
            return before

        def await_parts(pe, t, n):
            for _ in range(n):
                t.next("hi_ready")
                t.next("lo_ready")
            pe.wait_ge(lo_ready, t.count("lo_ready"))

        def att_tensor(pe, t, a, keys, next_block=True):
            def score(n):
                side, p = UNITS[n]
                rows = slice(64 * side, 64 * side + 64)
                first, count, _ = keys(p)
                s = claim(pe, t)
                for c0 in range(0, count, 512):
                    c1 = min(count, c0 + 512)
                    ins = pe.matmul(acc[s][:, c0:c1], a.q_t[rows, p * P:(p + 1) * P],
                                    a.k_t[rows, first + c0:first + c1], start=True, stop=True)
                ins.then_inc(acc_full[s], 1)
                t.next(f"acc{s}")
                t.turn += 1

            def turn_probs(n):
                side, p = UNITS[n]
                count = keys(p)[1]
                pe.wait_ge(p_ready, t.next("p_ready"))
                for c in range(-(-count // P)):
                    w = min(P, count - c * P)
                    ins = pe.transpose(turned[0:w, c * P:(c + 1) * P], a.probs[:, n % 3, c * P:c * P + w], ident[:, :])
                ins.then_inc(turned_full, 1)

            def weigh_values(n):
                side, p = UNITS[n]
                first, count, _ = keys(p)
                cols = slice(64 * side, 64 * side + 64)
                tiles = -(-count // P)
                for c in range(tiles):
                    w = min(P, count - c * P)
                    ins = pe.matmul(att_out[cols, p * P:(p + 1) * P], a.v_tok[0:w, first // P + c, cols],
                                    a.probs_t[0:w, n % 2, c, :], start=(c == 0), stop=(c == tiles - 1))
                ins.then_inc(pv_done, 1)

            for n in range(len(UNITS) + 3):
                if n < len(UNITS):
                    score(n)
                if n == len(UNITS) and next_block:
                    feature_block(pe, t)
                if n >= 3:
                    pe.wait_ge(turned_copied, t.next("turned_copied"))
                if 2 <= n <= len(UNITS) + 1:
                    turn_probs(n - 2)
                if n >= 3:
                    weigh_values(n - 3)

        def att_vector(dve, t, ch, a, keys, sink=None):
            for n in range(len(UNITS) + 1):
                if n < len(UNITS):
                    side, p = UNITS[n]
                    _, count, bias_at = keys(p)
                    s = await_acc(dve, t)
                    seed = small[:, 60 + n % 2:61 + n % 2] if sink is None else sink(side)
                    if sink is None:
                        ch.link(dve.memset(seed, 3e38))
                        ch.sync()
                    dve.tensor_tensor_reduce(
                        out=a.scores[:, n % 2, 0:count], in0=acc[s][:, 0:count],
                        in1=a.bias[:, side, bias_at:bias_at + count], scale=-1.0,
                        scalar=seed, op0=ALU.add, op1=ALU.min,
                        accum_out=small[:, n % 2:n % 2 + 1]).then_inc(acc_free[s], 1)
                if n >= 1:
                    b = (n - 1) % 2
                    count = keys(UNITS[n - 1][1])[1]
                    dve.wait_ge(exp_done, t.next("exp_done"))
                    total = small[:, 2 + b:3 + b]
                    if sink is not None:
                        ch.link(dve.tensor_tensor(total, total, small[:, 6 + b:7 + b], ALU.add))
                        ch.sync()
                    ch.link(dve.reciprocal(small[:, 4 + b:5 + b], total))
                    ch.sync()
                    probs = a.probs[:, (n - 1) % 3, 0:count]
                    dve.tensor_scalar(probs, probs, small[:, 4 + b:5 + b], None,
                                      ALU.mult).then_inc(p_ready, 1)

        def att_scalar(act, t, ch, a, keys, sink=None):
            for n in range(len(UNITS) + 2):
                if n < len(UNITS):
                    side, p = UNITS[n]
                    count = keys(p)[1]
                    s = t.turn % 2
                    pass_acc(t)
                    act.wait_ge(acc_free[s], t.count(f"acc{s}"))
                    if sink is not None:
                        ch.link(act.activation(small[:, 6 + n % 2:7 + n % 2], small[:, n % 2:n % 2 + 1], ACT.Exp,
                                               bias=sink(side)))
                    act.activation(a.probs[:, n % 3, 0:count], a.scores[:, n % 2, 0:count], ACT.Exp, scale=-1.0,
                                   bias=small[:, n % 2:n % 2 + 1],
                                   accum_out=small[:, 2 + n % 2:3 + n % 2]).then_inc(exp_done, 1)
                if n >= 2:
                    count = keys(UNITS[n - 2][1])[1]
                    act.wait_ge(turned_full, t.next("turned_full"))
                    if n >= 4:
                        act.wait_ge(pv_done, t.next("pv_done"))
                    t_full, w = count // P, count % P
                    ins = act.activation(a.probs_t[:, n % 2, 0:t_full, :],
                                         turned[:, 0:t_full * P].rearrange("p (c q) -> p c q", q=P), ACT.Copy)
                    if w:
                        ins = act.activation(a.probs_t[0:w, n % 2, t_full, :],
                                             turned[0:w, t_full * P:(t_full + 1) * P], ACT.Copy)
                    ins.then_inc(turned_copied, 1)
            t.next("pv_done")
            act.wait_ge(pv_done, t.next("pv_done"))

        def add_rows(dve, t, ch):
            for j in range(KT):
                s = await_acc(dve, t)
                dve.tensor_tensor(h[:, j, :], h[:, j, :], acc[s], ALU.add).then_inc(acc_free[s], 1)

        def projections_tensor(pe, t):
            feature_block(pe, t)
            turn_tiles(pe, t, band.v_t)
            feature_block(pe, t)
            await_all_taken(pe, t)

        def qkv_scalar(act, t, a):
            for dst, scale in ((a.v_t[:, :], 1.0), (a.q_t[:, :], 0.125),
                               (a.v_tok[:, :, :].rearrange("p a b -> p (a b)"), 1.0), (a.k_t[:, :], 1.0)):
                s = await_acc(act, t)
                act.activation(dst, acc[s], ACT.Copy, scale=scale).then_inc(acc_free[s], 1)


        def att1_tensor(pe, t):
            feature_block(pe, t, parts_from=expect_parts(t, KT))
            with t.loop(2, acc0=20, acc1=20, block=6, p_ready=32, turned_copied=32, hi_ready=2, lo_ready=2):
                for _ in range(2):
                    projections_tensor(pe, t)
                    att_tensor(pe, t, band, keys_1)
                    t.next("hi_ready")
                    t.next("lo_ready")

        def att1_scalar(act, t, ch):
            ch.reset()
            with t.loop(2, acc0=20, acc1=20, turned_full=32, pv_done=32, hi_ready=2, lo_ready=2) as i:
                for q in range(2):
                    act.dma_start(band.bias[:, :, :], bias_1[bass.ds(2 * i + q, 1)].rearrange("a p s k -> p (a s) k"))\
                        .then_inc(bias_in, 16)
                    qkv_scalar(act, t, band)
                    att_scalar(act, t, ch, band, keys_1)
                    act.wait_ge(lo_ready, t.count("lo_ready"))
                    ch.link(act.activation(band.total[:, :], att_out, ACT.Copy))
                    ch.sync()
                    split_hi(act, t, band.total[:, :],
                             att_hi[:, bass.ds(2 * i + q, 1), :].rearrange("p a n -> p (a n)"))
                    t.next("lo_ready")
                ch.reset()

        def att1_vector(dve, t, ch):
            ch.reset()
            with t.loop(2, acc0=20, acc1=20, exp_done=32, bias_in=2, hi_ready=2, lo_ready=2) as i:
                for q in range(2):
                    pass_acc(t, 4)
                    dve.wait_ge(bias_in, t.next("bias_in") * 16)
                    att_vector(dve, t, ch, band, keys_1)
                    where = bass.ds(2 * i + q, 1)
                    split_lo(dve, t, band.total[:, :], att_hi[:, where, :].rearrange("p a n -> p (a n)"),
                             att_lo[:, where, :].rearrange("p a n -> p (a n)"))
                ch.reset()

        def sgu_tensor(pe, t):
            for pair in range(2):
                if pair:
                    feature_block(pe, t)
                feature_block(pe, t)
                turn_tiles(pe, t, vs_t[:, 0, :])
                turn_tiles(pe, t, vs_t[:, 1, :])
            with t.loop(2, acc0=1, acc1=1, block=2):
                feature_block(pe, t)
                feature_block(pe, t)
            pe.wait_ge(sgu_w_ready, 1)
            pe.wait_ge(ln_ready, TT)
            for g in range(SGU_TILES):
                s = claim(pe, t)
                for n in range(TT):
                    ins = pe.matmul(acc[s][:, n * P:(n + 1) * P], vs_tok[:, n, g * P:(g + 1) * P], sgu_wt[:, g, :],
                                    start=True, stop=True)
                ins.then_inc(acc_full[s], 1)
                t.next(f"acc{s}")
                t.turn += 1
            await_parts(pe, t, SGU_TILES)

        def sgu_scalar(act, t, ch):
            act.wait_ge(lo_ready, t.count("lo_ready"))
            act.dma_start(sgu_par[:, :, :], sgu_rows.rearrange("r n -> (r n)").partition_broadcast(P)).then_inc(sgu_in, 16)
            for pair in range(2):
                for q in range(2):
                    s = await_acc(act, t)
                    act.activation(vs_t[:, q, :], acc[s], ACT.Gelu_apprx_tanh).then_inc(acc_free[s], 1)
                for j in (2 * pair, 2 * pair + 1):
                    s = await_acc(act, t)
                    act.activation(vs_tok[:, :, j * P:(j + 1) * P], acc[s].rearrange("p (a b) -> p a b", b=P), ACT.Copy)\
                       .then_inc(acc_free[s], 1)
            act.wait_ge(var_ready, TT)
            act.activation(small[:, 24:32], small[:, 32:48].rearrange("p (n two) -> p n two", two=2)[:, :, 1],
                           ACT.Sqrt, bias=col("eps6")).then_inc(std_ready, 1)
            for j in range(SGU_TILES):
                s = await_acc(act, t)
                act.activation(u_t[:, j, :], acc[s], ACT.Gelu_apprx_tanh).then_inc(acc_free[s], 1)
            for g in range(SGU_TILES):
                pass_acc(t)
                act.wait_ge(rows_ready, t.next("rows_ready"))
                split_hi(act, t, mixed[:, :], sgu_hi[:, g, :])
                t.next("lo_ready")
            act.wait_ge(lo_ready, t.count("lo_ready"))
            act.dma_start(h[:, :, :], x_t.rearrange("(k p) n -> p k n", p=P)).then_inc(x_back, 16)

        def sgu_vector(dve, t, ch):
            pass_acc(t, 8)
            for s in range(2):
                dve.wait_ge(acc_free[s], t.count(f"acc{s}"))
            for n in range(TT):
                ch.link(dve.bn_stats(small[:, 48:54], vs_tok[:, n, :]))
                ch.sync()
                ins = dve.bn_aggr(small[:, 32 + 2 * n:34 + 2 * n], small[:, 48:54])
                ins.then_inc(var_ready, 1)
                dve.wait_ge(var_ready, n + 1)
            dve.wait_ge(std_ready, 1)
            ch.link(dve.reciprocal(small[:, 24:32], small[:, 24:32]))
            dve.wait_ge(sgu_in, 32)
            for n in range(TT):
                ch.sync()
                row = vs_tok[:, n, :]
                ch.link(dve.tensor_scalar(row, row, small[:, 32 + 2 * n:33 + 2 * n], small[:, 24 + n:25 + n],
                                          ALU.subtract, ALU.mult))
                ch.sync()
                ch.link(dve.tensor_tensor(row, row, sgu_par[:, 0, :], ALU.mult))
                ch.sync()
                dve.tensor_tensor(row, row, sgu_par[:, 1, :], ALU.add).then_inc(ln_ready, 1)
            pass_acc(t, SGU_TILES)
            for g in range(SGU_TILES):
                s = await_acc(dve, t)
                if g:
                    dve.wait_ge(lo_ready, t.count("lo_ready"))
                b_row = sgu_par[:, 2, g * P:(g + 1) * P].unsqueeze(1).to_broadcast([P, TT, P])
                ins = dve.tensor_tensor(mixed[:, :].rearrange("p (n q) -> p n q", q=P),
                                        acc[s].rearrange("p (n q) -> p n q", q=P), b_row, ALU.add)
                ins.then_inc(acc_free[s], 1)
                dve.wait_ge(acc_free[s], t.count(f"acc{s}"))
                dve.tensor_tensor(mixed[:, :], mixed[:, :], u_t[:, g, :], ALU.mult).then_inc(rows_ready, 1)
                split_lo(dve, t, mixed[:, :], sgu_hi[:, g, :], sgu_lo[:, g, :])

        def merge_gates_tensor(pe, t):
            feature_block(pe, t)
            feature_block(pe, t)

        def merge_branches_tensor(pe, t):
            slot = take_block(pe, t)
            product(pe, t, [(slot, k, att_hi[:, k, :], att_lo[:, k, :]) for k in range(4)], True)
            product(pe, t, [(slot, 4 + k, sgu_hi[:, k, :], sgu_lo[:, k, :]) for k in range(4)], False)

        def merge_rows_tensor(pe, t):
            await_parts(pe, t, 1)
            row_block(pe, t, [(part_hi[:, :], part_lo[:, :])])

        def merge_tensor(pe, t):
            merge_gates_tensor(pe, t)
            merge_branches_tensor(pe, t)
            with t.loop(KT - 1, acc0=6, acc1=6, block=4, hi_ready=1, lo_ready=1):
                merge_gates_tensor(pe, t)
                merge_rows_tensor(pe, t)
                merge_branches_tensor(pe, t)
            merge_rows_tensor(pe, t)

        def merge_gates_scalar(act, t, ch, n):
            for branch in range(2):
                ch.link(act.activation(small[:, 56 + branch:57 + branch],
                                       par[:, bass.ds(n + COL["b_gate"] + 8 * branch, 1)], ACT.Copy))
            ch.reset()
            act.wait_ge(lo_ready, t.count("lo_ready"))
            for branch in range(2):
                s = await_acc(act, t)
                act.activation(gate[:, branch, :], acc[s], ACT.Sigmoid, bias=small[:, 56 + branch:57 + branch])\
                   .then_inc(acc_free[s], 1)

        def merge_branches_scalar(act, t):
            pass_acc(t, 2)
            act.wait_ge(rows_ready, t.next("rows_ready"))
            split_hi(act, t, gate[:, 0, :], part_hi[:, :])
            t.next("lo_ready")

        def merge_scalar(act, t, ch):
            merge_gates_scalar(act, t, ch, 0)
            merge_branches_scalar(act, t)
            ch.reset()
            with t.loop(KT - 1, acc0=6, acc1=6, rows_ready=1, hi_ready=1, lo_ready=1) as i:
                merge_gates_scalar(act, t, ch, i + 1)
                pass_acc(t, KT)
                merge_branches_scalar(act, t)

        def merge_branches_vector(dve, t, ch):
            for branch in range(2):
                s = await_acc(dve, t)
                dve.tensor_tensor(gate[:, branch, :], gate[:, branch, :], acc[s], ALU.mult).then_inc(acc_free[s], 1)
            for s in range(2):
                dve.wait_ge(acc_free[s], t.count(f"acc{s}"))
            dve.tensor_tensor(gate[:, 0, :], gate[:, 0, :], gate[:, 1, :], ALU.add).then_inc(rows_ready, 1)
            split_lo(dve, t, gate[:, 0, :], part_hi[:, :], part_lo[:, :])

        def merge_vector(dve, t, ch):
            pass_acc(t, 2)
            merge_branches_vector(dve, t, ch)
            dve.wait_ge(x_back, 16)
            with t.loop(KT - 1, acc0=6, acc1=6, hi_ready=1, lo_ready=1):
                pass_acc(t, 2)
                add_rows(dve, t, ch)
                merge_branches_vector(dve, t, ch)

        def ffn_tensor(pe, t):
            before = expect_parts(t, KT)
            for j in range(4):
                feature_block(pe, t, parts_from=before if j == 0 else None)
            with t.loop(FFN_PAIRS - 1, acc0=6, acc1=6, block=6, hi_ready=2, lo_ready=2):
                feature_block(pe, t)
                await_parts(pe, t, 2)
                row_block(pe, t, [(hid_hi[:, k, :], hid_lo[:, k, :]) for k in range(2)])
                for _ in range(3):
                    feature_block(pe, t)
            await_parts(pe, t, 2)
            row_block(pe, t, [(hid_hi[:, k, :], hid_lo[:, k, :]) for k in range(2)])

        def hidden_scalar(act, t, rows):
            for k in range(2):
                s = await_acc(act, t)
                if t.some("lo_ready"):
                    act.wait_ge(lo_ready, t.count("lo_ready"))
                act.activation(act_g[:, :], acc[s], ACT.Silu).then_inc(acc_free[s], 1)
                if k == 0 and rows:
                    pass_acc(t, KT)
                s = t.turn % 2
                pass_acc(t)
                act.wait_ge(acc_free[s], t.count(f"acc{s}"))
                split_hi(act, t, hid[:, :], hid_hi[:, k, :])
                t.next("lo_ready")

        def ffn_scalar(act, t, ch):
            hidden_scalar(act, t, False)
            with t.loop(FFN_PAIRS - 1, acc0=6, acc1=6, hi_ready=2, lo_ready=2):
                hidden_scalar(act, t, True)

        def hidden_vector(dve, t, ch, rows):
            for k in range(2):
                g = t.turn % 2
                pass_acc(t)
                gates = t.count(f"acc{g}")
                if k == 0 and rows:
                    add_rows(dve, t, ch)
                dve.wait_ge(acc_free[g], gates)
                s = await_acc(dve, t)
                dve.wait_ge(lo_ready, t.count("lo_ready"))
                dve.tensor_tensor(hid[:, :], act_g[:, :], acc[s], ALU.mult).then_inc(acc_free[s], 1)
                dve.wait_ge(acc_free[s], t.count(f"acc{s}"))
                split_lo(dve, t, hid[:, :], hid_hi[:, k, :], hid_lo[:, k, :])

        def ffn_vector(dve, t, ch):
            hidden_vector(dve, t, ch, False)
            with t.loop(FFN_PAIRS - 1, acc0=6, acc1=6, hi_ready=2, lo_ready=2):
                hidden_vector(dve, t, ch, True)

        def gates_tensor(pe, t):
            feature_block(pe, t, parts_from=expect_parts(t, KT))
            feature_block(pe, t)
            feature_block(pe, t)
            pe.wait_ge(rows_done, 3)
            s = claim(pe, t)
            for half, rows in enumerate((c_rows, m_rows)):
                for n in range(TT):
                    ins = pe.transpose(acc[s][:, half * HALF + n * 64:half * HALF + (n + 1) * 64],
                                       rows[:, n * P:(n + 1) * P], ident[0:64, 0:64])
            ins.then_inc(acc_full[s], 1)
            t.next(f"acc{s}")
            t.turn += 1
            pe.wait_ge(rows_done, 4)
            s = claim(pe, t)
            pe.matmul(acc[s][:, 0:HALF], mean_w[0:64, :], g_diag[:, :, :].rearrange("p a b -> p (a b)"),
                      start=True, stop=True).then_inc(acc_full[s], 1)
            t.next(f"acc{s}")
            t.turn += 1

        def conv_inputs(act, t):
            for part in range(2):
                s = await_acc(act, t)
                act.activation(conv_in[:, part, 4:TOK + 4], acc[s], ACT.Copy).then_inc(acc_free[s], 1)

        def gates_scalar(act, t, ch):
            act.dma_start(masks[:, :, :], consts[:, 2 * P:4 * P].rearrange("p (a b) -> p a b", b=P)).then_inc(mask_in, 16)
            s = await_acc(act, t)
            act.activation(gate_rows[:, :], acc[s], ACT.Identity, bias=col("gate_b")).then_inc(acc_free[s], 1)
            act.wait_ge(rows_done, 1)
            ch.link(act.activation(soft[:, :], soft[:, :], ACT.Exp, scale=-1.0))
            ch.sync()
            act.activation(soft[:, :], soft[:, :], ACT.Ln, bias=1.0).then_inc(soft_ready, 1)
            t.next("soft_ready")
            conv_inputs(act, t)
            s = await_acc(act, t)
            ch.link(act.activation(c_col[:, :, :].rearrange("p a b -> p (a b)"), acc[s][:, 0:HALF], ACT.Copy))
            act.activation(em_col[:, :, :, :].rearrange("p a b c -> p (a b c)"), acc[s][:, HALF:TOK], ACT.Exp)\
               .then_inc(acc_free[s], 1)
            s = await_acc(act, t)
            act.activation(g_all[:, :, :].rearrange("p a b -> p (a b)"), acc[s][:, 0:HALF], ACT.Copy,
                           scale=float(D)).then_inc(acc_free[s], 1)
            ch.sync()

        def gates_vector(dve, t, ch):
            s = t.turn % 2
            pass_acc(t)
            dve.wait_ge(acc_free[s], t.count(f"acc{s}"))
            ch.link(dve.tensor_copy(f_rows[:, :], gate_rows[64:128, :]))
            ch.link(dve.memset(carry[:, :], 1.0))
            ch.link(dve.memset(a_col[:, :, :, :, :], 0.0))
            ch.sync()
            ch.link(dve.tensor_scalar(log_f[:, :], f_rows[:, :], -1.0, None, ALU.mult))
            ch.sync()
            dve.tensor_tensor(soft[:, :], f_rows[:, :], log_f[:, :], ALU.max).then_inc(rows_done, 1)
            ch.link(dve.memset(carry[0:32, 0:TOK:P], 0.0))
            ch.link(dve.memset(carry[32:64, P - 1:TOK:P], 0.0))
            dve.wait_ge(soft_ready, t.next("soft_ready"))
            ch.link(dve.scalar_tensor_tensor(out=log_f[:, :], in0=f_rows[:, :], scalar=0.0, in1=soft[:, :],
                                             op0=ALU.min, op1=ALU.subtract))
            ch.sync()
            forward, backward = (slice(0, 32), slice(None)), (slice(32, 64), slice(None, None, -1))
            for at_ in (forward, backward):
                ch.link(dve.tensor_tensor_scan(m_rows[at_], log_f[at_], gate_rows[at_], 0.0, ALU.add, ALU.max))
                ch.link(dve.tensor_tensor_scan(b_rows[at_], carry[at_], log_f[at_], 0.0, ALU.mult, ALU.add))
            ch.sync()
            ch.link(dve.tensor_tensor(r_rows[:, :], b_rows[:, :], m_rows[:, :], ALU.subtract))
            ch.sync()
            dve.tensor_tensor(c_rows[:, :], gate_rows[0:64, :], b_rows[:, :], ALU.subtract).then_inc(rows_done, 1)
            dve.tensor_scalar(m_rows[:, :], m_rows[:, :], -1.0, None, ALU.mult).then_inc(rows_done, 1)
            for n in range(TT):
                for rows, end in ((slice(0, 32), n * P + P - 1), (slice(32, 64), n * P)):
                    ins = dve.tensor_scalar(g_diag[rows, n, :], ident[rows, 0:64], b_rows[rows, end:end + 1], None,
                                            ALU.mult)
                    if n == TT - 1 and end == n * P:
                        ins.then_inc(rows_done, 1)
                    else:
                        ch.link(ins)
            pass_acc(t, 2)
            for _ in range(2):
                s = t.turn % 2
                pass_acc(t)
                dve.wait_ge(acc_free[s], t.count(f"acc{s}"))
            for n in range(TT):
                back = TT - 1 - n
                if n:
                    g = g_all[:, n - 1, 0:4].unsqueeze(1).to_broadcast([P, n, 4])
                    ch.link(dve.tensor_tensor(a_col[:, 0, n, 0:n, :], a_col[:, 0, n - 1, 0:n, :], g, ALU.add))
                    g = g_all[:, back + 1, 32:36].unsqueeze(1).to_broadcast([P, n, 4])
                    ch.link(dve.tensor_tensor(a_col[:, 1, back, back + 1:TT, :], a_col[:, 1, back + 1, back + 1:TT, :],
                                              g, ALU.add))
                ch.link(dve.tensor_copy(a_col[:, 0, n, n, :], c_col[:, n, 0:4]))
                ch.link(dve.tensor_copy(a_col[:, 1, back, back, :], c_col[:, back, 32:36]))
                ch.sync()
            ch.link(dve.memset(conv_in[:, :, 0:4], 0.0))
            ch.link(dve.memset(conv_in[:, :, TOK + 4:TOK + 8], 0.0))
            ch.link(dve.memset(v_one[:, :, P:P + 1], 1.0))
            dve.wait_ge(mask_in, 16)
            ch.reset()

        NUM = [turned, att_out]

        def head_tensor(pe, t, rows):
            if rows:
                feature_block(pe, t)
                feature_block(pe, t)
                await_parts(pe, t, 1)
                row_block(pe, t, [(mix_hi[:, :], mix_lo[:, :])])
            feature_block(pe, t)
            feature_block(pe, t)
            s = t.turn % 2
            pe.wait_ge(acc_free[s], t.count(f"acc{s}"))
            if t.some("num"):
                pe.wait_ge(num_free, t.count("num"))
            for i in range(TT):
                ins = pe.transpose(NUM[0][:, i * P:(i + 1) * P], vm_t[:, i * P:(i + 1) * P], ident[:, :])
            ins.then_inc(num_full, 1)
            t.next("num")
            if rows:
                skip_block(pe, t)
            pe.wait_ge(pick_ready, t.next("pick_ready"))
            for way in range(2):
                s = claim(pe, t)
                for half in range(2):
                    c = slice(half * HALF, (half + 1) * HALF)
                    ins = pe.matmul(acc[s][:, c], pick[:, way, :], r_rows[:, c], start=True, stop=True)
                ins.then_inc(acc_full[s], 1)
                t.next(f"acc{s}")
                t.turn += 1
            for _ in range(2):
                pe.wait_ge(conv_ready, t.next("conv_ready"))

            def score(i):
                s = claim(pe, t)
                for j in range(TT):
                    ins = pe.matmul(acc[s][:, j * P:(j + 1) * P], conv_out[:, 1, j * P:(j + 1) * P],
                                    conv_out[:, 0, i * P:(i + 1) * P], start=True, stop=True)
                ins.then_inc(acc_full[s], 1)
                t.next(f"acc{s}")
                t.turn += 1

            def weigh(i):
                s = (t.turn - (2 if i < TT - 1 else 1)) % 2
                pe.wait_ge(acc_free[s], t.count(f"acc{s}"))
                made = t.count("num")
                if t.some("num") and (i == 0 or t.base["num"] >= 2):
                    pe.wait_ge(num_free, made if i == 0 else made - 1)
                for way, tiles in enumerate((range(i + 1), range(i, TT))):
                    out = NUM[i % 2][:, way * HALF:way * HALF + P + 1]
                    for j in tiles:
                        ins = pe.matmul(out, wts[:, i % 3, j + way, :], v_one[:, j, 0:P + 1],
                                        start=(j == tiles[0]), stop=(j == tiles[-1]))
                ins.then_inc(num_full, 1)
                t.next("num")

            score(0)
            for i in range(TT):
                if i < TT - 1:
                    score(i + 1)
                weigh(i)
            pe.wait_ge(h_ready, t.next("h_ready"))
            for i in range(TT):
                ins = pe.transpose(NUM[0][:, i * P:(i + 1) * P], h_tok[:, i, :], ident[:, :])
            ins.then_inc(num_full, 1)
            t.next("num")

        def head_scalar(act, t, ch, rows):
            act.wait_ge(head_ready, t.next("head_ready"))
            if rows:
                conv_inputs(act, t)

            def conv_silu(part):
                act.wait_ge(conv_summed, t.next("conv_summed"))
                act.activation(conv_out[:, part, :], conv_out[:, part, :], ACT.Silu,
                               bias=head_par[:, TAPS + part * (TAPS + 1):TAPS + 1 + part * (TAPS + 1)])\
                   .then_inc(conv_ready, 1)

            conv_silu(0)
            if rows:
                pass_acc(t, KT)
            s = await_acc(act, t)
            act.activation(vm_t[:, :], acc[s], ACT.Copy).then_inc(acc_free[s], 1)
            conv_silu(1)
            s = await_acc(act, t)
            act.activation(o_gate[:, :], acc[s], ACT.Sigmoid).then_inc(acc_free[s], 1)
            act.wait_ge(num_full, t.next("num"))
            act.activation(v_one[:, :, 0:P], NUM[0].rearrange("p (a b) -> p a b", b=P), ACT.Copy).then_inc(num_free, 1)
            for way in range(2):
                s = await_acc(act, t)
                act.activation(r_all[:, way, :], acc[s], ACT.Copy).then_inc(acc_free[s], 1)
            for i in range(TT):
                pass_acc(t)
                act.wait_ge(args_ready, t.next("args_ready"))
                diagonal = wts[:, i % 3, i:i + 2, :]
                ins = act.activation(diagonal, diagonal, ACT.Exp)
                for way, tiles in enumerate((range(i), range(i + 1, TT))):
                    for j in tiles:
                        ins = act.activation(wts[:, i % 3, j + way, :], r_all[:, way, i * P:(i + 1) * P], ACT.Exp,
                                             bias=a_head[:, way, i, j:j + 1])
                ins.then_inc(w_exp, 1)
                t.next("num")
            act.wait_ge(cols_ready, t.next("cols_ready"))
            act.activation(stats[:, 32:40], stats[:, 16:32].rearrange("p (n two) -> p n two", two=2)[:, :, 1], ACT.Sqrt,
                           bias=col("eps6")).then_inc(soft_ready, 1)
            t.next("soft_ready")
            if t.some("lo_ready"):
                act.wait_ge(lo_ready, t.count("lo_ready"))
            act.wait_ge(num_free, t.next("num"))
            split_hi(act, t, mix_t[:, :], mix_hi[:, :])
            t.next("lo_ready")

        def head_vector(dve, t, ch, head, rows):
            ch.link(dve.tensor_copy(a_head[:, :, :, :].rearrange("p a b c -> p (a b c)"),
                                    a_col[:, :, :, :, :].rearrange("p a b c d -> p (a b c) d")[:, :, bass.ds(head, 1)]
                                    .rearrange("p a b -> p (a b)")))
            ch.link(dve.tensor_copy(em_head[:, :, :].rearrange("p a b -> p (a b)"),
                                    em_col[:, :, :, :].rearrange("p a b c -> p (a b) c")[:, :, bass.ds(head, 1)]
                                    .rearrange("p a b -> p (a b)")))
            dve.tensor_copy(head_par[:, :], par[:, bass.ds(COL["heads"] + head * HEAD_PAR, HEAD_PAR)])\
               .then_inc(head_ready, 1)
            t.next("head_ready")
            for way in range(2):
                ins = dve.tensor_copy(pick[:, way, :], ident[0:64, bass.ds(32 * way + head, 1)].to_broadcast([64, P]))
                ch.link(ins) if way == 0 else ins.then_inc(pick_ready, 1)
            dve.wait_ge(head_ready, t.count("head_ready"))
            taken = []
            for part in range(2 if rows else 0):
                s = t.turn % 2
                pass_acc(t)
                taken.append((acc_free[s], t.count(f"acc{s}")))
            for part in range(2):
                if part and rows:
                    add_rows(dve, t, ch)
                if taken:
                    dve.wait_ge(*taken[part])
                for j in range(TAPS):
                    shifted = conv_in[:, part, 2 + j:2 + j + TOK]
                    tap = head_par[:, part * (TAPS + 1) + j:part * (TAPS + 1) + j + 1]
                    out = conv_out[:, part, :]
                    if j == 0:
                        ins = dve.tensor_scalar(out, shifted, tap, None, ALU.mult)
                    else:
                        ch.sync()
                        ins = dve.scalar_tensor_tensor(out=out, in0=shifted, scalar=tap, in1=out, op0=ALU.mult, op1=ALU.add)
                    ch.link(ins) if j < TAPS - 1 else ins.then_inc(conv_summed, 1)
            pass_acc(t, 2)
            t.next("num")
            for _ in range(2):
                s = t.turn % 2
                pass_acc(t)
                dve.wait_ge(acc_free[s], t.count(f"acc{s}"))
            ch.sync()

            def arguments(i):
                for way in range(2):
                    ins = dve.scalar_tensor_tensor(out=wts[:, i % 3, i + way, :], in0=r_all[:, way, i * P:(i + 1) * P],
                                                   scalar=a_head[:, way, i, i:i + 1], in1=masks[:, way, :],
                                                   op0=ALU.add, op1=ALU.add)
                    ch.link(ins) if way == 0 else ins.then_inc(args_ready, 1)

            def weights(i):
                dve.wait_ge(w_exp, t.next("w_exp"))
                s = await_acc(dve, t)
                for way in range(2):
                    j0, j1 = (0, i + 1) if way == 0 else (i, TT)
                    w = wts[:, i % 3, j0 + way:j1 + way, :].rearrange("p a b -> p (a b)")
                    ins = dve.scalar_tensor_tensor(out=w, in0=acc[s][:, j0 * P:j1 * P], scalar=float(P) ** -0.5, in1=w,
                                                   op0=ALU.mult, op1=ALU.mult)
                    ch.link(ins) if way == 0 else ins.then_inc(acc_free[s], 1)

            def take_sums(i):
                num = NUM[i % 2]
                both = num.rearrange("p (w c) -> p w c", w=2)[:, :, P]
                ch.link(dve.scalar_tensor_tensor(out=stats[:, 0:2], in0=both, scalar=-1.0, in1=em_head[:, i, :],
                                                 op0=ALU.mult, op1=ALU.max))
                ch.sync()
                ch.link(dve.tensor_tensor(stats[:, 0:2], stats[:, 0:2], both, ALU.max))
                ch.sync()
                ch.link(dve.reciprocal(stats[:, 2:4], stats[:, 0:2]))
                ch.sync()
                ch.link(dve.tensor_scalar(h_tok[:, i, :], num[:, 0:P], stats[:, 2:3], None, ALU.mult))
                ch.sync()
                dve.scalar_tensor_tensor(out=h_tok[:, i, :], in0=num[:, HALF:HALF + P], scalar=stats[:, 3:4],
                                         in1=h_tok[:, i, :], op0=ALU.mult, op1=ALU.add).then_inc(num_free, 1)
                dve.wait_ge(num_free, t.count("num"))
                ch.link(dve.bn_stats(stats[:, 4:10], h_tok[:, i, :]))
                ch.sync()
                ins = dve.bn_aggr(stats[:, 16 + 2 * i:18 + 2 * i], stats[:, 4:10])
                ch.link(ins) if i < TT - 1 else ins.then_inc(cols_ready, 1)

            arguments(0)
            arguments(1)
            for i in range(TT + 1):
                if i < TT:
                    weights(i)
                if i >= 1:
                    dve.wait_ge(num_full, t.next("num"))
                if i + 2 < TT:
                    arguments(i + 2)
                if i >= 1:
                    take_sums(i - 1)
            dve.wait_ge(soft_ready, t.next("soft_ready"))
            ch.link(dve.reciprocal(stats[:, 32:40], stats[:, 32:40]))
            mean = stats[:, 16:32].rearrange("p (n two) -> p n two", two=2)[:, :, 0:1].to_broadcast([P, TT, P])
            ch.link(dve.tensor_tensor(h_tok[:, :, :], h_tok[:, :, :], mean, ALU.subtract))
            ch.sync()
            dve.tensor_tensor(h_tok[:, :, :], h_tok[:, :, :], stats[:, 32:40].unsqueeze(2).to_broadcast([P, TT, P]),
                              ALU.mult).then_inc(h_ready, 1)
            dve.wait_ge(num_full, t.next("num"))
            dve.scalar_tensor_tensor(out=mix_t[:, :], in0=NUM[0], scalar=head_par[:, HEAD_PAR - 1:HEAD_PAR],
                                     in1=o_gate[:, :], op0=ALU.mult, op1=ALU.mult).then_inc(num_free, 1)
            split_lo(dve, t, mix_t[:, :], mix_hi[:, :], mix_lo[:, :])

        def mlstm_tensor(pe, t):
            head_tensor(pe, t, False)
            with t.loop(M_HEADS - 1, acc0=11, acc1=11, block=6, hi_ready=1, lo_ready=1, pick_ready=1, conv_ready=2,
                        num=10, h_ready=1):
                head_tensor(pe, t, True)

        def mlstm_scalar(act, t, ch):
            head_scalar(act, t, ch, False)
            with t.loop(M_HEADS - 1, acc0=11, acc1=11, hi_ready=1, lo_ready=1, head_ready=1, conv_summed=2,
                        num=10, args_ready=8, cols_ready=1, soft_ready=1):
                head_scalar(act, t, ch, True)

        def mlstm_vector(dve, t, ch):
            head_vector(dve, t, ch, 0, False)
            ch.reset()
            with t.loop(M_HEADS - 1, acc0=11, acc1=11, hi_ready=1, lo_ready=1, head_ready=1, w_exp=8,
                        num=10, soft_ready=1) as i:
                head_vector(dve, t, ch, i + 1, True)
                ch.reset()

        def window_tensor(pe, t):
            await_parts(pe, t, 1)
            row_block(pe, t, [(mix_hi[:, :], mix_lo[:, :])])
            feature_block(pe, t)
            feature_block(pe, t)
            turn_tiles(pe, t, local.v_t)
            feature_block(pe, t)
            for n in range(HEAD_PAIRS):
                if n:
                    await_parts(pe, t, 1)
                    row_block(pe, t, [(att2_hi[:, :], att2_lo[:, :])])
                await_all_taken(pe, t)
                att_tensor(pe, t, local, keys_2, next_block=n < HEAD_PAIRS - 1)
            await_parts(pe, t, 1)
            row_block(pe, t, [(att2_hi[:, :], att2_lo[:, :])])

        def take_total(act, t, ch, a, hi):
            act.wait_ge(lo_ready, t.count("lo_ready"))
            ch.link(act.activation(a.total[:, :], att_out, ACT.Copy))
            ch.sync()
            split_hi(act, t, a.total[:, :], hi)
            t.next("lo_ready")

        def window_scalar(act, t, ch):
            pass_acc(t, KT)
            act.wait_ge(lo_ready, t.count("lo_ready"))
            for dst in (local.v_t[:, :], local.k_t[:, :], local.v_tok[:, :, :].rearrange("p a b -> p (a b)")):
                s = await_acc(act, t)
                act.activation(dst, acc[s], ACT.Copy).then_inc(acc_free[s], 1)
            for n in range(HEAD_PAIRS):
                act.dma_start(local.bias[:, :, 0:3 * P], bias_2[n]).then_inc(bias_in, 16)
                s = await_acc(act, t)
                act.activation(local.q_t[:, :], acc[s], ACT.Copy, scale=0.125).then_inc(acc_free[s], 1)
                if n:
                    pass_acc(t, KT)
                att_scalar(act, t, ch, local, keys_2, sink=lambda side: col("sink", 2 * n + side))
                take_total(act, t, ch, local, att2_hi[:, :])

        def window_vector(dve, t, ch):
            add_rows(dve, t, ch)
            pass_acc(t, 3)
            ch.link(dve.tensor_scalar(small[:, 40:48], par[:, COL["sink"]:COL["sink"] + 8], -1.0, None, ALU.mult))
            ch.sync()
            for n in range(HEAD_PAIRS):
                pass_acc(t)
                if n:
                    add_rows(dve, t, ch)
                dve.wait_ge(bias_in, t.next("bias_in") * 16)
                att_vector(dve, t, ch, local, keys_2, sink=lambda side: small[:, 40 + 2 * n + side:41 + 2 * n + side])
                split_lo(dve, t, local.total[:, :], att2_hi[:, :], att2_lo[:, :])

        def ple_tensor(pe, t):
            await_parts(pe, t, 2)
            row_block(pe, t, [(p_hi[:, k, :], p_lo[:, k, :]) for k in range(2)])
            with t.loop(KT // 2, acc0=1, acc1=1, block=2):
                feature_block(pe, t)
                feature_block(pe, t)

        def ple_scalar(act, t, ch):
            act.wait_ge(lo_ready, t.count("lo_ready"))
            act.dma_start(p_rows[:, :, :], p_t.rearrange("(k p) n -> p k n", p=P)).then_inc(p_in, 16)
            act.wait_ge(p_in, 16)
            for k in range(2):
                split_hi(act, t, p_rows[:, k, :], p_hi[:, k, :])
                t.next("lo_ready")
            for n in range(KT):
                s = await_acc(act, t)
                act.activation(ple[:, n, :], acc[s], ACT.Copy).then_inc(acc_free[s], 1)
            act.wait_ge(lo_ready, t.count("lo_ready"))

            def gates(first):
                for q in range(2):
                    if not first:
                        act.wait_ge(ple_used, t.next("ple_used"))
                    s = await_acc(act, t)
                    act.activation(ple_gate[:, q, :], acc[s], ACT.Sigmoid).then_inc(acc_free[s], 1)

            gates(True)
            with t.loop(KT // 2 - 1, acc0=1, acc1=1, ple_used=2):
                gates(False)

        def ple_vector(dve, t, ch):
            for k in range(2):
                split_lo(dve, t, p_rows[:, k, :], p_hi[:, k, :], p_lo[:, k, :])
            pass_acc(t, KT)
            for s in range(2):
                dve.wait_ge(acc_free[s], t.count(f"acc{s}"))
            ch.reset()
            with t.loop(KT // 2, acc0=1, acc1=1) as i:
                for q in range(2):
                    where = bass.ds(2 * i + q, 1)
                    s = t.turn % 2
                    pass_acc(t)
                    dve.wait_ge(acc_free[s], t.count(f"acc{s}"))
                    ch.link(dve.tensor_tensor(ple_gate[:, q, :], ple_gate[:, q, :],
                                              ple[:, where, :].rearrange("p a n -> p (a n)"), ALU.mult))
                    ch.sync()
                    row = h[:, where, :].rearrange("p a n -> p (a n)")
                    dve.tensor_tensor(row, row, ple_gate[:, q, :], ALU.add).then_inc(ple_used, 1)
                ch.reset()
            dve.wait_ge(ple_used, KT)

        def glu_tensor(pe, t):
            before = expect_parts(t, KT)
            with t.loop(CONV_TILES // 2, acc0=2, acc1=2, block=4):
                for j in range(4):
                    feature_block(pe, t, parts_from=before if j == 0 else None)
            with t.loop(CONV_TILES // 2, acc0=1, acc1=1, block=2):
                for _ in range(2):
                    feature_block(pe, t)

        def glu_scalar(act, t, ch):
            with t.loop(CONV_TILES // 2, acc0=2, acc1=2, head_ready=1):
                act.wait_ge(head_ready, t.next("head_ready"))
                for q in range(2):
                    act.wait_ge(acc_free[(t.turn + 1) % 2], t.count(f"acc{(t.turn + 1) % 2}"))
                    s = await_acc(act, t)
                    act.activation(sigmoid[:, q, :], acc[s], ACT.Sigmoid, bias=glu_par[:, q, GLU_PAR - 1:GLU_PAR])\
                       .then_inc(acc_free[s], 1)
                    pass_acc(t)
            for j in range(CONV_TILES):
                s = await_acc(act, t)
                act.activation(z_conv[j], acc[s], ACT.Silu, bias=col("b_z", j)).then_inc(acc_free[s], 1)

        def glu_vector(dve, t, ch):
            ch.link(dve.memset(u_pad[:, :, :], 0.0))
            ch.reset()
            with t.loop(CONV_TILES // 2, acc0=2, acc1=2, head_ready=1) as i:
                dve.tensor_copy(glu_par[:, :, :].rearrange("p a b -> p (a b)"),
                                par[:, bass.ds(COL["glu"] + i * (2 * GLU_PAR), 2 * GLU_PAR)]).then_inc(head_ready, 1)
                t.next("head_ready")
                for q in range(2):
                    s = t.turn % 2
                    pass_acc(t)
                    dve.wait_ge(acc_free[s], t.count(f"acc{s}"))
                    s = await_acc(dve, t)
                    if q == 0:
                        dve.wait_ge(head_ready, t.count("head_ready"))
                    dve.scalar_tensor_tensor(out=u_pad[:, q, REACH:REACH + TOK], in0=acc[s],
                                             scalar=glu_par[:, q, GLU_PAR - 2:GLU_PAR - 1], in1=sigmoid[:, q, :],
                                             op0=ALU.add, op1=ALU.mult).then_inc(acc_free[s], 1)
                    dve.wait_ge(acc_free[s], t.count(f"acc{s}"))
                    out = conv_sum[:, bass.ds(2 * i + q, 1), :].rearrange("p a n -> p (a n)")
                    for j in range(CONV_TAPS):
                        tap, shifted = glu_par[:, q, j:j + 1], u_pad[:, q, j:j + TOK]
                        if j == 0:
                            ch.link(dve.tensor_scalar(out, shifted, tap, glu_par[:, q, CONV_TAPS:CONV_TAPS + 1],
                                                      ALU.mult, ALU.add))
                        else:
                            ch.sync()
                            ch.link(dve.scalar_tensor_tensor(out=out, in0=shifted, scalar=tap, in1=out,
                                                             op0=ALU.mult, op1=ALU.add))
                ch.reset()
            pass_acc(t, CONV_TILES)
            dve.memset(small[:, 62:63], 0.0).then_inc(conv_done, 1)

        def conv_tensor(pe, t):
            pe.wait_ge(conv_done, 1)
            s = claim(pe, t)
            for k in range(CONV_TILES):
                for half in range(2):
                    c = slice(half * HALF, (half + 1) * HALF)
                    ins = pe.matmul(acc[s][:, c], mean_w[:, :], conv_sum[:, k, c], start=(k == 0), stop=(k == CONV_TILES - 1))
            ins.then_inc(acc_full[s], 1)
            take_turn(pe, t)
            sum_squares(pe, t, CONV_TILES)
            await_parts(pe, t, CONV_TILES)
            for _ in range(CONV_TILES // 2):
                slot = take_block(pe, t)
                for o in range(2):
                    product(pe, t, [(slot, 4 * o + k, c_hi[:, k, :], c_lo[:, k, :]) for k in range(4)], o == 0)
            for g in range(CONV_TILES):
                group_sums(pe, t, square3[:, g % 3, :])
            await_parts(pe, t, CONV_TILES)
            row_block(pe, t, [(c_hi[:, k, :], c_lo[:, k, :]) for k in range(CONV_TILES)])

        def group_sums(pe, t, squares_of):
            pe.wait_ge(group_in, 16)
            pe.wait_ge(squared, t.next("squared"))
            s = claim(pe, t)
            for half in range(2):
                c = slice(half * HALF, (half + 1) * HALF)
                ins = pe.matmul(acc[s][:, c], group_w[:, :], squares_of[:, c], start=True, stop=True)
            ins.then_inc(acc_full[s], 1)
            take_turn(pe, t)

        def conv_scalar(act, t, ch):
            act.dma_start(group_w[:, :], consts[:, 4 * P:5 * P]).then_inc(group_in, 16)
            pass_acc(t)
            for k in range(CONV_TILES):
                if k < CONV_TILES - 1:
                    act.wait_ge(centred, t.next("centred"))
                else:
                    act.wait_ge(acc_free[(t.turn - 1) % 2], t.count(f"acc{(t.turn - 1) % 2}"))
                squares(act, t, k, conv_sum[:, k, :])
            t.next("square_used")
            s = await_acc(act, t)
            inverse_root(act, ch, rstd[:, :], acc[s], "eps6", 2.0).then_inc(acc_free[s], 1)
            for k in range(CONV_TILES):
                row = conv_sum[:, k, :]
                act.wait_ge(rows_ready, t.next("rows_ready"))
                ch.link(act.activation(row, row, ACT.Silu, bias=col("cln_b", k)))
                ch.sync()
                split_hi(act, t, row, c_hi[:, k, :])
                t.next("lo_ready")

            def square_group(g):
                act.activation(square3[:, g % 3, :], y_conv[:, g, :], ACT.Square).then_inc(squared, 1)

            for g in range(CONV_TILES):
                s = await_acc(act, t)
                act.activation(y_conv[:, g, :], acc[s], ACT.Identity, bias=col("pw_b", g)).then_inc(acc_free[s], 1)
                if g < 3:
                    act.wait_ge(acc_free[s], t.count(f"acc{s}"))
                    if g == 2:
                        act.wait_ge(lo_ready, t.count("lo_ready"))
                    square_group(g)
            for g in range(CONV_TILES):
                s = await_acc(act, t)
                inverse_root(act, ch, square3[:, g % 3, :], acc[s], "eps6").then_inc(acc_free[s], 1)
                act.wait_ge(rows_ready, t.next("rows_ready"))
                split_hi(act, t, y_conv[:, g, :], c_hi[:, g, :])
                t.next("lo_ready")
                if g == 0:
                    square_group(3)
            pass_acc(t, KT)
            await_all_taken(act, t)

        def gate_group(dve, ch, t, y, root, gain, z):
            ch.link(dve.scalar_tensor_tensor(out=y, in0=y, scalar=gain, in1=root, op0=ALU.mult, op1=ALU.mult))
            ch.sync()
            dve.tensor_tensor(y, y, z, ALU.mult).then_inc(rows_ready, 1)

        def conv_vector(dve, t, ch):
            for k in range(2 * CONV_TILES):
                t.next("squared")
                if k < CONV_TILES - 1:
                    t.next("square_used")
            s = await_acc(dve, t)
            for k in range(CONV_TILES):
                ins = dve.scalar_tensor_tensor(out=conv_sum[:, k, :], in0=acc[s], scalar=-2.0, in1=conv_sum[:, k, :],
                                               op0=ALU.mult, op1=ALU.add)
                ins.then_inc(centred if k < CONV_TILES - 1 else acc_free[s], 1)
            s = t.turn % 2
            pass_acc(t)
            dve.wait_ge(acc_free[s], t.count(f"acc{s}"))
            for k in range(CONV_TILES + 1):
                if k < CONV_TILES:
                    row = conv_sum[:, k, :]
                    dve.scalar_tensor_tensor(out=row, in0=row, scalar=col("cln_g", k), in1=rstd[:, :],
                                             op0=ALU.mult, op1=ALU.mult).then_inc(rows_ready, 1)
                if k >= 1:
                    split_lo(dve, t, conv_sum[:, k - 1, :], c_hi[:, k - 1, :], c_lo[:, k - 1, :])
            pass_acc(t, CONV_TILES)
            for g in range(CONV_TILES):
                s = t.turn % 2
                pass_acc(t)
                dve.wait_ge(acc_free[s], t.count(f"acc{s}"))
                gate_group(dve, ch, t, y_conv[:, g, :], square3[:, g % 3, :], col("gn_conv", g), z_conv[g])
                split_lo(dve, t, y_conv[:, g, :], c_hi[:, g, :], c_lo[:, g, :])
            add_rows(dve, t, ch)

        def near_projections(pe, t, first):
            feature_block(pe, t)
            if not first:
                group_sums(pe, t, square[:, 1, :])
            turn_tiles(pe, t, local.v_t)
            feature_block(pe, t)
            feature_block(pe, t)

        def near_rows(pe, t):
            await_parts(pe, t, 1)
            row_block(pe, t, [(att2_hi[:, :], att2_lo[:, :])])

        def near_tensor(pe, t):
            feature_block(pe, t)
            near_projections(pe, t, True)
            await_all_taken(pe, t)
            att_tensor(pe, t, local, keys_3)
            with t.loop(HEAD_PAIRS - 1, acc0=15, acc1=15, block=6, p_ready=16, turned_copied=16, squared=1,
                        hi_ready=1, lo_ready=1):
                near_projections(pe, t, False)
                near_rows(pe, t)
                await_all_taken(pe, t)
                att_tensor(pe, t, local, keys_3)
                skip_block(pe, t)
            group_sums(pe, t, square[:, 1, :])
            near_rows(pe, t)

        def near_scalar(act, t, ch):
            def take(dst, func, scale=1.0, bias=0.0):
                s = await_acc(act, t)
                act.activation(dst, acc[s], func, scale=scale, bias=bias).then_inc(acc_free[s], 1)

            def take_root():
                s = await_acc(act, t)
                inverse_root(act, ch, rstd[:, :], acc[s], "eps6").then_inc(acc_free[s], 1)

            def split_gated():
                act.wait_ge(rows_ready, t.next("rows_ready"))
                split_hi(act, t, local.total[:, :], att2_hi[:, :])
                t.next("lo_ready")

            def project(pair, first):
                own = COL["pairs"] + pair * PAIR_PAR
                act.dma_start(local.bias[:, :, :], bias_3[bass.ds(pair, 1)].rearrange("a p s k -> p (a s) k"))\
                    .then_inc(bias_in, 16)
                ch.link(act.activation(pair_par[:, 0:4], par[:, bass.ds(own, 4)], ACT.Copy))
                ch.sync()
                ch.link(act.activation(pair_par[:, 5:6], pair_par[:, 0:1], ACT.Copy, scale=0.125))
                ch.sync()
                take(local.v_t[:, :], ACT.Copy)
                take(local.q_t[:, :], ACT.Identity, 0.125, pair_par[:, 5:6])
                if not first:
                    take_root()
                take(local.v_tok[:, :, :].rearrange("p a b -> p (a b)"), ACT.Copy)
                take(local.k_t[:, :], ACT.Identity, 1.0, pair_par[:, 1:2])
                if not first:
                    split_gated()
                ch.link(act.activation(pair_par[:, 4:5], par[:, bass.ds(own + 4, 1)], ACT.Copy))
                ch.sync()
                take(z_att[:, :], ACT.Silu, 1.0, pair_par[:, 3:4])

            def outputs():
                ch.link(act.activation(local.total[:, :], att_out, ACT.Identity, bias=pair_par[:, 2:3]))
                ch.sync()
                act.activation(square[:, 1, :], local.total[:, :], ACT.Square).then_inc(squared, 1)

            project(0, True)
            att_scalar(act, t, ch, local, keys_3)
            outputs()
            ch.reset()
            with t.loop(HEAD_PAIRS - 1, acc0=15, acc1=15, turned_full=16, pv_done=16, rows_ready=1, hi_ready=1,
                        lo_ready=1) as i:
                project(i + 1, False)
                pass_acc(t, KT)
                att_scalar(act, t, ch, local, keys_3)
                act.wait_ge(lo_ready, t.count("lo_ready"))
                outputs()
                ch.reset()
            take(local.v_t[:, :], ACT.Copy)
            take_root()
            split_gated()
            pass_acc(t, KT)

        def near_vector(dve, t, ch):
            def gated_outputs():
                t.next("squared")
                s = t.turn % 2
                pass_acc(t)
                dve.wait_ge(acc_free[s], t.count(f"acc{s}"))
                gate_group(dve, ch, t, local.total[:, :], rstd[:, :], pair_par[:, 4:5], z_att[:, :])
                split_lo(dve, t, local.total[:, :], att2_hi[:, :], att2_lo[:, :])

            pass_acc(t, 5)
            dve.wait_ge(bias_in, t.next("bias_in") * 16)
            att_vector(dve, t, ch, local, keys_3)
            ch.reset()
            with t.loop(HEAD_PAIRS - 1, acc0=15, acc1=15, exp_done=16, bias_in=1, squared=1, hi_ready=1, lo_ready=1):
                pass_acc(t, 2)
                gated_outputs()
                pass_acc(t, 3)
                add_rows(dve, t, ch)
                dve.wait_ge(bias_in, t.next("bias_in") * 16)
                att_vector(dve, t, ch, local, keys_3)
                ch.reset()
            pass_acc(t)
            gated_outputs()
            add_rows(dve, t, ch)


        @block.sync
        def _(sp):
            sp.dma_start(raw[:, 0, :], blocks[0]).then_inc(raw_in[0], 16)
            sp.dma_start(raw[:, 1, :], blocks[1]).then_inc(raw_in[1], 16)
            with sp.Fori(1, n_blocks // 2) as i:
                for slot in range(2):
                    sp.wait_ge(w_split, 2 * i - 1 + slot)
                    sp.dma_start(raw[:, slot, :], blocks[bass.ds(2 * i + slot, 1)].rearrange("a p n -> p (a n)"))\
                      .then_inc(raw_in[slot], 16)

        @block.gpsimd
        def _(pool):
            pool.memset(zero[:, :], 0.0).then_inc(zero_ready, 1)
            pool.wait_ge(zero_ready, 1)
            pool.wait_ge(sgu_in, 16)
            pool.affine_select(out=sgu_wt[:, :, :], in_=sgu_wt[:, :, :], compare_op=ALU.is_ge, fill=0.0, base=0,
                               pattern=[[0, 4], [1, P]], channel_multiplier=-1).then_inc(sgu_w_ready, 1)
            nothing = zero[:, 0:1].to_broadcast([P, 1024])

            def split_block(slot):
                whole = raw[:, slot, :]
                hi = w_hi[:, slot, :, :].rearrange("p a b -> p (a b)")
                pool.tensor_tensor(hi, whole, nothing, ALU.add).then_inc(hi_split, 1)
                return whole, hi, w_lo[:, slot, :, :].rearrange("p a b -> p (a b)")

            for b in range(2):
                pool.wait_ge(raw_in[b], 16)
                whole, hi, lo = split_block(b)
                pool.wait_ge(hi_split, b + 1)
                pool.tensor_tensor(lo, whole, hi.bitcast(F32), ALU.subtract).then_inc(w_split, 1)
            with pool.Fori(1, n_blocks // 2) as i:
                for slot in range(2):
                    pool.wait_ge(w_used, 2 * i + slot)
                    pool.wait_ge(raw_in[slot], 16 * i + 16)
                    whole, hi, lo = split_block(slot)
                    pool.wait_ge(hi_split, 2 * i + slot + 1)
                    pool.tensor_tensor(lo, whole, hi.bitcast(F32), ALU.subtract).then_inc(w_split, 1)

        @block.tensor
        def _(pe):
            t = Turns(pe)
            pe.wait_ge(const_in, 48)
            norm_tensor(pe, t)
            att1_tensor(pe, t)
            sgu_tensor(pe, t)
            merge_tensor(pe, t)
            norm_tensor(pe, t)
            ffn_tensor(pe, t)
            norm_tensor(pe, t)
            gates_tensor(pe, t)
            mlstm_tensor(pe, t)
            window_tensor(pe, t)
            norm_tensor(pe, t, centre=True)
            ffn_tensor(pe, t)
            ple_tensor(pe, t)
            norm_tensor(pe, t, centre=True)
            norm_tensor(pe, t)
            glu_tensor(pe, t)
            conv_tensor(pe, t)
            near_tensor(pe, t)
            norm_tensor(pe, t)

        @block.scalar
        def _(act):
            t, ch = Turns(act), Chain(act, s_chain)
            act.dma_start(par[:, :], params).then_inc(const_in, 16)
            act.dma_start(ident[:, :], consts[:, 0:P]).then_inc(const_in, 16)
            act.dma_start(mean_w[:, :], consts[:, P:2 * P]).then_inc(const_in, 16)
            act.dma_start(sgu_wt[:, :, :], sgu_w).then_inc(sgu_in, 16)
            for k in range(KT):
                act.dma_start(h[:, k, :], x_t[k * P:(k + 1) * P, :]).then_inc(x_in[k], 16)
            act.wait_ge(const_in, 48)
            norm_scalar(act, t, ch, "split")
            att1_scalar(act, t, ch)
            sgu_scalar(act, t, ch)
            merge_scalar(act, t, ch)
            norm_scalar(act, t, ch, "split", rows=True)
            ffn_scalar(act, t, ch)
            norm_scalar(act, t, ch, "keep", rows=True)
            gates_scalar(act, t, ch)
            mlstm_scalar(act, t, ch)
            window_scalar(act, t, ch)
            norm_scalar(act, t, ch, "keep", centre=True, rows=True, eps="eps5", beta="ln1_b")
            ffn_scalar(act, t, ch)
            pass_acc(t, KT)
            ple_scalar(act, t, ch)
            norm_scalar(act, t, ch, "hold", centre=True, eps="eps5", beta="ln2_b")
            norm_scalar(act, t, ch, "split", summed=True)
            glu_scalar(act, t, ch)
            conv_scalar(act, t, ch)
            near_scalar(act, t, ch)
            norm_scalar(act, t, ch, "out")
            act.wait_ge(stored, 16 * KT)

        @block.vector
        def _(dve):
            t, ch = Turns(dve), Chain(dve, v_chain)
            dve.wait_ge(const_in, 48)
            norm_vector(dve, t, ch, "split", "norm_mix")
            att1_vector(dve, t, ch)
            sgu_vector(dve, t, ch)
            merge_vector(dve, t, ch)
            norm_vector(dve, t, ch, "split", "norm_ffn", rows=True)
            ffn_vector(dve, t, ch)
            norm_vector(dve, t, ch, "keep", "norm_final", rows=True)
            gates_vector(dve, t, ch)
            mlstm_vector(dve, t, ch)
            window_vector(dve, t, ch)
            norm_vector(dve, t, ch, "keep", "ln1_g", centre=True, rows=True)
            ffn_vector(dve, t, ch)
            add_rows(dve, t, ch)
            ple_vector(dve, t, ch)
            norm_vector(dve, t, ch, "hold", "ln2_g", centre=True)
            norm_vector(dve, t, ch, "split", "ln3_g", summed=True)
            glu_vector(dve, t, ch)
            conv_vector(dve, t, ch)
            near_vector(dve, t, ch)
            norm_vector(dve, t, ch, "out", "final_g")


def tile(w, k, n):
    return w[k * P:(k + 1) * P, n * P:(n + 1) * P]


def column_block(w, n):
    return w[:, n * P:(n + 1) * P].reshape(KT, P, P).transpose(1, 0, 2)


def row_blocks(w, k, n=1):
    parts = w[k * P:(k + n) * P].reshape(n, P, KT, P).transpose(1, 2, 0, 3)
    return [parts[:, g * (KT // n):(g + 1) * (KT // n)].reshape(P, KT, P) for g in range(n)]


def ffn_blocks(w_in, w_out):
    hidden = w_in.shape[1] // 2 // P
    for i in range(hidden // 2 + 1):
        columns = [c for k in (2 * i, 2 * i + 1) if k < hidden for c in (k, hidden + k)]
        rows = row_blocks(w_out, 2 * i - 2, 2) if i else []
        yield from [column_block(w_in, c) for c in columns[:1]] + rows + [column_block(w_in, c) for c in columns[1:]]


def first_blocks(w_in, w_br_att, w_br_sgu, w_out, w_ffn_in, w_ffn_out):
    for hp in range(HEAD_PAIRS):
        for group in (2, 0, 1):
            yield column_block(w_in, 4 * group + hp)
    for group in (4, 3):
        for j in range(4):
            yield column_block(w_in, 4 * group + j)
    for n in range(KT + 1):
        if n < KT:
            yield column_block(w_in, 20 + n)
            yield column_block(w_in, 28 + n)
        if n:
            yield from row_blocks(w_out, n - 1)
        if n < KT:
            both = np.concatenate([w_br_att, w_br_sgu])[:, n * P:(n + 1) * P]
            yield both.reshape(KT, P, P).transpose(1, 0, 2)
    yield from ffn_blocks(w_ffn_in, w_ffn_out)


def spread_gates(v):
    out = np.zeros(v.shape[:-1] + (P,), np.float32)
    for group in range(4):
        out[..., 32 * group:32 * group + M_HEADS] = v[..., M_HEADS * group:M_HEADS * (group + 1)]
    return out


def second_blocks(w_in, w_out, w_ffn_in, w_ffn_out, w_ple_gate, w_ple_proj):
    gates, a_q, a_k = 2048, 2064, 2576
    yield column_block(spread_gates(w_in[:, gates:a_q]), 0)
    for head in range(M_HEADS):
        yield column_block(w_in, head)
        yield column_block(w_in, 4 + head)
        if head:
            yield from row_blocks(w_out, head - 1)
        yield column_block(w_in, 8 + head)
        yield column_block(w_in, 12 + head)
        if head:
            yield np.zeros((P, KT, P), np.float32)
    yield from row_blocks(w_out, M_HEADS - 1)
    yield column_block(w_in[:, a_k:], 1)
    yield column_block(w_in[:, a_k:], 0)
    q_heads = w_in[:, a_q:a_k].reshape(D, 2, 4, 64)
    out_heads = w_out[512:].reshape(2, 4, 64, D)
    for n in range(HEAD_PAIRS + 1):
        if n < HEAD_PAIRS:
            yield column_block(q_heads[:, :, n].reshape(D, P), 0)
        if n:
            yield from row_blocks(out_heads[:, n - 1].reshape(P, D), 0)
    yield from ffn_blocks(w_ffn_in, w_ffn_out)
    yield from row_blocks(w_ple_proj, 0, 2)
    for n in range(KT):
        yield column_block(w_ple_gate, n)


def third_blocks(w_in, pw_w, w_out):
    for j in range(CONV_TILES):
        yield column_block(w_in, 4 + j)
        yield column_block(w_in, j)
    for j in range(CONV_TILES):
        yield column_block(w_in, 8 + j)
    for b in range(2):
        yield pw_w[:, 2 * b * P:(2 * b + 2) * P].reshape(4, P, 2, P).transpose(1, 2, 0, 3).reshape(P, KT, P)
    yield from row_blocks(w_out, 0, 4)
    yield column_block(w_in, 20)
    for pair in range(HEAD_PAIRS):
        for group in (12, 16, 24):
            yield column_block(w_in, group + pair)
        if pair:
            yield from row_blocks(w_out, 4 + pair - 1)
        yield column_block(w_in, 21 + pair) if pair < HEAD_PAIRS - 1 else np.zeros((P, KT, P), np.float32)
        if pair:
            yield np.zeros((P, KT, P), np.float32)
    yield from row_blocks(w_out, 4 + HEAD_PAIRS - 1)


def near_bias(rpb):
    table = np.full((HEADS, P, N_BIAS_3), NEG, np.float32)
    for p in (0, 1, 2, 6, 7):
        first, count, at = BIAS_3[p]
        q, k = p * P + np.arange(P)[:, None], first + np.arange(count)[None, :]
        row, column, key_row, key_column = q // 64, q % 64, k // 64, k % 64
        row_start, column_start = np.clip(row - 4, 0, 8), np.clip(column - 8, 0, 48)
        seen = (key_row >= row_start) & (key_row < row_start + 8) \
            & (key_column >= column_start) & (key_column < column_start + 16)
        row_at, column_at = np.clip(key_row - row + 7, 0, 14), np.clip(key_column - column + 15, 0, 30)
        table[:, :, at:at + count] = np.where(seen, rpb[:, row_at, column_at], np.float32(NEG))
    return np.ascontiguousarray(table.reshape(HEAD_PAIRS, 2, P, N_BIAS_3).transpose(0, 2, 1, 3))


def window_bias():
    q, k = np.arange(P)[:, None], np.arange(3 * P)[None, :] - P
    distance = np.abs(k - q).astype(np.float32)
    slopes = np.exp2(-np.arange(1, HEADS + 1, dtype=np.float32))
    table = np.where(distance <= P, -slopes[:, None, None] * distance, np.float32(NEG))
    return np.ascontiguousarray(table.reshape(2, HEAD_PAIRS, P, 3 * P).transpose(1, 2, 0, 3))


def per_feature(v):
    return np.asarray(v).reshape(-1, P).T


def banded_bias(rel_bias):
    q, k = np.arange(P)[:, None], np.arange(ATT_BIAS_1)[None, :]
    distance = np.clip(q - (k - 512), -128, 128) + 128
    key_chunk, query_chunk = k // 64 - 8, q // 64
    seen = (key_chunk <= query_chunk) & (key_chunk >= query_chunk - 8)
    table = np.where(seen[None], rel_bias[:, distance], np.float32(NEG))
    return np.ascontiguousarray(table.reshape(HEAD_PAIRS, 2, P, ATT_BIAS_1).transpose(0, 2, 1, 3))


_INS = ["x_t", "blocks", "params", "consts", "bias_1", "bias_2", "bias_3", "sgu_rows", "sgu_w", "p_t"]


def kernel(**inputs):
    import concourse.bacc as bacc
    from concourse.bass_utils import run_bass_kernel_spmd

    g = {name: np.asarray(a) for name, a in inputs.items()}
    stream = list(first_blocks(g["w_in"][0], g["w_br_att"][0], g["w_br_sgu"][0], g["w_out"][0],
                               g["w_ffn_in"][0], g["w_ffn_out"][0]))
    stream += second_blocks(g["w_in_2"][0], g["w_out_2"][0], g["w_ffn_in_2"][0], g["w_ffn_out_2"][0],
                            g["w_ple_gate_2"][0], g["w_ple_proj_2"][0])
    stream += third_blocks(g["w_in_3"][0], g["pw_w_3"][0], g["w_out_3"][0])
    if len(stream) % 2:
        stream.append(stream[-1])
    params = np.zeros((P, N_PARAMS), np.float32)

    def put(name, columns):
        columns = np.asarray(columns)
        params[:, COL[name]:COL[name] + columns.shape[1]] = columns

    put("norm_mix", per_feature(g["norm_mix"][0]))
    put("b_gate", per_feature(g["b_gate"][0]))
    put("norm_ffn", per_feature(g["norm_ffn"][0]))
    put("norm_final", per_feature(g["norm_final"]))
    conv = np.concatenate([g["conv_w_2"][0], g["conv_b_2"]]).reshape(TAPS + 1, 2, M_HEADS, P)
    for head in range(M_HEADS):
        own = np.concatenate([conv[:, :, head].transpose(2, 1, 0).reshape(P, -1),
                              g["mlstm_norm_g_2"][0, head * P:(head + 1) * P, None]], 1)
        params[:, COL["heads"] + head * HEAD_PAR:COL["heads"] + (head + 1) * HEAD_PAR] = own
    put("gate_b", spread_gates(g["b_gate_2"]).T)
    put("sink", np.broadcast_to(g["attn_sink_2"][0].reshape(2, HEAD_PAIRS).T.reshape(1, HEADS), (P, HEADS)))
    for name in ("ln1_g", "ln1_b", "ln2_g", "ln2_b"):
        put(name, per_feature(g[name + "_2"][0]))
    put("ln3_g", per_feature(g["ln_g_3"][0]))
    b_in = per_feature(g["b_in_3"][0])
    taps = g["dw_w_3"][0].reshape(CONV_TAPS, CONV_TILES, P).transpose(2, 1, 0)
    glu = np.concatenate([taps, per_feature(g["dw_b_3"][0])[:, :, None], b_in[:, 0:4, None], b_in[:, 4:8, None]], 2)
    put("glu", glu.reshape(P, -1))
    put("b_z", b_in[:, 8:12])
    gains = per_feature(g["gn_att_g_3"][0])
    put("pairs", np.stack([b_in[:, 12:16], b_in[:, 16:20], b_in[:, 20:24], b_in[:, 24:28], gains], 2).reshape(P, -1))
    for name, source in (("cln_g", "cln_g_3"), ("cln_b", "cln_b_3"), ("pw_b", "pw_b_3"), ("gn_conv", "gn_conv_g_3")):
        put(name, per_feature(g[source][0]))
    put("final_g", per_feature(g["final_g_3"]))
    put("eps5", np.full((P, 1), 1e-5))
    put("eps6", np.full((P, 1), EPS))
    arrays = {
        "x_t": np.ascontiguousarray(g["x"][0].T),
        "blocks": np.stack(stream).reshape(len(stream), P, 1024),
        "params": params,
        "consts": np.concatenate([np.eye(P), np.full((P, P), 1.0 / D), np.tril(np.full((P, P), NEG), -1),
                                  np.triu(np.full((P, P), NEG), 1),
                                  np.kron(np.eye(2), np.full((64, 64), 1.0 / 64))], 1).astype(np.float32),
        "bias_1": banded_bias(g["att_rel_bias"][0]),
        "bias_2": window_bias(),
        "bias_3": near_bias(g["rpb_3"][0]),
        "p_t": np.ascontiguousarray(g["p_2"][0, 0].T),
        "sgu_rows": np.stack([g["sgu_norm_gain"][0], g["sgu_norm_bias"][0], g["sgu_b"][0].reshape(-1)]),
        "sgu_w": np.ascontiguousarray(g["sgu_w"][0].transpose(2, 0, 1)),
    }
    nc = bacc.Bacc("TRN2", target_bir_lowering=False, num_devices=1)
    refs = {n: nc.dram_tensor(n, arrays[n].shape, F32, kind="ExternalInput").ap() for n in _INS}
    out_t = nc.dram_tensor("out_t", (D, TOK), F32, kind="ExternalOutput").ap()
    mixer_program(nc, n_blocks=len(stream), out_t=out_t, **refs)
    got = run_bass_kernel_spmd(nc, [arrays], core_ids=[0]).results[0]["out_t"]
    return np.ascontiguousarray(got.T)[None]
```
